# Optimizing a Trainium2 kernel written in Bass

```python
import jax, jax.numpy as jnp
from jax import lax
import numpy as np
import jax
import jax.numpy as jnp

D_MODEL = 1024
BATCH = 1
SEQ = 256
DEPTH = 2

LRU_WIDTH = D_MODEL // 2
LRU_BLOCKS = 8
LRU_BLOCK = LRU_WIDTH // LRU_BLOCKS
CONV_WIDTH = 4
LRU_C = 8.0
RET_HEADS = 8
RET_DIM = 64
RET_WIDTH = RET_HEADS * RET_DIM
RET_CHUNK = 128
RET_THETA = 10000.0
AB_IN = 2 * LRU_WIDTH + 4 * RET_WIDTH
AB_OUT = LRU_WIDTH + RET_WIDTH

NSA_HEADS = 16
NSA_KV_GROUPS = 4
NSA_HEAD_DIM = 64
NSA_REP = NSA_HEADS // NSA_KV_GROUPS
KV_WIDTH = NSA_KV_GROUPS * NSA_HEAD_DIM
CMP_LEN = 32
CMP_STRIDE = 16
SLC_LEN = 64
SLC_TOPK = 16
WINDOW = 512
NSA_QBLOCK = 32
ROPE_THETA = 500000.0
ROT_DIM = NSA_HEAD_DIM // 4
NSA_IN = NSA_HEADS * NSA_HEAD_DIM + 6 * KV_WIDTH + 3 * NSA_HEADS

FFN_HIDDEN = ((8 * D_MODEL // 3 + 255) // 256) * 256

EPS = 1e-6
NEG = -1e30
BIG = 1e30
N_EVEN = (DEPTH + 1) // 2
N_ODD = DEPTH // 2


def rmsnorm(x, g):
    xf = x.astype(jnp.float32)
    y = xf * lax.rsqrt(jnp.mean(xf * xf, axis=-1, keepdims=True) + EPS)
    return (y * g.astype(jnp.float32)).astype(x.dtype)

def rotary(x, pos, rot_dim, theta):
    half = rot_dim // 2
    inv = theta ** (-jnp.arange(0, rot_dim, 2, dtype=jnp.float32) / rot_dim)
    ang = jnp.asarray(pos).astype(jnp.float32)[:, None] * inv
    cos = jnp.cos(ang)[:, None, :]
    sin = jnp.sin(ang)[:, None, :]
    x1 = x[..., :half].astype(jnp.float32)
    x2 = x[..., half:rot_dim].astype(jnp.float32)
    rot = jnp.concatenate([x1 * cos - x2 * sin, x2 * cos + x1 * sin], axis=-1).astype(x.dtype)
    return jnp.concatenate([rot, x[..., rot_dim:]], axis=-1)

def swiglu(x, w1, w3, w2):
    return (jax.nn.silu(x @ w1) * (x @ w3)) @ w2

def causal_depthwise_conv(x, w, b):
    S = x.shape[1]
    xp = jnp.pad(x, ((0, 0), (CONV_WIDTH - 1, 0), (0, 0)))
    out = b
    for k in range(CONV_WIDTH):
        out = out + xp[:, k:k + S] * w[k]
    return out

def block_diag_linear(x, w, b):
    B, S, _ = x.shape
    xb = x.reshape(B, S, LRU_BLOCKS, LRU_BLOCK)
    return jnp.einsum('bsni,nij->bsnj', xb, w).reshape(B, S, LRU_WIDTH) + b

def rg_lru(x, ga_w, ga_b, gx_w, gx_b, lam):
    r = jax.nn.sigmoid(block_diag_linear(x, ga_w, ga_b)).astype(jnp.float32)
    i = jax.nn.sigmoid(block_diag_linear(x, gx_w, gx_b))
    log_a = -LRU_C * r * jax.nn.softplus(-lam.astype(jnp.float32))
    a = jnp.exp(log_a)
    mult = jnp.sqrt(-jnp.expm1(2.0 * log_a))
    u = mult * (i * x).astype(jnp.float32)

    def combine(left, right):
        a1, b1 = left
        a2, b2 = right
        return a1 * a2, a2 * b1 + b2

    _, h = lax.associative_scan(combine, (a, u), axis=1)
    return h.astype(x.dtype)

def retention(q, k, v):
    B, S, H, d = q.shape
    C = RET_CHUNK
    N = S // C
    pos = jnp.arange(S)
    q = rotary(q, pos, d, RET_THETA)
    k = rotary(k, pos, d, RET_THETA) * (d ** -0.5)
    log_g = jnp.log1p(-(2.0 ** (-5.0 - jnp.arange(H, dtype=jnp.float32))))
    ci = jnp.arange(C, dtype=jnp.float32)
    diff = ci[:, None] - ci[None, :]
    inner_decay = jnp.where(diff >= 0, jnp.exp(jnp.maximum(diff, 0.0) * log_g[:, None, None]), 0.0)
    q_decay = jnp.exp((ci + 1.0) * log_g[:, None])
    k_decay = jnp.exp((C - 1.0 - ci) * log_g[:, None])
    chunk_decay = jnp.exp(C * log_g)

    def to_chunks(t):
        return t.reshape(B, N, C, H, d).transpose(1, 0, 3, 2, 4)

    def step(state, inp):
        qi, ki, vi = inp
        qf, kf, vf = qi.astype(jnp.float32), ki.astype(jnp.float32), vi.astype(jnp.float32)
        s = jnp.einsum('bhid,bhjd->bhij', qf, kf) * inner_decay
        o = jnp.einsum('bhij,bhjd->bhid', s, vf) + jnp.einsum('bhid,bhde->bhie', qf * q_decay[..., None], state)
        state = state * chunk_decay[:, None, None] + jnp.einsum('bhjd,bhje->bhde', kf * k_decay[..., None], vf)
        return state, o

    state0 = jnp.zeros((B, H, d, d), jnp.float32)
    _, o = lax.scan(step, state0, (to_chunks(q), to_chunks(k), to_chunks(v)))
    o = o.transpose(1, 0, 3, 2, 4).reshape(B, S, H, d)
    mu = jnp.mean(o, axis=-1, keepdims=True)
    var = jnp.mean(jnp.square(o - mu), axis=-1, keepdims=True)
    return ((o - mu) * lax.rsqrt(var + EPS)).astype(v.dtype)

def hybrid_ab(h, w_in, conv_w, conv_b, ga_w, ga_b, gx_w, gx_b, lam, w_out):
    B, S, _ = h.shape
    proj = h @ w_in
    L, R = LRU_WIDTH, RET_WIDTH
    y, xr, q, k, v, g = jnp.split(proj, [L, 2 * L, 2 * L + R, 2 * L + 2 * R, 2 * L + 3 * R], axis=-1)
    xr = causal_depthwise_conv(xr, conv_w, conv_b)
    lru_out = rg_lru(xr, ga_w, ga_b, gx_w, gx_b, lam) * jax.nn.gelu(y)
    shp = (B, S, RET_HEADS, RET_DIM)
    ret = retention(q.reshape(shp), k.reshape(shp), v.reshape(shp)).reshape(B, S, R)
    ret_out = ret * jax.nn.silu(g)
    return jnp.concatenate([lru_out, ret_out], axis=-1) @ w_out

def nsa(h, w_in, pe_k, k_w1, k_w2, pe_v, v_w1, v_w2, w_out):
    B, S, _ = h.shape
    H, G, Rr, dh, QB = NSA_HEADS, NSA_KV_GROUPS, NSA_REP, NSA_HEAD_DIM, NSA_QBLOCK
    HD = H * dh
    proj = h @ w_in
    q = proj[..., :HD].reshape(B, S, H, dh)
    kv = proj[..., HD:HD + 6 * KV_WIDTH].reshape(B, S, 6, G, dh)
    k_cmp, v_cmp, k_slc, v_slc, k_win, v_win = [kv[:, :, j] for j in range(6)]
    gates = jax.nn.sigmoid(proj[..., HD + 6 * KV_WIDTH:].reshape(B, S, H, 3))
    pos = jnp.arange(S)
    q = rotary(q, pos, ROT_DIM, ROPE_THETA) * (dh ** -0.5)
    k_slc = rotary(k_slc, pos, ROT_DIM, ROPE_THETA)
    k_win = rotary(k_win, pos, ROT_DIM, ROPE_THETA)

    n_cmp = (S - CMP_LEN) // CMP_STRIDE + 1
    blk_idx = np.arange(n_cmp)[:, None] * CMP_STRIDE + np.arange(CMP_LEN)[None, :]
    cmp_end_np = blk_idx[:, -1]
    cmp_end = jnp.asarray(cmp_end_np)

    def compress(t, pe, w1, w2):
        blocks = t[:, blk_idx] + pe[:, None, :]
        blocks = blocks.transpose(0, 1, 3, 2, 4).reshape(B, n_cmp, G, CMP_LEN * dh)
        return jax.nn.gelu(blocks @ w1) @ w2

    kc = rotary(compress(k_cmp, pe_k, k_w1, k_w2), cmp_end_np, ROT_DIM, ROPE_THETA)
    vc = compress(v_cmp, pe_v, v_w1, v_w2)

    n_slc = S // SLC_LEN
    c_start = blk_idx[:, 0][:, None]
    s_start = np.arange(n_slc)[None, :] * SLC_LEN
    overlap = np.clip(np.minimum(c_start + CMP_LEN, s_start + SLC_LEN) - np.maximum(c_start, s_start), 0, None) / CMP_LEN
    cmp_to_slc = jnp.asarray(overlap, jnp.float32)
    top_k = min(SLC_TOPK, n_slc)
    ks_blocks = k_slc.reshape(B, n_slc, SLC_LEN, G, dh).transpose(0, 3, 1, 2, 4)
    vs_blocks = v_slc.reshape(B, n_slc, SLC_LEN, G, dh).transpose(0, 3, 1, 2, 4)
    gather = jax.vmap(jax.vmap(lambda blocks, idx: blocks[idx]))
    kw_pad = jnp.pad(k_win, ((0, 0), (WINDOW, 0), (0, 0), (0, 0)))
    vw_pad = jnp.pad(v_win, ((0, 0), (WINDOW, 0), (0, 0), (0, 0)))
    blk = jnp.arange(n_slc)

    def attend_block(qi):
        t0 = qi * QB
        qpos = t0 + jnp.arange(QB)
        qb = lax.dynamic_slice_in_dim(q, t0, QB, axis=1).reshape(B, QB, G, Rr, dh)
        s = jnp.einsum('bqgrd,bngd->bgrqn', qb, kc).astype(jnp.float32)
        vis = cmp_end[None, :] <= qpos[:, None]
        p_cmp = jnp.where(vis, jax.nn.softmax(jnp.where(vis, s, NEG), axis=-1), 0.0)
        o_cmp = jnp.einsum('bgrqn,bngd->bqgrd', p_cmp.astype(vc.dtype), vc)
        imp = jnp.einsum('bgrqn,nj->bgqj', p_cmp, cmp_to_slc)
        cur = qpos[:, None] // SLC_LEN
        forced = (blk[None, :] == 0) | (blk[None, :] == cur) | (blk[None, :] == cur - 1)
        causal_blk = blk[None, :] * SLC_LEN <= qpos[:, None]
        imp = jnp.where(forced, BIG, jnp.where(causal_blk, imp, NEG))
        _, sel = lax.top_k(imp, top_k)
        kg = gather(ks_blocks, sel)
        vg = gather(vs_blocks, sel)
        s = jnp.einsum('bqgrd,bgqkld->bgrqkl', qb, kg).astype(jnp.float32)
        tok = sel[..., None] * SLC_LEN + jnp.arange(SLC_LEN)
        ok = tok <= qpos[:, None, None]
        s = jnp.where(ok[:, :, None], s, NEG).reshape(B, G, Rr, QB, top_k * SLC_LEN)
        p_slc = jax.nn.softmax(s, axis=-1).reshape(B, G, Rr, QB, top_k, SLC_LEN)
        o_slc = jnp.einsum('bgrqkl,bgqkld->bqgrd', p_slc.astype(vg.dtype), vg)
        kw = lax.dynamic_slice_in_dim(kw_pad, t0, WINDOW + QB, axis=1)
        vw = lax.dynamic_slice_in_dim(vw_pad, t0, WINDOW + QB, axis=1)
        kpos = t0 - WINDOW + jnp.arange(WINDOW + QB)
        dist = qpos[:, None] - kpos[None, :]
        band = (dist >= 0) & (dist < WINDOW) & (kpos[None, :] >= 0)
        s = jnp.einsum('bqgrd,bkgd->bgrqk', qb, kw).astype(jnp.float32)
        p_win = jax.nn.softmax(jnp.where(band, s, NEG), axis=-1)
        o_win = jnp.einsum('bgrqk,bkgd->bqgrd', p_win.astype(vw.dtype), vw)
        gb = lax.dynamic_slice_in_dim(gates, t0, QB, axis=1).reshape(B, QB, G, Rr, 3)
        o = gb[..., 0:1] * o_cmp + gb[..., 1:2] * o_slc + gb[..., 2:3] * o_win
        return o.reshape(B, QB, HD)

    out = lax.map(attend_block, jnp.arange(S // QB))
    out = out.transpose(1, 0, 2, 3).reshape(B, S, HD)
    return out @ w_out

def first_inputs(seed: int = 0) -> dict:
    key = jax.random.key(seed)
    ks = jax.random.split(key, 24)
    f32 = jnp.float32

    def w(k, shape, fan_in):
        return jax.random.normal(k, shape, f32) * (fan_in ** -0.5)

    def gain(k, shape):
        return 1.0 + 0.01 * jax.random.normal(k, shape, f32)

    a_pow_c = jax.random.uniform(ks[9], (N_EVEN, LRU_WIDTH), f32, 0.9, 0.999)
    root = a_pow_c ** (1.0 / LRU_C)
    lru_lambda = jnp.log(root) - jnp.log1p(-root)
    return {
        'x': jax.random.normal(ks[0], (BATCH, SEQ, D_MODEL), f32),
        'attn_norm': gain(ks[1], (DEPTH, D_MODEL)),
        'ab_w_in': w(ks[2], (N_EVEN, D_MODEL, AB_IN), D_MODEL),
        'conv_w': w(ks[3], (N_EVEN, CONV_WIDTH, LRU_WIDTH), CONV_WIDTH),
        'conv_b': 0.01 * jax.random.normal(ks[4], (N_EVEN, LRU_WIDTH), f32),
        'gate_a_w': w(ks[5], (N_EVEN, LRU_BLOCKS, LRU_BLOCK, LRU_BLOCK), LRU_BLOCK),
        'gate_a_b': 0.01 * jax.random.normal(ks[6], (N_EVEN, LRU_WIDTH), f32),
        'gate_x_w': w(ks[7], (N_EVEN, LRU_BLOCKS, LRU_BLOCK, LRU_BLOCK), LRU_BLOCK),
        'gate_x_b': 0.01 * jax.random.normal(ks[8], (N_EVEN, LRU_WIDTH), f32),
        'lru_lambda': lru_lambda,
        'ab_w_out': w(ks[10], (N_EVEN, AB_OUT, D_MODEL), AB_OUT),
        'nsa_w_in': w(ks[11], (N_ODD, D_MODEL, NSA_IN), D_MODEL),
        'cmp_pe_k': 0.02 * jax.random.normal(ks[12], (N_ODD, CMP_LEN, NSA_HEAD_DIM), f32),
        'cmp_k_w1': w(ks[13], (N_ODD, CMP_LEN * NSA_HEAD_DIM, NSA_HEAD_DIM), CMP_LEN * NSA_HEAD_DIM),
        'cmp_k_w2': w(ks[14], (N_ODD, NSA_HEAD_DIM, NSA_HEAD_DIM), NSA_HEAD_DIM),
        'cmp_pe_v': 0.02 * jax.random.normal(ks[15], (N_ODD, CMP_LEN, NSA_HEAD_DIM), f32),
        'cmp_v_w1': w(ks[16], (N_ODD, CMP_LEN * NSA_HEAD_DIM, NSA_HEAD_DIM), CMP_LEN * NSA_HEAD_DIM),
        'cmp_v_w2': w(ks[17], (N_ODD, NSA_HEAD_DIM, NSA_HEAD_DIM), NSA_HEAD_DIM),
        'nsa_w_out': w(ks[18], (N_ODD, NSA_HEADS * NSA_HEAD_DIM, D_MODEL), NSA_HEADS * NSA_HEAD_DIM),
        'ffn_norm': gain(ks[19], (DEPTH, D_MODEL)),
        'ffn_w1': w(ks[20], (DEPTH, D_MODEL, FFN_HIDDEN), D_MODEL),
        'ffn_w3': w(ks[21], (DEPTH, D_MODEL, FFN_HIDDEN), D_MODEL),
        'ffn_w2': w(ks[22], (DEPTH, FFN_HIDDEN, D_MODEL), FFN_HIDDEN),
        'final_norm': gain(ks[23], (D_MODEL,)),
    }

def first_block(x, attn_norm, ab_w_in, conv_w, conv_b, gate_a_w, gate_a_b, gate_x_w, gate_x_b,
              lru_lambda, ab_w_out, nsa_w_in, cmp_pe_k, cmp_k_w1, cmp_k_w2, cmp_pe_v, cmp_v_w1,
              cmp_v_w2, nsa_w_out, ffn_norm, ffn_w1, ffn_w3, ffn_w2, final_norm):
    h = x
    for layer in range(DEPTH):
        hn = rmsnorm(h, attn_norm[layer])
        i = layer // 2
        if layer % 2 == 0:
            h = h + hybrid_ab(hn, ab_w_in[i], conv_w[i], conv_b[i], gate_a_w[i], gate_a_b[i],
                              gate_x_w[i], gate_x_b[i], lru_lambda[i], ab_w_out[i])
        else:
            h = h + nsa(hn, nsa_w_in[i], cmp_pe_k[i], cmp_k_w1[i], cmp_k_w2[i],
                        cmp_pe_v[i], cmp_v_w1[i], cmp_v_w2[i], nsa_w_out[i])
        h = h + swiglu(rmsnorm(h, ffn_norm[layer]), ffn_w1[layer], ffn_w3[layer], ffn_w2[layer])
    return rmsnorm(h, final_norm)


GRID_W = 64
CTX_LEN = 256
HEAD_DIM = 64
BRANCH_W = 256
N_BRANCH = 4
A_Q_HEADS = 4
A_KV_HEADS = 2
D_Q_HEADS = 4
D_KV_HEADS = 2
FNET_GROUPS = 4
SGU_GROUPS = 4
GROUP_W = 64
CHUNK = 128
Q_BLOCK = 128
WINDOW_2 = 128
ROPE_BASE = 10000.0
KV_W = 128
IN_SIZES = (BRANCH_W, KV_W, KV_W, BRANCH_W,
            BRANCH_W, KV_W, KV_W, BRANCH_W,
            BRANCH_W, BRANCH_W,
            BRANCH_W, BRANCH_W, BRANCH_W)
IN_W = 9 * BRANCH_W + 4 * KV_W


def _rms(x, w):
    xf = x.astype(jnp.float32)
    y = xf * lax.rsqrt(jnp.mean(xf * xf, axis=-1, keepdims=True) + EPS)
    return (y * w.astype(jnp.float32)).astype(x.dtype)

def _split_in(p):
    idx, acc = [], 0
    for s in IN_SIZES[:-1]:
        acc += s
        idx.append(acc)
    return jnp.split(p, idx, axis=-1)

def _modulation(cvec, w_ada, b_ada):
    m = jax.nn.silu(cvec) @ w_ada + b_ada
    return jnp.split(m, 3, axis=-1)

def _axial_rope_tables(rows):
    t = jnp.arange(rows * GRID_W, dtype=jnp.int32)
    r = (t // GRID_W).astype(jnp.float32)
    col = (t % GRID_W).astype(jnp.float32)
    nf = HEAD_DIM // 4
    inv = ROPE_BASE ** (-jnp.arange(nf, dtype=jnp.float32) / nf)
    ar = r[:, None] * inv[None, :]
    ac = col[:, None] * inv[None, :]
    return (jnp.cos(ar), jnp.sin(ar), jnp.cos(ac), jnp.sin(ac))

def _rot_half(x, cos, sin):
    nf = cos.shape[-1]
    x1, x2 = x[..., :nf], x[..., nf:]
    cos = cos[None, :, None, :]
    sin = sin[None, :, None, :]
    return jnp.concatenate([x1 * cos - x2 * sin, x1 * sin + x2 * cos], axis=-1)

def _axial_rope(x, tabs):
    cr, sr, cc, sc = tabs
    xf = x.astype(jnp.float32)
    half = HEAD_DIM // 2
    y = jnp.concatenate([_rot_half(xf[..., :half], cr, sr),
                         _rot_half(xf[..., half:], cc, sc)], axis=-1)
    return y.astype(x.dtype)

def _heads(t, n):
    return t.reshape(t.shape[0], t.shape[1], n, HEAD_DIM)

def _flat(o):
    return o.reshape(o.shape[0], o.shape[1], -1)

def _q_groups(q, qn, n_q, n_kv, tabs):
    b, n = q.shape[:2]
    q = _rms(_heads(q, n_q), qn)
    if tabs is not None:
        q = _axial_rope(q, tabs)
    return (q * HEAD_DIM ** -0.5).reshape(b, n, n_kv, n_q // n_kv, HEAD_DIM)

def _k_heads(k, kn, n_kv, tabs):
    k = _rms(_heads(k, n_kv), kn)
    if tabs is not None:
        k = _axial_rope(k, tabs)
    return k

def _attend(q, k, v, sink):
    s = jnp.einsum('bqkgd,bnkd->bkgqn', q, k, preferred_element_type=jnp.float32)
    if sink is not None:
        s_sink = jnp.broadcast_to(sink.astype(jnp.float32)[None, :, :, None, None], s.shape[:-1] + (1,))
        p = jax.nn.softmax(jnp.concatenate([s, s_sink], axis=-1), axis=-1)[..., :-1]
    else:
        p = jax.nn.softmax(s, axis=-1)
    return jnp.einsum('bkgqn,bnkd->bqkgd', p.astype(v.dtype), v)

def _attend_blocked(q, k, v):
    b, s = q.shape[:2]
    nb = s // Q_BLOCK
    qb = jnp.moveaxis(q.reshape(b, nb, Q_BLOCK, *q.shape[2:]), 1, 0)
    ob = lax.map(lambda qq: _attend(qq, k, v, None), qb)
    return jnp.moveaxis(ob, 0, 1).reshape(b, s, -1)

def _attend_window_sink(q, k, v, kc, vc, sink):
    b, s = q.shape[:2]
    nb = s // Q_BLOCK
    nc = kc.shape[1]
    pad = ((0, 0), (Q_BLOCK, Q_BLOCK), (0, 0), (0, 0))

    def band(t):
        tb = jnp.pad(t, pad).reshape(b, nb + 2, Q_BLOCK, *t.shape[2:])
        bt = jnp.concatenate([tb[:, :-2], tb[:, 1:-1], tb[:, 2:]], axis=2)
        return jnp.moveaxis(bt, 1, 0)

    kb, vb = band(k), band(v)
    qb = jnp.moveaxis(q.reshape(b, nb, Q_BLOCK, *q.shape[2:]), 1, 0)
    a_idx = jnp.arange(Q_BLOCK)[:, None]
    j_idx = jnp.arange(3 * Q_BLOCK)[None, :]
    rel = j_idx - Q_BLOCK - a_idx
    sink_f = sink.astype(jnp.float32)

    def one(args):
        qq, kk, vv, i = args
        kpos = (i - 1) * Q_BLOCK + j_idx
        mask = (jnp.abs(rel) <= WINDOW_2) & (kpos >= 0) & (kpos < s)
        s_loc = jnp.einsum('bqkgd,bjkd->bkgqj', qq, kk, preferred_element_type=jnp.float32)
        s_loc = jnp.where(mask, s_loc, -jnp.inf)
        s_ctx = jnp.einsum('bqkgd,bnkd->bkgqn', qq, kc, preferred_element_type=jnp.float32)
        s_sink = jnp.broadcast_to(sink_f[None, :, :, None, None], s_loc.shape[:-1] + (1,))
        p = jax.nn.softmax(jnp.concatenate([s_ctx, s_loc, s_sink], axis=-1), axis=-1).astype(vv.dtype)
        return (jnp.einsum('bkgqn,bnkd->bqkgd', p[..., :nc], vc)
                + jnp.einsum('bkgqj,bjkd->bqkgd', p[..., nc:nc + 3 * Q_BLOCK], vv))

    ob = lax.map(one, (qb, kb, vb, jnp.arange(nb)))
    return jnp.moveaxis(ob, 0, 1).reshape(b, s, -1)

def _fourier_mix(f, w_fnet):
    b, n = f.shape[:2]
    fg = f.astype(jnp.float32).reshape(b, n, FNET_GROUPS, GROUP_W)
    y = jnp.fft.fft2(fg, axes=(1, 3), norm='ortho').real.astype(f.dtype)
    return jnp.einsum('bngc,gcd->bngd', y, w_fnet).reshape(b, n, BRANCH_W)

def _spatial_gate(u, v, w_sp, b_sp):
    b, n = u.shape[:2]
    nch = n // CHUNK
    u = jax.nn.gelu(u, approximate=False).reshape(b, nch, CHUNK, SGU_GROUPS, GROUP_W)
    v = jax.nn.gelu(v, approximate=False).reshape(b, nch, CHUNK, SGU_GROUPS, GROUP_W)
    sp = jnp.einsum('gpq,bmqgc->bmpgc', w_sp, v) + b_sp.T[None, None, :, :, None]
    return (u * sp).reshape(b, n, BRANCH_W)

def _merge(h, outs, gates, w_br, w_merge, b_merge, w_out):
    b, n = h.shape[:2]
    yb = jnp.stack([o * jax.nn.silu(z) for o, z in zip(outs, gates)], axis=2)
    y = jnp.einsum('bnrw,rwd->bnrd', yb, w_br)
    g = jax.nn.sigmoid(h @ w_merge + b_merge).reshape(b, n, N_BRANCH, D_MODEL)
    return jnp.sum(g * y, axis=2) @ w_out

def _layer(x, xc, c, c_ctx, tabs, norm_w, w_ada, b_ada, w_in, qn_a, kn_a, qn_d, kn_d,
           sink_d, w_fnet, w_sp, b_sp, w_br, w_merge, b_merge, w_out, need_ctx_out):
    sh, sc, gt = _modulation(c, w_ada, b_ada)
    sh_c, sc_c, gt_c = _modulation(c_ctx, w_ada, b_ada)
    h = _rms(x, norm_w) * (1.0 + sc[:, None, :]) + sh[:, None, :]
    hc = _rms(xc, norm_w) * (1.0 + sc_c) + sh_c
    aq, ak, av, az, dq, dk, dv, dz, bf, bz, cu, cv, cz = _split_in(h @ w_in)
    aqc, akc, avc, azc, dqc, dkc, dvc, dzc, bfc, bzc, cuc, cvc, czc = _split_in(hc @ w_in)
    sink = sink_d.reshape(D_KV_HEADS, D_Q_HEADS // D_KV_HEADS)

    ka_c = _k_heads(akc, kn_a, A_KV_HEADS, None)
    va_c = _heads(avc, A_KV_HEADS)
    kd_c = _k_heads(dkc, kn_d, D_KV_HEADS, None)
    vd_c = _heads(dvc, D_KV_HEADS)

    qa = _q_groups(aq, qn_a, A_Q_HEADS, A_KV_HEADS, tabs)
    ka = jnp.concatenate([ka_c, _k_heads(ak, kn_a, A_KV_HEADS, tabs)], axis=1)
    va = jnp.concatenate([va_c, _heads(av, A_KV_HEADS)], axis=1)
    o_a = _attend_blocked(qa, ka, va)
    qd = _q_groups(dq, qn_d, D_Q_HEADS, D_KV_HEADS, tabs)
    o_d = _attend_window_sink(qd, _k_heads(dk, kn_d, D_KV_HEADS, tabs), _heads(dv, D_KV_HEADS),
                              kd_c, vd_c, sink)
    o_b = _fourier_mix(bf, w_fnet)
    o_c = _spatial_gate(cu, cv, w_sp, b_sp)
    y = _merge(h, (o_a, o_d, o_b, o_c), (az, dz, bz, cz), w_br, w_merge, b_merge, w_out)
    x = x + gt[:, None, :] * y

    if need_ctx_out:
        qa_c = _q_groups(aqc, qn_a, A_Q_HEADS, A_KV_HEADS, None)
        o_ac = _flat(_attend(qa_c, ka_c, va_c, None))
        qd_c = _q_groups(dqc, qn_d, D_Q_HEADS, D_KV_HEADS, None)
        o_dc = _flat(_attend(qd_c, kd_c, vd_c, sink))
        o_bc = _fourier_mix(bfc, w_fnet)
        o_cc = _spatial_gate(cuc, cvc, w_sp, b_sp)
        yc = _merge(hc, (o_ac, o_dc, o_bc, o_cc), (azc, dzc, bzc, czc), w_br, w_merge, b_merge, w_out)
        xc = xc + gt_c * yc
    return x, xc

def second_inputs(seed: int = 0) -> dict:
    key = jax.random.key(seed)
    ks = jax.random.split(key, 24)
    f32 = jnp.float32
    nrm = lambda k, shape, s: jax.random.normal(k, shape, f32) * s
    return {
        'x': nrm(ks[0], (BATCH, SEQ, D_MODEL), 1.0),
        'c': nrm(ks[1], (BATCH, D_MODEL), 1.0),
        'ctx': nrm(ks[2], (BATCH, CTX_LEN, D_MODEL), 1.0),
        'c_ctx': nrm(ks[3], (D_MODEL,), 1.0),
        'norm_w': 1.0 + nrm(ks[4], (DEPTH, D_MODEL), 0.02),
        'w_ada': nrm(ks[5], (DEPTH, D_MODEL, 3 * D_MODEL), 0.5 * D_MODEL ** -0.5),
        'b_ada': nrm(ks[6], (DEPTH, 3 * D_MODEL), 0.02),
        'w_in': nrm(ks[7], (DEPTH, D_MODEL, IN_W), D_MODEL ** -0.5),
        'qn_a': 1.0 + nrm(ks[8], (DEPTH, HEAD_DIM), 0.02),
        'kn_a': 1.0 + nrm(ks[9], (DEPTH, HEAD_DIM), 0.02),
        'qn_d': 1.0 + nrm(ks[10], (DEPTH, HEAD_DIM), 0.02),
        'kn_d': 1.0 + nrm(ks[11], (DEPTH, HEAD_DIM), 0.02),
        'sink_d': nrm(ks[12], (DEPTH, D_Q_HEADS), 0.5),
        'w_fnet': nrm(ks[13], (DEPTH, FNET_GROUPS, GROUP_W, GROUP_W), GROUP_W ** -0.5),
        'w_sp': nrm(ks[14], (DEPTH, SGU_GROUPS, CHUNK, CHUNK), CHUNK ** -0.5),
        'b_sp': 1.0 + nrm(ks[15], (DEPTH, SGU_GROUPS, CHUNK), 0.02),
        'w_br': nrm(ks[16], (DEPTH, N_BRANCH, BRANCH_W, D_MODEL), BRANCH_W ** -0.5),
        'w_merge': nrm(ks[17], (DEPTH, D_MODEL, N_BRANCH * D_MODEL), D_MODEL ** -0.5),
        'b_merge': nrm(ks[18], (DEPTH, N_BRANCH * D_MODEL), 0.02),
        'w_out': nrm(ks[19], (DEPTH, D_MODEL, D_MODEL), D_MODEL ** -0.5),
    }

def second_block(x, c, ctx, c_ctx, norm_w, w_ada, b_ada, w_in, qn_a, kn_a, qn_d, kn_d, sink_d,
              w_fnet, w_sp, b_sp, w_br, w_merge, b_merge, w_out):
    rows = x.shape[1] // GRID_W
    tabs = _axial_rope_tables(rows)
    xc = ctx
    for l in range(DEPTH):
        x, xc = _layer(x, xc, c, c_ctx, tabs, norm_w[l], w_ada[l], b_ada[l], w_in[l],
                       qn_a[l], kn_a[l], qn_d[l], kn_d[l], sink_d[l], w_fnet[l], w_sp[l],
                       b_sp[l], w_br[l], w_merge[l], b_merge[l], w_out[l],
                       need_ctx_out=(l < DEPTH - 1))
    return x


def setup_inputs(seed=0):
    out = dict(first_inputs(seed))
    for name, value in second_inputs(seed + 1).items():
        if name != "x":
            out[name + "_2"] = value
    return out


def reference(
    x, attn_norm, ab_w_in, conv_w, conv_b, gate_a_w, gate_a_b, gate_x_w, gate_x_b, lru_lambda,
    ab_w_out, nsa_w_in, cmp_pe_k, cmp_k_w1, cmp_k_w2, cmp_pe_v, cmp_v_w1, cmp_v_w2, nsa_w_out,
    ffn_norm, ffn_w1, ffn_w3, ffn_w2, final_norm, c_2, ctx_2, c_ctx_2, norm_w_2, w_ada_2,
    b_ada_2, w_in_2, qn_a_2, kn_a_2, qn_d_2, kn_d_2, sink_d_2, w_fnet_2, w_sp_2, b_sp_2, w_br_2,
    w_merge_2, b_merge_2, w_out_2,
):
    x = first_block(
        x, attn_norm, ab_w_in, conv_w, conv_b, gate_a_w, gate_a_b, gate_x_w, gate_x_b,
        lru_lambda, ab_w_out, nsa_w_in, cmp_pe_k, cmp_k_w1, cmp_k_w2, cmp_pe_v, cmp_v_w1,
        cmp_v_w2, nsa_w_out, ffn_norm, ffn_w1, ffn_w3, ffn_w2, final_norm,
    )
    return second_block(
        x, c_2, ctx_2, c_ctx_2, norm_w_2, w_ada_2, b_ada_2, w_in_2, qn_a_2, kn_a_2, qn_d_2,
        kn_d_2, sink_d_2, w_fnet_2, w_sp_2, b_sp_2, w_br_2, w_merge_2, b_merge_2, w_out_2,
    )


_drawn_inputs = setup_inputs


def setup_inputs(seed=0):
    import zlib

    import numpy as np

    out = dict(_drawn_inputs(seed))
    spreads = {}
    factors = {'attn_norm': 4.966,
     'conv_b': 2.922,
     'gate_a_b': 8.0,
     'gate_x_b': 8.0,
     'cmp_pe_k': 8.0,
     'cmp_pe_v': 32.118,
     'ffn_norm': 5.9,
     'final_norm': 5.69,
     'ctx_2': 4.615,
     'norm_w_2': 8.0,
     'b_ada_2': 3.622,
     'qn_a_2': 8.0,
     'kn_a_2': 8.0,
     'qn_d_2': 8.0,
     'kn_d_2': 8.0,
     'sink_d_2': 8.0,
     'b_sp_2': 8.0,
     'b_merge_2': 8.0}
    for name, (base, spread) in spreads.items():
        noise = np.random.default_rng([zlib.crc32(name.encode()), seed]).standard_normal(out[name].shape)
        drawn = base * np.exp(spread * noise) if base else spread * noise
        out[name] = jnp.asarray(drawn.astype(out[name].dtype))
    for name, factor in factors.items():
        out[name] = (out[name] * factor).astype(out[name].dtype)
    return out
```

```python
import math
import numpy as np
import concourse.bass as bass
from concourse import mybir
from contextlib import ExitStack

F32 = mybir.dt.float32
ALU = mybir.AluOpType
ACT = mybir.ActivationFunctionType
AX = mybir.AxisListType
EPS = 1e-6
NSLOT = 6
SLOT = 2816
ARENA = 20000


class Queue:

    def __init__(self, sem):
        self.sem, self.n, self.items, self.seen = sem, 0, [], {}

    def last(self):
        return (self.sem, self.n)

    def wait(self, *tokens):
        for t in tokens:
            if isinstance(t, list):
                self.wait(*t)
                continue
            sem, value = t
            if value > self.seen.get(id(sem), 0):
                self.seen[id(sem)] = value
                self.items.append(lambda e, s=sem, v=value: e.wait_ge(s, v))

    def do(self, fn, *tokens, chain=True):
        self.wait(*tokens)
        if chain:
            self.wait(self.last())
        self.n += 1
        self.items.append(lambda e, f=fn, s=self.sem: f(e).then_inc(s, 1))
        return self.last()

    def plain(self, fn):
        self.items.append(fn)

    def run(self, e):
        for f in self.items:
            f(e)


class Bank:
    def __init__(self, ap, banks, free):
        self.ap, self.banks, self.free = ap, banks, free
        self.w = [t for b in banks for t in free[b]]
        for b in banks:
            free[b] = None

    def read(self, *tokens):
        for b in self.banks:
            self.free[b] = list(tokens)


def _params_layout():
    cols, at = {}, 0
    for name, n in [("attn_norm", 16), ("ffn_norm", 16), ("final_norm", 8), ("conv_w", 16), ("conv_b", 4),
                    ("ga_b", 4), ("gx_b", 4), ("lam", 4), ("b_ada", 48), ("norm_w2", 16), ("b_merge", 64),
                    ("qkn", 8), ("cvec", 16), ("sink", 8)]:
        cols[name] = (at, n)
        at += n
    return cols, at


def _consts_layout():
    cols, at = {}, 0
    for name, n in [("ident", 128), ("ones", 2), ("bones2", 2), ("bones", 128), ("p32", 128), ("p8", 128),
                    ("p16", 128), ("rcos", 256), ("rsin", 256), ("ncos", 256), ("nsin", 256), ("ecos", 15),
                    ("esin", 15), ("acos", 256), ("asin", 256), ("cmask", 256), ("emask", 30), ("evis", 2),
                    ("wmask", 1024), ("cs", 256), ("cn", 512), ("sn", 512), ("mhalf", 64), ("onerow", 64),
                    ("decay", 2048)]:
        cols[name] = (at, n)
        at += n
    return cols, at


def build(nc, A, out):
    ctx = ExitStack()
    with ctx:
        def sb(name, cols):
            return ctx.enter_context(nc.sbuf_tensor(name, [128, cols], F32))

        def sem(name):
            return ctx.enter_context(nc.semaphore(name))

        PL, PN = _params_layout()
        CL, CN = _consts_layout()
        ring = sb("ring", NSLOT * SLOT)
        par = sb("par", PN)
        con = sb("con", CN)
        X = sb("X", 4096)[:, :].rearrange("p (k n) -> p k n", k=8)
        XN = sb("XN", 4096)[:, :].rearrange("p (k n) -> p k n", k=8)
        MOD = sb("MOD", 96 + 64)
        SM = sb("SM", 640)
        arena = sb("arena", ARENA)
        psum = ctx.enter_context(nc.psum_tensor("psum", [128, 4096], F32))

        SP, PE, VE, AC, GP = [Queue(sem(n)) for n in ("s_sp", "s_pe", "s_ve", "s_ac", "s_gp")]
        s_const = [sem(f"s_const{i}") for i in range(8)]
        s_slot = [sem(f"s_slot{i}") for i in range(NSLOT)]
        s_out = sem("s_out")

        def P(name, i=0, n=1):
            a = PL[name][0] + i
            return par[:, a:a + n]

        def C(name, i=0, n=None):
            a, m = CL[name]
            return con[:, a + i:a + (m if n is None else i + n)]

        top = [0]

        def area(cols, shape=None, **dims):
            a = top[0]
            top[0] += cols
            assert top[0] <= ARENA, top[0]
            v = arena[:, a:a + cols]
            return v.rearrange(shape, **dims) if shape else v

        small_at = [0]

        def small(n):
            if small_at[0] + n > 640:
                small_at[0] = 0
            a = small_at[0]
            small_at[0] += n
            return SM[:, a:a + n]

        bank_free = [[] for _ in range(8)]
        next_bank = [0]

        def bank():
            b = next_bank[0] % 8
            next_bank[0] += 1
            assert bank_free[b] is not None
            return Bank(psum[:, b * 512:(b + 1) * 512], [b], bank_free)

        def pair():
            next_bank[0] += next_bank[0] % 2
            b = next_bank[0] % 8
            next_bank[0] += 2
            assert bank_free[b] is not None and bank_free[b + 1] is not None
            return Bank(psum[:, b * 512:(b + 2) * 512], [b, b + 1], bank_free)

        slot_use = [[] for _ in range(NSLOT)]
        slot_n = [0] * NSLOT
        next_slot = [0]

        def load(src, shape, parts=None, **dims):
            i = next_slot[0] % NSLOT
            next_slot[0] += 1
            cols = src.shape[-1]
            SP.wait(slot_use[i])
            slot_use[i] = None
            view = ring[:, i * SLOT:i * SLOT + cols]
            for lo, hi in parts or [(0, 128)]:
                slot_n[i] += 16
                SP.plain(lambda e, d=ring[lo:hi, i * SLOT:i * SLOT + cols], s=src, m=s_slot[i]:
                         e.dma_start(d, s).then_inc(m, 16))
            return view.rearrange(shape, **dims), (s_slot[i], slot_n[i]), i

        def done(i, token):
            slot_use[i] = [token]

        def barrier():
            tokens = [q.last() for q in (PE, VE, AC, GP)]
            for q in (PE, VE, AC, GP):
                q.wait(tokens)
            top[0] = 0

        def mm(dst, lhsT, rhs, start, stop, *w, sig=False):
            PE.wait(*w)
            f = lambda e: e.matmul(dst, lhsT, rhs, start=start, stop=stop)
            if sig:
                return PE.do(f, chain=False)
            PE.plain(f)

        def tr(dst, src, ident, *w, sig=False):
            PE.wait(*w)
            f = lambda e: e.transpose(dst, src, ident)
            if sig:
                return PE.do(f, chain=False)
            PE.plain(f)

        def tt(q, dst, a, b, op, *w):
            return q.do(lambda e: e.tensor_tensor(dst, a, b, op), *w)

        def stt(dst, a, s, b, op0, op1, *w):
            return VE.do(lambda e: e.scalar_tensor_tensor(out=dst, in0=a, scalar=s, in1=b, op0=op0, op1=op1), *w)

        def ts(q, dst, a, s1, s2, op0, op1, *w):
            if s2 is None:
                return q.do(lambda e: e.tensor_scalar(dst, a, s1, None, op0), *w)
            return q.do(lambda e: e.tensor_scalar(dst, a, s1, s2, op0, op1), *w)

        def act(dst, src, fn, *w, bias=0.0, scale=1.0, accum=None):
            if accum is None:
                return AC.do(lambda e: e.activation(dst, src, fn, bias=bias, scale=scale), *w)
            return AC.do(lambda e: e.activation(dst, src, fn, bias=bias, scale=scale, accum_out=accum), *w)

        def copy(q, dst, src, *w):
            if q is AC:
                return AC.do(lambda e: e.activation(dst, src, ACT.Copy), *w)
            return q.do(lambda e: e.tensor_copy(dst, src), *w)

        turn = [0]

        def evac(dst, src, *w):
            turn[0] ^= 1
            return copy(AC if turn[0] else VE, dst, src, *w)

        const_n = [0] * 8

        def cload(i, dst, src):
            const_n[i] += 16
            AC.plain(lambda e: e.dma_start(dst, src).then_inc(s_const[i], 16))
            return (s_const[i], const_n[i])

        x_in = A["xT"].rearrange("p (k n) -> p k n", k=8)
        c_in = A["ctxT"].rearrange("p (k n) -> p k n", k=8)
        t_x = cload(0, X[:, :, 0:256], x_in)
        t_par = cload(1, par[:, :], A["params"])
        cut = CL["decay"][0]
        t_con = cload(2, con[:, 0:cut], A["consts"][:, 0:cut])
        t_dec = cload(3, con[:, cut:CN], A["consts"][:, cut:CN])
        t_ctx = cload(4, X[:, :, 256:512], c_in)
        ident = C("ident")
        PE.wait(t_con)
        VE.wait(t_con, t_par)
        AC.wait(t_con, t_par)
        GP.wait(t_con, t_par)

        def power(n, src, *w):
            r = small(n)
            return r, tt(GP, r, src, C("mhalf", 0, n), ALU.pow, *w)

        def inv_rms(src, sq, t_src):
            toks = []
            for j, q in enumerate((AC, VE, GP, AC)):
                d, s = sq[:, 2 * j:2 * j + 2, :], src[:, 2 * j:2 * j + 2, :]
                if q is AC:
                    toks.append(act(d, s, ACT.Square, t_src))
                else:
                    toks.append(tt(q, d, s, s, ALU.mult, t_src))
            b = bank()
            for n in range(2):
                for k in range(8):
                    t = mm(b.ap[:, n:n + 1], sq[:, k, n * 128:(n + 1) * 128], C("ones", 0, 1), k == 0, k == 7,
                           b.w, toks[k // 2], sig=(n == 1 and k == 7))
            ms = small(2)
            t = ts(VE, ms, b.ap[:, 0:2], 1.0 / 1024, EPS, ALU.mult, ALU.add, t)
            b.read(t)
            r, t = power(2, ms, t)
            wide = small(256).rearrange("p (a n) -> p a n", a=2)
            t = copy(VE, wide, r.rearrange("p (a n) -> p a n", n=1).to_broadcast([128, 2, 128]), t)
            b = bank()
            for n in range(2):
                t2 = mm(b.ap[:, n * 128:(n + 1) * 128], wide[:, n, :], ident, True, True, b.w, t, sig=(n == 1))
            return b, t2

        def norm(src, dst, sq, gain, t_src):
            b, t = inv_rms(src, sq, t_src)
            toks = []
            for k in range(8):
                toks.append(stt(dst[:, k, :], src[:, k, :], gain(k), b.ap[:, 0:256], ALU.mult, ALU.mult, t))
            b.read(toks[-1])
            return toks

        def feats(dst_cols, chunk, t_w, rhs, t_rhs, b, nk=8, m0=0, n=256):
            for j, c in enumerate(dst_cols):
                for k in range(nk):
                    t = mm(b.ap[:, j * n:(j + 1) * n], chunk[:, k, c:c + 128], rhs(k), k == 0, k == nk - 1,
                           b.w, t_w, t_rhs[k] if isinstance(t_rhs, list) and len(t_rhs) == nk else t_rhs,
                           sig=(k == nk - 1))
            return t

        def wchunk(name, i):
            return load(A[name][i], "p (k c) -> p k c", k=8)

        def residual(name, rhs, t_rhs):
            for c in range(4):
                w, t_w, i = wchunk(name, c)
                b = bank()
                t = feats([0, 128], w, t_w, rhs, t_rhs, b)
                done(i, t)
                v = b.ap.rearrange("p (a n) -> p a n", a=2)
                t = tt(VE, X[:, 2 * c:2 * c + 2, 0:256], v, X[:, 2 * c:2 * c + 2, 0:256], ALU.add, t)
                b.read(t)
            return t

        def rope(raw, tmp, nt, perm, cos, sin, t_raw, n=256):
            toks = []
            per = 512 // n
            for j in range(0, nt, per):
                m = min(per, nt - j)
                b = bank()
                bv = b.ap[:, 0:m * n].rearrange("p (a n) -> p a n", a=m)
                t = mm(bv, perm, raw[:, j:j + m, :], True, True, b.w, t_raw, sig=True)
                s3 = sin.rearrange("p (a n) -> p a n", a=1).to_broadcast([128, m, n])
                c3 = cos.rearrange("p (a n) -> p a n", a=1).to_broadcast([128, m, n])
                t1 = tt(VE, tmp[:, j:j + m, :], bv, s3, ALU.mult, t)
                b.read(t1)
                t2 = tt(GP, raw[:, j:j + m, :], raw[:, j:j + m, :], c3, ALU.mult, t)
                toks.append(tt(GP, raw[:, j:j + m, :], raw[:, j:j + m, :], tmp[:, j:j + m, :], ALU.add, t1, t2))
            return toks[-1]

        def hybrid():
            barrier()
            SQ = XN[:, :, 256:512]
            t_xn = norm(X[:, :, 0:256], XN[:, :, 0:256], SQ, lambda k: P("attn_norm", k), t_x)
            rhs = lambda k: XN[:, k, 0:256]
            four = dict(shape="p (a n) -> p a n", a=4)
            xr = area(4 * 260, **four)
            conv = area(1024, **four)
            gr, gi = area(1024, **four), area(1024, **four)
            aa, uu = area(1024, **four), area(1024, **four)
            cat = area(2048, "p (a n) -> p a n", a=8)
            qq, kk, gg, ro, sq = [area(1024, **four) for _ in range(5)]
            vv = area(1024, "p (t c) -> p t c", t=2)
            tmp = area(1024, **four)
            tmp2 = area(1024, **four)
            sT = [area(768, "p (h c) -> p h c", h=2) for _ in range(2)]
            rx = area(1024, "p (t h d) -> p t h d", t=2, h=8)
            gates, t_gates, gslot = load(A["lru_gates"], "p (g t c) -> p g t c", g=2, t=4)
            t_pad = GP.do(lambda e: e.memset(xr[:, :, 0:3], 0.0))
            sp = small(4)
            neg, e_, z_, z2 = small(4), small(4), small(4), small(4)
            ts(VE, neg, P("lam", 0, 4), -1.0, None, ALU.mult, None)
            t = tt(VE, e_, neg, P("lam", 0, 4), ALU.min)
            t = act(e_, e_, ACT.Exp, t)
            ts(VE, z_, e_, 2.0, None, ALU.add, None, t)
            VE.do(lambda e: e.reciprocal(z_, z_))
            tt(VE, z_, z_, e_, ALU.mult)
            tt(VE, z2, z_, z_, ALU.mult)
            ts(VE, sp, z2, 16.0 / 15, 16.0 / 13, ALU.mult, ALU.add)
            for n in (11, 9, 7, 5, 3, 1):
                tt(VE, sp, sp, z2, ALU.mult)
                ts(VE, sp, sp, 16.0 / n, None, ALU.add, None)
            tt(VE, sp, sp, z_, ALU.mult)
            ts(VE, neg, neg, 0.0, 8.0, ALU.max, ALU.mult)
            t_sp = tt(VE, sp, sp, neg, ALU.add)

            def project(c, fn):
                w, t_w, i = wchunk("ab_in", c)
                b = bank()
                t = feats([0, 128], w, t_w, rhs, t_xn, b)
                done(i, t)
                t = fn(b.ap.rearrange("p (a n) -> p a n", a=2), t)
                b.read(t)
                return t

            toks = [project(2 + j, lambda v, t: evac(xr[:, 2 * j:2 * j + 2, 3:259], v, t)) for j in range(2)]
            for t_ in range(4):
                w = lambda k: P("conv_w", t_ * 4 + k)
                ts(VE, conv[:, t_, :], xr[:, t_, 0:256], w(0), P("conv_b", t_), ALU.mult, ALU.add, t_pad, toks[t_ // 2])
                for k in range(1, 4):
                    t_conv = stt(conv[:, t_, :], xr[:, t_, k:k + 256], w(k), conv[:, t_, :], ALU.mult, ALU.add)
            for g, dst, bias in ((0, gr, "ga_b"), (1, gi, "gx_b")):
                for j in range(2):
                    b = bank()
                    for h in range(2):
                        t = mm(b.ap[:, h * 256:(h + 1) * 256], gates[:, g, 2 * j + h, :], conv[:, 2 * j + h, :],
                               True, True, b.w, t_gates, t_conv, sig=True)
                    for h in range(2):
                        t2 = act(dst[:, 2 * j + h, :], b.ap[:, h * 256:(h + 1) * 256], ACT.Sigmoid, t,
                                 bias=P(bias, 2 * j + h))
                    b.read(t2)
            done(gslot, t)
            for t_ in range(4):
                ts(VE, gr[:, t_, :], gr[:, t_, :], sp[:, t_:t_ + 1], None, ALU.mult, None, t2, t_sp)
            t_s = VE.last()
            t_a = act(aa, gr, ACT.Exp, t_s, scale=-1.0)
            t_t = act(gr, gr, ACT.Tanh)
            tt(VE, uu, aa, aa, ALU.mult, t_a)
            t = stt(uu, uu, 1.0, gr, ALU.add, ALU.mult, t_t)
            t_g = tt(GP, gi, gi, conv, ALU.mult, t2, t_conv)
            t = act(uu, uu, ACT.Sqrt, t)
            tt(VE, uu, uu, gi, ALU.mult, t, t_g)
            for t_ in range(4):
                t_scan = VE.do(lambda e, a=t_: e.tensor_tensor_scan(conv[:, a, :], aa[:, a, :], uu[:, a, :], 0.0,
                                                                    ALU.mult, ALU.add))
            tq = [project(4 + j, lambda v, t: evac(qq[:, 2 * j:2 * j + 2, :], v, t)) for j in range(2)]
            tk = [project(6 + j, lambda v, t: evac(kk[:, 2 * j:2 * j + 2, :], v, t)) for j in range(2)]
            t_q = rope(qq, tmp, 4, C("p32"), C("rcos"), C("rsin"), tq)
            t_k = rope(kk, tmp2, 4, C("p32"), C("rcos"), C("rsin"), tk)
            tv = []
            for j in range(2):
                w, t_w, i = wchunk("ab_in", 8 + j)
                b = bank()
                for n in range(2):
                    for k in range(8):
                        t = mm(b.ap[:, n * 256:(n + 1) * 256], XN[:, k, n * 128:(n + 1) * 128], w[:, k, :],
                               k == 0, k == 7, b.w, t_w, t_xn, sig=(k == 7))
                done(i, t)
                tv.append(evac(vv[:, :, j * 256:(j + 1) * 256], b.ap.rearrange("p (t c) -> p t c", t=2), t))
                b.read(tv[-1])
            tg = [project(10 + j, lambda v, t: act(gg[:, 2 * j:2 * j + 2, :], v, ACT.Silu, t)) for j in range(2)]
            ty = [project(j, lambda v, t: act(cat[:, 2 * j:2 * j + 2, :], v, ACT.Gelu_apprx_tanh, t))
                  for j in range(2)]
            t_lru = tt(GP, cat[:, 0:4, :], cat[:, 0:4, :], conv, ALU.mult, ty, t_scan)
            t_pv = [[], []]
            for t_ in range(4):
                pr = pair()
                for p in range(2):
                    r = slice(p * 64, p * 64 + 64)
                    c = p * 512
                    mm(pr.ap[:, c:c + 256], kk[r, t_, 0:128], qq[r, t_, 0:256], True, True, pr.w, t_q, t_k)
                    t = mm(pr.ap[:, c + 256:c + 384], kk[r, t_, 128:256], qq[r, t_, 128:256], True, True, sig=True)
                v = pr.ap.rearrange("p (h c) -> p h c", h=2)
                s = sT[t_ % 2]
                dec = C("decay").rearrange("p (h c) -> p h c", h=8)[:, 2 * t_:2 * t_ + 2, :]
                tt(VE, s[:, :, 0:256], v[:, :, 0:256], dec, ALU.mult, t, t_dec, t_pv[t_ % 2])
                t = tt(VE, s[:, :, 256:384], v[:, :, 256:384], dec[:, :, 0:128], ALU.mult)
                pr.read(t)
                b = bank()
                for p in range(2):
                    r = slice(p * 64, p * 64 + 64)
                    vc = (2 * t_ + p) * 64
                    mm(b.ap[r, 0:256], vv[:, 0, vc:vc + 64], s[:, p, 0:256], True, False, b.w, t, tv)
                    t2 = mm(b.ap[r, 128:256], vv[:, 1, vc:vc + 64], s[:, p, 256:384], False, True, sig=True)
                t_pv[t_ % 2] = [t2]
                t_ro = copy(AC, ro[:, t_, :], b.ap[:, 0:256], t2)
                b.read(t_ro)
            for j in range(2):
                b = bank()
                v = b.ap.rearrange("p (a n) -> p a n", a=2)
                t = mm(v, C("bones"), ro[:, 2 * j:2 * j + 2, :], True, True, b.w, t_ro, sig=True)
                t = stt(ro[:, 2 * j:2 * j + 2, :], v, -1.0, ro[:, 2 * j:2 * j + 2, :], ALU.mult, ALU.add, t)
                b.read(t)
                t_sq = act(sq[:, 2 * j:2 * j + 2, :], ro[:, 2 * j:2 * j + 2, :], ACT.Square, t)
            t_ro = t
            b = bank()
            for n in range(2):
                for a in range(4):
                    c = n * 8 + 2 * a
                    t = mm(b.ap[:, c:c + 2], sq[:, a, n * 128:(n + 1) * 128], C("bones2"), True, True, b.w, t_sq,
                           sig=True)
            ms = small(16)
            t = ts(VE, ms, b.ap[:, 0:16], 1.0, EPS, ALU.mult, ALU.add, t)
            b.read(t)
            r, t = power(16, ms, t)
            t = copy(VE, rx, r.rearrange("p (t h d) -> p t h d", t=2, d=1).to_broadcast([128, 2, 8, 64]), t)
            for j in range(2):
                b = bank()
                v = b.ap.rearrange("p (a n) -> p a n", a=2)
                for h in range(2):
                    for n in range(2):
                        a = 2 * j + h
                        t2 = mm(v[:, h, n * 128:(n + 1) * 128], rx[:, n, 2 * a:2 * a + 2, :], ident, True, True,
                                b.w, t, sig=True)
                t3 = tt(VE, ro[:, 2 * j:2 * j + 2, :], v, ro[:, 2 * j:2 * j + 2, :], ALU.mult, t2, t_ro)
                b.read(t3)
                t_ret = tt(VE, cat[:, 4 + 2 * j:6 + 2 * j, :], ro[:, 2 * j:2 * j + 2, :], gg[:, 2 * j:2 * j + 2, :],
                           ALU.mult, tg)
            return residual("ab_out", lambda k: cat[:, k, :], [t_lru, t_ret])

        def ffn(l, t_h):
            barrier()
            t_xn = norm(X[:, :, 0:256], XN[:, :, 0:256], XN[:, :, 256:512], lambda k: P("ffn_norm", 8 * l + k), t_h)
            rhs = lambda k: XN[:, k, 0:256]
            hh = area(22 * 256, "p (a n) -> p a n", a=22)
            sg = [area(512) for _ in range(2)]
            t_free = [[], []]
            t_hh = []
            for c in range(11):
                w, t_w, i = wchunk(f"w1_{l}", c)
                b1 = bank()
                t1 = feats([0, 128], w, t_w, rhs, t_xn, b1)
                done(i, t1)
                w, t_w, i = wchunk(f"w3_{l}", c)
                b3 = bank()
                t3 = feats([0, 128], w, t_w, rhs, t_xn, b3)
                done(i, t3)
                s = sg[c % 2]
                t = act(s, b1.ap, ACT.Silu, t1, t_free[c % 2])
                b1.read(t)
                d = hh[:, 2 * c:2 * c + 2, :].rearrange("p a n -> p (a n)")
                t = tt(VE, d, s, b3.ap, ALU.mult, t, t3)
                b3.read(t)
                t_free[c % 2] = [t]
                t_hh += [t, t]
            for m in range(8):
                w, t_w, i = load(A[f"w2_{l}"][m], "p (k c) -> p k c", k=22)
                b = bank()
                t = feats([0], w, t_w, lambda k: hh[:, k, :], t_hh, b, nk=22)
                done(i, t)
                t = tt(VE, X[:, m, 0:256], b.ap[:, 0:256], X[:, m, 0:256], ALU.add, t)
                b.read(t)
            return t

        class Scratch:
            def __init__(self):
                self.S = [area(1024) for _ in range(2)]
                self.T = [area(1024) for _ in range(2)]
                self.Sf, self.Tf, self.n = [[], []], [[], []], 0

        def softmax(sc, pr, t_s, heads, J, scale, mask=None, sink=None, gate=None, rowvis=None):
            i = sc.n % 2
            sc.n += 1
            W = pr.ap.shape[-1] // heads
            v = pr.ap.rearrange("p (h j) -> p h j", h=heads)[:, :, 0:J]
            s = sc.S[i][:, 0:heads * J].rearrange("p (h j) -> p h j", h=heads)
            nm = small(heads)
            if mask is not None:
                t = stt(s, v, scale, mask.rearrange("p (a j) -> p a j", a=1).to_broadcast([128, heads, J]),
                        ALU.mult, ALU.add, t_s, sc.Sf[i])
                pr.read(t)
                t = VE.do(lambda e: e.tensor_reduce(nm, s, AX.X, ALU.max))
                src, esc = s, 1.0
            else:
                t = VE.do(lambda e: e.tensor_reduce(nm, v, AX.X, ALU.max), t_s, sc.Sf[i])
                ts(VE, nm, nm, scale, None, ALU.mult, None)
                src, esc = v, scale
            if sink is not None:
                tt(VE, nm, nm, sink, ALU.max)
            t = ts(VE, nm, nm, -1.0, None, ALU.mult, None)
            sm = small(heads)
            for h in range(heads):
                t_e = act(s[:, h, :], src[:, h, :], ACT.Exp, t, bias=nm[:, h:h + 1], scale=esc,
                          accum=sm[:, h:h + 1])
            if mask is None:
                pr.read(t_e)
            if sink is not None:
                se = small(heads)
                t_n = tt(VE, se, sink, nm, ALU.add)
                t_n = act(se, se, ACT.Exp, t_n)
                tt(VE, sm, sm, se, ALU.add, t_n, t_e)
            VE.do(lambda e: e.reciprocal(sm, sm), t_e)
            if gate is not None:
                tt(VE, sm, sm, gate, ALU.mult)
            if rowvis is not None:
                ts(VE, sm, sm, rowvis, None, ALU.mult, None)
            t = VE.do(lambda e: e.tensor_tensor(s, s, sm.rearrange("p (h a) -> p h a", a=1)
                                                .to_broadcast([128, heads, J]), ALU.mult))
            return s, t, i

        def turned(sc, s, t_p, i, heads, J):
            nj = (J + 127) // 128
            kp = min(J, 128)
            w = heads * 128
            b = pair() if nj * w > 512 else bank()
            for jt in range(nj):
                for h in range(heads):
                    c = jt * w + h * 128
                    t = tr(b.ap[0:kp, c:c + 128], s[:, h, jt * 128:jt * 128 + kp], ident, b.w, t_p, sig=True)
            sc.Sf[i] = [t]
            T = sc.T[i]
            t = copy(AC, T[0:kp, 0:nj * w], b.ap[0:kp, 0:nj * w], t, sc.Tf[i])
            b.read(t)
            return T, t

        def nsa(t_h):
            barrier()
            t_xn = norm(X[:, :, 0:256], XN[:, :, 0:256], XN[:, :, 256:512], lambda k: P("attn_norm", 8 + k), t_h)
            rhs = lambda k: XN[:, k, 0:256]
            two = dict(shape="p (a n) -> p a n", a=2)
            q = area(2048, "p (a n) -> p a n", a=8)
            tmp = area(2048, "p (a n) -> p a n", a=8)
            att = tmp
            kc, vc, ks, kw = [area(512, **two) for _ in range(4)]
            vs, vw = [area(512, "p (t c) -> p t c", t=2) for _ in range(2)]
            bufk, bufv = [area(960, "p (l n) -> p l n", l=32) for _ in range(2)]
            gk, gv = area(30), area(30)
            kcT = area(30, **two)
            kct = area(30, **two)
            vcs = area(256, "p (g d) -> p g d", g=4)
            gt = area(96, "p (t c) -> p t c", t=2)
            pe2 = area(64)
            t_pe = cload(5, pe2[0:64, :], A["pe"])
            t_pe = cload(5, pe2[64:128, :], A["pe"])
            sc = Scratch()
            sc2 = Scratch()

            def fm(c, dst):
                w, t_w, i = wchunk("nsa_in", c)
                b = bank()
                t = feats([0, 128], w, t_w, rhs, t_xn, b)
                done(i, t)
                t = evac(dst, b.ap.rearrange("p (a n) -> p a n", a=2), t)
                b.read(t)
                return t

            def tm(c, dst):
                w, t_w, i = wchunk("nsa_in", c)
                b = bank()
                for n in range(2):
                    for k in range(8):
                        t = mm(b.ap[:, n * 256:(n + 1) * 256], XN[:, k, n * 128:(n + 1) * 128], w[:, k, :],
                               k == 0, k == 7, b.w, t_w, t_xn, sig=(k == 7))
                done(i, t)
                t = evac(dst, b.ap.rearrange("p (t c) -> p t c", t=2), t)
                b.read(t)
                return t

            w, t_w, i = load(A["nsa_gates"], "p (k c) -> p k c", k=8)
            b = bank()
            for n in range(2):
                for k in range(8):
                    t = mm(b.ap[:, n * 48:(n + 1) * 48], XN[:, k, n * 128:(n + 1) * 128], w[:, k, :],
                           k == 0, k == 7, b.w, t_w, t_xn, sig=(k == 7))
            done(i, t)
            t_gt = act(gt, b.ap[:, 0:96].rearrange("p (t c) -> p t c", t=2), ACT.Sigmoid, t)
            b.read(t_gt)
            t_kc, t_vc = fm(4, kc), fm(5, vc)
            t_ks, t_kw = fm(6, ks), fm(8, kw)
            t_ks = rope(ks, tmp[:, 0:2, :], 2, C("p8"), C("ncos"), C("nsin"), t_ks)
            t_kw = rope(kw, tmp[:, 2:4, :], 2, C("p8"), C("ncos"), C("nsin"), t_kw)
            for src, dst, pe, t in ((kc, bufk, 0, t_kc), (vc, bufv, 1, t_vc)):
                for a in range(2):
                    for lh in range(2):
                        sv = src[:, a, lh * 16:lh * 16 + 240].rearrange("p (n l) -> p l n", l=16)
                        pv = pe2[:, pe * 32 + lh * 16:pe * 32 + lh * 16 + 16].rearrange("p (l a) -> p l a", a=1)
                        t_b = tt(VE, dst[:, lh * 16:lh * 16 + 16, a * 15:a * 15 + 15], sv,
                                 pv.to_broadcast([128, 16, 15]), ALU.add, t, t_pe)
            t_g2 = []
            halves = [(0, 64), (64, 128)]
            for src, g2, name in ((bufk, gk, "cmp_k1"), (bufv, gv, "cmp_v1")):
                w, t_w, i = load(A[name], "p (l c) -> p l c", parts=halves, l=32)
                for p in range(2):
                    r = slice(p * 64, p * 64 + 64)
                    b = bank()
                    for l in range(32):
                        t = mm(b.ap[r, 0:30], w[r, l, :], src[r, l, :], l == 0, l == 31, b.w, t_w, t_b,
                               sig=(l == 31))
                    t2 = act(g2[r, :], b.ap[r, 0:30], ACT.Gelu_apprx_tanh, t)
                    b.read(t2)
                done(i, t)
                t_g2.append(t2)
            w2, t_w2, i = load(A["cmp_w2"], "p (a c) -> p a c", parts=halves, a=2)
            for p in range(2):
                r = slice(p * 64, p * 64 + 64)
                b = bank()
                t = mm(b.ap[r, 0:30], w2[r, 0, :], gk[r, :], True, True, b.w, t_w2, t_g2, sig=True)
                t_kc = copy(VE, kcT[r, :, :], b.ap[r, 0:30].rearrange("p (a n) -> p a n", a=2), t)
                b.read(t_kc)
                b = bank()
                for a in range(2):
                    t = mm(b.ap[0:15, a * 64:a * 64 + 64], gv[r, a * 15:a * 15 + 15], w2[r, 1, :], True, True, b.w,
                           sig=True)
                for a in range(2):
                    t_vc = copy(VE, vcs[0:15, 2 * a + p, :], b.ap[0:15, a * 64:a * 64 + 64], t)
                b.read(t_vc)
            done(i, t)
            t_kc = rope(kcT, kct, 2, C("p8"), C("ecos"), C("esin"), t_kc, n=15)
            t_vs, t_vw = tm(7, vs), tm(9, vw)
            tq = [fm(c, q[:, 2 * c:2 * c + 2, :]) for c in range(4)]
            t_q = rope(q, tmp, 8, C("p8"), C("ncos"), C("nsin"), [t_ks, t_kw] + tq)

            t_att = []
            for it in range(2):
                J = 128 * (it + 1)
                cmask = C("cmask", 0 if it else 128, J)
                for g in range(4):
                    p, t2_ = g % 2, g // 2
                    r = slice(p * 64, p * 64 + 64)
                    parts = []
                    for br, (k_, v_, tk_, tv_) in enumerate(((kcT, vcs, t_kc, t_vc), (ks, vs, t_ks, t_vs),
                                                            (kw, vw, t_kw, t_vw))):
                        gate = gt[:, it, g * 12 + br:g * 12 + 12:3]
                        if br == 0:
                            pr = bank()
                            W, Jb = 128, 15
                        else:
                            pr = pair()
                            W, Jb = 256, J
                        for h in range(4):
                            t = mm(pr.ap[:, h * W:h * W + Jb], q[r, t2_ * 4 + h, it * 128:it * 128 + 128],
                                   k_[r, t2_, 0:Jb], True, True, pr.w, t_q, tk_, sig=True)
                        if br == 0:
                            s, t, i = softmax(sc2, pr, t, 4, 15, 0.125, mask=C("emask", it * 15, 15), gate=gate,
                                              rowvis=C("evis", it, 1))
                            T, t = turned(sc2, s, t, i, 4, 15)
                        else:
                            s, t, i = softmax(sc, pr, t, 4, J, 0.125, mask=cmask, gate=gate)
                            T, t = turned(sc, s, t, i, 4, J)
                        parts.append((br, T, t, i, v_, tv_))
                    b = bank()
                    todo = []
                    for br, T, t, i, v_, tv_ in parts:
                        if br == 0:
                            todo.append((v_[0:15, g, :], T[0:15, 0:512], t, tv_))
                        else:
                            for jt in range(it + 1):
                                todo.append((v_[:, jt, g * 64:g * 64 + 64], T[:, jt * 512:(jt + 1) * 512], t, tv_))
                    for n, (lh, rh, t, tv_) in enumerate(todo):
                        t_o = mm(b.ap[r, :], lh, rh, n == 0, n == len(todo) - 1, b.w, t, tv_, sig=True)
                    for br, T, t, i, v_, tv_ in parts:
                        (sc if br else sc2).Tf[i] = [t_o]
                    t = copy(VE, att[r, t2_ * 4:t2_ * 4 + 4, it * 128:it * 128 + 128],
                             b.ap[r, :].rearrange("p (h n) -> p h n", h=4), t_o, t_q)
                    b.read(t)
            return residual("nsa_out", lambda k: att[:, k, :], t)

        def modulation():
            barrier()
            sc = small(16)
            t_c = act(sc, P("cvec", 0, 16), ACT.Silu)
            s2 = sc.rearrange("p (k v) -> p k v", v=2)
            toks = []
            for l in range(2):
                b = bank()
                for c in range(12):
                    w, t_w, i = wchunk(f"ada_{l}", c)
                    for j in range(2):
                        m = 2 * c + j
                        for k in range(8):
                            t = mm(b.ap[:, 2 * m:2 * m + 2], w[:, k, j * 128:(j + 1) * 128], s2[:, k, :], k == 0,
                                   k == 7, b.w, t_w, t_c, sig=(k == 7))
                    done(i, t)
                m3 = MODS[l]
                bias = P("b_ada", 24 * l, 24).rearrange("p (m a) -> p m a", a=1).to_broadcast([128, 24, 2])
                t = tt(VE, m3, b.ap[:, 0:48].rearrange("p (m v) -> p m v", v=2), bias, ALU.add, t)
                b.read(t)
                nw = P("norm_w2", 8 * l, 8).rearrange("p (m a) -> p m a", a=1).to_broadcast([128, 8, 2])
                toks.append(stt(m3[:, 8:16, :], m3[:, 8:16, :], 1.0, nw, ALU.add, ALU.mult))
            return toks

        MODS = [MOD[:, 0:48].rearrange("p (m v) -> p m v", v=2), MOD[:, 48:96].rearrange("p (m v) -> p m v", v=2)]

        def layer(l, t_h):
            NT = 512 if l == 0 else 256
            NC = 512
            nt = NT // 128
            barrier()
            base = top[0]
            m3 = MODS[l]
            SQ = area(2048, "p (a n) -> p a n", a=8)
            H = XN
            t_H = []
            for v in range(2):
                cs = slice(v * 256, v * 256 + 256)
                b, t = inv_rms(X[:, :, cs], SQ, [PE.last()] + t_h)
                for k in range(8):
                    t1 = stt(H[:, k, cs], X[:, k, cs], m3[:, 8 + k, v:v + 1], b.ap[:, 0:256], ALU.mult, ALU.mult, t)
                    t2 = ts(GP, H[:, k, cs], H[:, k, cs], m3[:, k, v:v + 1], None, ALU.add, None, t1)
                b.read(t1)
                t_H.append(t2)
            top[0] = base
            barrier()
            Z = area(8 * NT, "p (r a n) -> p r a n", r=4, a=2)
            tail = top[0]
            R = [area(1536, "p (a n) -> p a n", a=3) for _ in range(2)]
            V = [area(512, "p (t c) -> p t c", t=4) for _ in range(2)]
            mid = top[0]

            def fm(w, t_w, cols, n, n0=0):
                b = bank()
                for k in range(8):
                    t = mm(b.ap[:, 0:n], w[:, k, cols:cols + 128], H[:, k, n0:n0 + n], k == 0, k == 7, b.w, t_w, t_H,
                           sig=(k == 7))
                return b, t

            t_z = []
            for r, c in enumerate((2, 5, 7, 10)):
                w, t_w, i = wchunk(f"in_{l}", c)
                for a in range(2):
                    b, t = fm(w, t_w, a * 128, NT)
                    t1 = act(Z[:, r, a, :], b.ap[:, 0:NT], ACT.Silu, t)
                    b.read(t1)
                    t_z.append(t1)
                done(i, t)
            U = area(2 * NT, "p (a n) -> p a n", a=2)
            VT = area(256 * nt, "p (t c) -> p t c", t=nt)
            w, t_w, i = wchunk(f"in_{l}", 8)
            for a in range(2):
                b, t = fm(w, t_w, a * 128, NT)
                t_u = act(U[:, a, :], b.ap[:, 0:NT], ACT.Gelu, t)
                b.read(t_u)
            done(i, t)
            w, t_w, i = wchunk(f"in_{l}", 9)
            for j in range(nt // 2):
                b = bank()
                for n in range(2):
                    for k in range(8):
                        c = (2 * j + n) * 128
                        t = mm(b.ap[:, n * 256:(n + 1) * 256], H[:, k, c:c + 128], w[:, k, :], k == 0, k == 7,
                               b.w, t_w, t_H, sig=(k == 7))
                t_v = act(VT[:, 2 * j:2 * j + 2, :], b.ap.rearrange("p (t c) -> p t c", t=2), ACT.Gelu, t)
                b.read(t_v)
            done(i, t)
            t_zu = tt(GP, Z[:, 3, :, :], Z[:, 3, :, :], U, ALU.mult, t_z, t_u)
            w, t_w, i = load(A[f"sp_{l}"], "p (g q) -> p g q", g=4)
            bsp, t_bsp, i2 = load(A[f"bsp_{l}"], "p (g q) -> p g q", parts=[(0, 1)], g=4)
            for a in range(2):
                b = bank()
                for n in range(nt):
                    for h in range(2):
                        g = 2 * a + h
                        r = slice(h * 64, h * 64 + 64)
                        mm(b.ap[r, n * 128:(n + 1) * 128], VT[:, n, g * 64:g * 64 + 64], w[:, g, :], True, False,
                           b.w, t_w, t_v)
                        t = mm(b.ap[r, n * 128:(n + 1) * 128], C("onerow")[0:1, :], bsp[0:1, g, :], False, True,
                               t_bsp, sig=True)
                t_yc = tt(VE, Z[:, 3, a, :], b.ap[:, 0:NT], Z[:, 3, a, :], ALU.mult, t, t_zu)
                b.read(t_yc)
            done(i, t)
            done(i2, t)
            barrier()
            top[0] = mid
            Fm = area(2 * NT, "p (a n) -> p a n", a=2)
            ZZ = area(1024, "p (t a c) -> p t a c", t=2, a=2)
            Y = area(512, "p (a n) -> p a n", a=2)
            w, t_w, i = wchunk(f"in_{l}", 6)
            for a in range(2):
                b, t = fm(w, t_w, a * 128, NT)
                t_f = evac(Fm[:, a, :], b.ap[:, 0:NT], t)
                t_f2 = t_f if a == 0 else [t_f, t_f2]
                b.read(t_f)
            done(i, t)
            w, t_w, i = load(A[f"fnet_{l}"], "p (a c) -> p a c", a=2)
            for v in range(NT // 256):
                for n in range(2):
                    b = bank()
                    for a in range(2):
                        c = v * 256 + n * 128
                        t = mm(b.ap[:, a * 256:(a + 1) * 256], Fm[:, a, c:c + 128], C("cs"), True, True, b.w, t_f2,
                               sig=True)
                    t = copy(VE, ZZ[:, n, :, :], b.ap.rearrange("p (a c) -> p a c", a=2), t, PE.last())
                    b.read(t)
                b = bank()
                for a in range(2):
                    for n in range(2):
                        mm(b.ap[:, a * 256:(a + 1) * 256], ZZ[:, n, a, 0:128], C("cn", n * 256, 256), n == 0, False,
                           b.w, t)
                        t2 = mm(b.ap[:, a * 256:(a + 1) * 256], ZZ[:, n, a, 128:256], C("sn", n * 256, 256), False,
                                n == 1, sig=True)
                t = copy(VE, Y, b.ap.rearrange("p (a n) -> p a n", a=2), t2, PE.last())
                b.read(t)
                b = bank()
                for a in range(2):
                    t2 = mm(b.ap[:, a * 256:(a + 1) * 256], w[:, a, :], Y[:, a, :], True, True, b.w, t, t_w, sig=True)
                zz = Z[:, 2, :, v * 256:v * 256 + 256]
                t = tt(VE, zz, b.ap.rearrange("p (a n) -> p a n", a=2), zz, ALU.mult, t2, t_z)
                b.read(t)
            done(i, t2)
            barrier()
            top[0] = mid
            sc = Scratch()
            S3 = area(1536, "p (a n) -> p a n", a=3)
            T3 = area(768, "p (a n) -> p a n", a=3)
            RX = area(1536, "p (t h d) -> p t h d", t=4, h=6)
            t_qk, t_vv = [], []
            for br, (cq, ck) in enumerate(((0, 1), (3, 4))):
                raw = R[br]
                w, t_w, i = wchunk(f"in_{l}", cq)
                tr_ = []
                for a in range(2):
                    b, t = fm(w, t_w, a * 128, NT)
                    tr_.append(evac(raw[:, a, 0:NT], b.ap[:, 0:NT], t))
                    b.read(tr_[-1])
                done(i, t)
                w, t_w, i = wchunk(f"in_{l}", ck)
                b, t = fm(w, t_w, 0, 512)
                tr_.append(evac(raw[:, 2, :], b.ap, t))
                b.read(tr_[-1])
                b = bank()
                for n in range(4):
                    for k in range(8):
                        t = mm(b.ap[:, n * 128:(n + 1) * 128], H[:, k, n * 128:(n + 1) * 128], w[:, k, 128:256],
                               k == 0, k == 7, b.w, t_w, t_H, sig=(k == 7))
                done(i, t)
                t = evac(V[br], b.ap.rearrange("p (t c) -> p t c", t=4), t)
                b.read(t)
                t_vv.append(t)
                t_rx = PE.last()
                sq = [act(S3[:, 0:2, 0:NT], raw[:, 0:2, 0:NT], ACT.Square, tr_, t_rx),
                      act(S3[:, 2, :], raw[:, 2, :], ACT.Square)]
                b = bank()
                for n in range(4):
                    for a in range(3):
                        if a < 2 and n >= nt:
                            continue
                        c = n * 6 + 2 * a
                        t = mm(b.ap[:, c:c + 2], S3[:, a, n * 128:(n + 1) * 128], C("bones2"), True, True, b.w, sq,
                               sig=True)
                ms = small(24)
                ms3 = ms.rearrange("p (t h) -> p t h", h=6)
                b3 = b.ap[:, 0:24].rearrange("p (t h) -> p t h", h=6)
                if nt == 4:
                    t = ts(VE, ms, b.ap[:, 0:24], 1.0, EPS, ALU.mult, ALU.add, t)
                else:
                    ts(VE, ms3[:, 0:2, :], b3[:, 0:2, :], 1.0, EPS, ALU.mult, ALU.add, t)
                    VE.do(lambda e: e.memset(ms3[:, 2:4, 0:4], 1.0))
                    t = ts(VE, ms3[:, 2:4, 4:6], b3[:, 2:4, 4:6], 1.0, EPS, ALU.mult, ALU.add)
                b.read(t)
                r_, t = power(24, ms, t)
                t = copy(VE, RX, r_.rearrange("p (t h d) -> p t h d", t=4, d=1).to_broadcast([128, 4, 6, 64]), t,
                         t_rx)
                tn = []
                for a in range(3):
                    n_ = nt if a < 2 else 4
                    b = bank()
                    for n in range(n_):
                        t2 = mm(b.ap[:, n * 128:(n + 1) * 128], RX[:, n, 2 * a:2 * a + 2, :], ident, True, True,
                                b.w, t, sig=True)
                    t3 = stt(raw[:, a, 0:n_ * 128], raw[:, a, 0:n_ * 128],
                             P("qkn", l * 4 + br * 2 + (0 if a < 2 else 1)), b.ap[:, 0:n_ * 128], ALU.mult,
                             ALU.mult, t2)
                    b.read(t3)
                    tn.append(t3)
                t_qk.append(rope(raw[:, :, 0:256], T3, 3, C("p16"), C("acos"), C("asin"), tn))
            t_o = []
            for br in range(2):
                raw, vv = R[br], V[br]
                for it in range(nt):
                    k0 = 0 if it < 2 else 256
                    J = 512 - k0
                    for p in range(2):
                        r = slice(p * 64, p * 64 + 64)
                        pr = pair()
                        for h in range(2):
                            t = mm(pr.ap[:, h * 512:h * 512 + J], raw[r, h, it * 128:it * 128 + 128],
                                   raw[r, 2, k0:512], True, True, pr.w, t_qk[br], sig=True)
                        mask = C("wmask", it * 512, 512) if br == 1 and it < 2 else None
                        sink = P("sink", l * 4 + 2 * p, 2) if br == 1 else None
                        s, t, i = softmax(sc, pr, t, 2, J, 0.125, mask=mask, sink=sink)
                        T, t = turned(sc, s, t, i, 2, J)
                        b = bank()
                        nj = J // 128
                        for jt in range(nj):
                            t2 = mm(b.ap[r, 0:256], vv[:, k0 // 128 + jt, p * 64:p * 64 + 64],
                                    T[:, jt * 256:(jt + 1) * 256], jt == 0, jt == nj - 1, b.w, t, t_vv[br],
                                    sig=(jt == nj - 1))
                        sc.Tf[i] = [t2]
                        zz = Z[r, br, :, it * 128:it * 128 + 128]
                        t = tt(VE, zz, b.ap[r, 0:256].rearrange("p (h n) -> p h n", h=2), zz, ALU.mult, t2, t_z)
                        b.read(t)
            barrier()
            top[0] = tail
            M = area(8 * NT, "p (a n) -> p a n", a=8)
            SG = [area(NT) for _ in range(2)]
            T2 = [area(NT) for _ in range(2)]
            t_sg, t_t2 = [[], []], [[], []]
            n_ = 0
            for c in range(4):
                wb, t_wb, ib = load(A[f"br_{l}"][c], "p (r k c) -> p r k c", r=4, k=2)
                for r in range(4):
                    w, t_w, i = wchunk(f"merge_{l}", r * 4 + c)
                    for j in range(2):
                        m = 2 * c + j
                        b, t = fm(w, t_w, j * 128, NT)
                        s = SG[n_ % 2]
                        t = act(s, b.ap[:, 0:NT], ACT.Sigmoid, t, t_sg[n_ % 2],
                                bias=P("b_merge", l * 32 + r * 8 + m))
                        b.read(t)
                        b = bank()
                        for k in range(2):
                            t_y = mm(b.ap[:, 0:NT], wb[:, r, k, j * 128:(j + 1) * 128], Z[:, r, k, :], k == 0,
                                     k == 1, b.w, t_wb, sig=(k == 1))
                        if r == 0:
                            t_m = tt(VE, M[:, m, :], b.ap[:, 0:NT], s, ALU.mult, t, t_y)
                            b.read(t_m)
                            t_sg[n_ % 2] = [t_m]
                        else:
                            u = T2[n_ % 2]
                            t = tt(VE, u, b.ap[:, 0:NT], s, ALU.mult, t, t_y, t_t2[n_ % 2])
                            b.read(t)
                            t_sg[n_ % 2] = [t]
                            t_m = tt(GP, M[:, m, :], M[:, m, :], u, ALU.add, t)
                            t_t2[n_ % 2] = [t_m]
                        n_ += 1
                    done(i, t_y)
                done(ib, t_y)
            t_x = []
            for c in range(4):
                w, t_w, i = wchunk(f"out_{l}", c)
                for j in range(2):
                    m = 2 * c + j
                    b = bank()
                    for k in range(8):
                        t = mm(b.ap[:, 0:NT], w[:, k, j * 128:(j + 1) * 128], M[:, k, :], k == 0, k == 7, b.w, t_w,
                               t_m, sig=(k == 7))
                    for v in range(NT // 256):
                        cs = slice(v * 256, v * 256 + 256)
                        t2 = stt(X[:, m, cs], b.ap[:, cs], m3[:, 16 + m, v:v + 1], X[:, m, cs], ALU.mult, ALU.add, t)
                    b.read(t2)
                done(i, t)
            return t2

        t = hybrid()
        t = ffn(0, t)
        t = nsa(t)
        t = ffn(1, t)
        t_f = norm(X[:, :, 0:256], X[:, :, 0:256], XN[:, :, 256:512], lambda k: P("final_norm", k), t)
        t_m = modulation()
        VE.wait(t_ctx)
        AC.wait(t_ctx)
        GP.wait(t_ctx)
        t = layer(0, [t_f[-1]] + t_m)
        t = layer(1, [t])
        SP.wait(t)
        SP.plain(lambda e: e.dma_start(out.rearrange("p (k n) -> p k n", k=8), X[:, :, 0:256]).then_inc(s_out, 16))
        SP.wait((s_out, 16))

        with nc.Block() as block:
            @block.sync
            def _(e):
                SP.run(e)

            @block.tensor
            def _(e):
                PE.run(e)

            @block.vector
            def _(e):
                VE.run(e)

            @block.scalar
            def _(e):
                AC.run(e)

            @block.gpsimd
            def _(e):
                GP.run(e)


def constants():
    CL, CN = _consts_layout()
    c = np.zeros((128, CN), np.float32)

    def put(name, v):
        a, n = CL[name]
        c[:, a:a + n] = np.asarray(v, np.float64).reshape(128, n)

    eye = np.eye(128)
    half = np.kron(np.eye(2), np.ones((64, 64)))
    put("ident", eye)
    put("ones", np.ones((128, 2)))
    put("bones2", np.kron(np.eye(2), np.ones((64, 1))) / 64)
    put("bones", half / 64)
    put("mhalf", np.full((128, 64), -0.5))
    put("onerow", np.ones((128, 64)))
    pos = np.arange(256, dtype=np.float32)
    d = np.arange(128) % 64

    def swap(partner):
        m = np.zeros((128, 128))
        for i in range(128):
            if partner[i] >= 0:
                m[partner[i], i] = 1
        return m

    def angles(p, rot, theta, idx):
        inv = np.float32(theta) ** (-np.arange(0, rot, 2, dtype=np.float32) / np.float32(rot))
        return (p[None, :].astype(np.float32) * inv.astype(np.float32)[idx][:, None]).astype(np.float32)

    base = (np.arange(128) // 64) * 64
    put("p32", swap(base + (d + 32) % 64))
    a = angles(pos, 64, 10000.0, d % 32).astype(np.float64)
    put("rcos", np.cos(a))
    put("rsin", np.sin(a) * np.where(d < 32, -1.0, 1.0)[:, None])
    put("p8", swap(np.where(d < 16, base + (d + 8) % 16, -1)))
    for name, p in (("n", pos), ("e", np.arange(15, dtype=np.float32) * 16 + 31)):
        a = angles(p, 16, 500000.0, d % 8).astype(np.float64)
        on = (d < 16)[:, None]
        put(name + "cos", np.where(on, np.cos(a), 1.0))
        put(name + "sin", np.where(on, np.sin(a) * np.where(d < 8, -1.0, 1.0)[:, None], 0.0))
    put("p16", swap(base + (d // 32) * 32 + (d % 32 + 16) % 32))
    inv = np.float32(10000.0) ** (-np.arange(16, dtype=np.float32) / np.float32(16))
    t = np.arange(256)
    where = np.where((d < 32)[:, None], (t // 64)[None, :], (t % 64)[None, :]).astype(np.float32)
    a = (where * inv.astype(np.float32)[d % 16][:, None]).astype(np.float32).astype(np.float64)
    put("acos", np.cos(a))
    put("asin", np.sin(a) * np.where(d % 32 < 16, -1.0, 1.0)[:, None])
    i = np.arange(128)
    NEG = -1e30
    causal = np.where(i[None, :] <= i[:, None], 0.0, NEG)
    put("cmask", np.concatenate([np.zeros((128, 128)), causal], 1))
    end = np.arange(15) * 16 + 31
    vis = end[None, None, :] <= (np.arange(2)[:, None, None] * 128 + i[None, :, None])
    put("emask", np.where(vis, 0.0, NEG).transpose(1, 0, 2))
    put("evis", vis.any(-1).T.astype(float))
    w = np.zeros((128, 2, 512))
    w[:, 0, 128:256] = causal
    w[:, 1, 0:128] = np.where(i[None, :] >= i[:, None], 0.0, NEG)
    put("wmask", w)
    k = np.arange(64)
    f = 2 * np.pi * ((k[:, None] * k[None, :]) % 64) / 64
    put("cs", np.concatenate([np.kron(np.eye(2), np.cos(f)), np.kron(np.eye(2), np.sin(f))], 1))
    n = np.arange(256)
    f = 2 * np.pi * ((n[:, None] * n[None, :]) % 256) / 256
    put("cn", (np.cos(f) / 128).reshape(2, 128, 256).transpose(1, 0, 2))
    put("sn", (-np.sin(f) / 128).reshape(2, 128, 256).transpose(1, 0, 2))
    g = np.log1p(-(2.0 ** (-5.0 - np.arange(8))))
    diff = np.arange(256)[None, :] - i[:, None]
    dec = np.where(diff[None] >= 0, np.exp(np.maximum(diff, 0)[None] * g[:, None, None]), 0.0) * 0.125
    put("decay", dec.transpose(1, 0, 2))
    return c


def kernel(**inputs):
    import concourse.bacc as _bacc
    from concourse.bass_utils import run_bass_kernel_spmd as _run

    I = {k: np.asarray(v) for k, v in inputs.items()}

    def cols(w, c=256):
        K, N = w.shape
        return np.ascontiguousarray(w.reshape(K // 128, 128, N // c, c).transpose(2, 1, 0, 3)).reshape(
            N // c, 128, K // 128 * c)

    def tiles(v):
        return v.reshape(-1, 128).T

    def tokens(x):
        return np.ascontiguousarray(x.T.reshape(8, 128, 256).transpose(1, 0, 2)).reshape(128, 2048)

    def diag(w):
        n = w.shape[0]
        o = np.zeros((128, n // 2, 128), np.float32)
        for b in range(n):
            h = b % 2
            o[h * 64:h * 64 + 64, b // 2, h * 64:h * 64 + 64] = w[b]
        return o

    arr = {"xT": tokens(I["x"][0]), "ctxT": tokens(I["ctx_2"][0]), "consts": constants()}
    PL, PN = _params_layout()
    par = np.zeros((128, PN), np.float32)

    def put(name, v):
        a, n = PL[name]
        par[:, a:a + n] = v

    put("attn_norm", tiles(I["attn_norm"]))
    put("ffn_norm", tiles(I["ffn_norm"]))
    put("final_norm", tiles(I["final_norm"]))
    put("conv_w", I["conv_w"][0].reshape(4, 4, 128).transpose(2, 1, 0).reshape(128, 16))
    put("conv_b", tiles(I["conv_b"]))
    put("ga_b", tiles(I["gate_a_b"]))
    put("gx_b", tiles(I["gate_x_b"]))
    put("lam", tiles(I["lru_lambda"]))
    put("b_ada", tiles(I["b_ada_2"]))
    put("norm_w2", tiles(I["norm_w_2"]))
    put("b_merge", tiles(I["b_merge_2"]))
    qkn = np.stack([I[n] for n in ("qn_a_2", "kn_a_2", "qn_d_2", "kn_d_2")], 1)
    put("qkn", np.tile(qkn.reshape(8, 64).T, (2, 1)))
    put("cvec", np.stack([I["c_2"][0].reshape(8, 128), I["c_ctx_2"].reshape(8, 128)], 2).transpose(1, 0, 2)
        .reshape(128, 16))
    put("sink", np.broadcast_to(I["sink_d_2"].reshape(1, 8), (128, 8)))
    arr["params"] = par
    arr["ab_in"] = cols(I["ab_w_in"][0])
    arr["ab_out"] = cols(I["ab_w_out"][0])
    arr["lru_gates"] = np.stack([diag(I["gate_a_w"][0]), diag(I["gate_x_w"][0])], 1).reshape(128, 1024)
    for l in range(2):
        arr[f"w1_{l}"] = cols(I["ffn_w1"][l])
        arr[f"w3_{l}"] = cols(I["ffn_w3"][l])
        arr[f"w2_{l}"] = cols(I["ffn_w2"][l], 128)
    w = I["nsa_w_in"][0]
    heads = [(2 * t2 + p) * 4 + r for t2 in range(2) for r in range(4) for p in range(2)]
    qcols = np.concatenate([np.arange(h * 64, h * 64 + 64) for h in heads])
    arr["nsa_in"] = cols(np.concatenate([w[:, qcols], w[:, 1024:2560]], 1))
    arr["nsa_gates"] = np.ascontiguousarray(w[:, 2560:].reshape(8, 128, 48).transpose(1, 0, 2)).reshape(128, 384)
    arr["nsa_out"] = cols(I["nsa_w_out"][0][qcols])
    arr["pe"] = np.ascontiguousarray(np.concatenate([I["cmp_pe_k"][0].T, I["cmp_pe_v"][0].T], 1))
    for n in "kv":
        arr[f"cmp_{n}1"] = np.ascontiguousarray(I[f"cmp_{n}_w1"][0].reshape(32, 64, 64).transpose(1, 0, 2)).reshape(
            64, 2048)
    arr["cmp_w2"] = np.concatenate([I["cmp_k_w2"][0], I["cmp_v_w2"][0]], 1)
    hd = np.concatenate([np.arange(h * 64, h * 64 + 64) for h in (0, 2, 1, 3)])
    for l in range(2):
        w = I["w_in_2"][l]
        order = np.arange(2816)
        for c in (0, 2, 3, 5):
            order[c * 256:(c + 1) * 256] = c * 256 + hd
        arr[f"in_{l}"] = cols(w[:, order])
        arr[f"ada_{l}"] = cols(I["w_ada_2"][l])
        arr[f"merge_{l}"] = cols(I["w_merge_2"][l])
        arr[f"out_{l}"] = cols(I["w_out_2"][l])
        br = I["w_br_2"][l].copy()
        br[0], br[1] = br[0][hd], br[1][hd]
        arr[f"br_{l}"] = np.ascontiguousarray(br.reshape(4, 2, 128, 4, 256).transpose(3, 2, 0, 1, 4)).reshape(
            4, 128, 2048)
        arr[f"fnet_{l}"] = diag(I["w_fnet_2"][l]).reshape(128, 256)
        arr[f"sp_{l}"] = np.ascontiguousarray(I["w_sp_2"][l].transpose(2, 0, 1)).reshape(128, 512)
        arr[f"bsp_{l}"] = np.ascontiguousarray(I["b_sp_2"][l].reshape(1, 512))
    nc = _bacc.Bacc("TRN2", target_bir_lowering=False, num_devices=1)
    arr = {k: np.ascontiguousarray(v) for k, v in arr.items()}
    A = {k: nc.dram_tensor(k, v.shape, mybir.dt.from_np(v.dtype), kind="ExternalInput").ap() for k, v in arr.items()}
    out = nc.dram_tensor("out", (128, 2048), F32, kind="ExternalOutput").ap()
    build(nc, A, out)
    r = _run(nc, [arr], core_ids=[0])
    y = np.asarray(r.results[0]["out"])
    return np.ascontiguousarray(y.reshape(128, 8, 256).transpose(2, 1, 0)).reshape(1, 256, 1024)
```

```python
import math
import numpy as np
import concourse.bass as bass
from concourse import mybir
from contextlib import ExitStack

F32 = mybir.dt.float32
F32R = mybir.dt.float32r
ALU = mybir.AluOpType
ACT = mybir.ActivationFunctionType
AX = mybir.AxisListType
EPS = 1e-6
NSLOT = 3
SLOT = 2048
NSTAGE = 4
ARENA = 14470


class Queue:

    def __init__(self, sem):
        self.sem, self.n, self.items, self.seen = sem, 0, [], {}

    def last(self):
        return (self.sem, self.n)

    def wait(self, *tokens):
        for t in tokens:
            if isinstance(t, list):
                self.wait(*t)
                continue
            sem, value = t
            if value > self.seen.get(id(sem), 0):
                self.seen[id(sem)] = value
                self.items.append(lambda e, s=sem, v=value: e.wait_ge(s, v))

    def do(self, fn, *tokens, chain=True):
        self.wait(*tokens)
        if chain:
            self.wait(self.last())
        self.n += 1
        self.items.append(lambda e, f=fn, s=self.sem: f(e).then_inc(s, 1))
        return self.last()

    def plain(self, fn):
        self.items.append(fn)

    def run(self, e):
        for f in self.items:
            f(e)


class Bank:
    clock = None

    def __init__(self, ap, banks, free):
        self.ap, self.banks, self.free = ap, banks, free
        self.w = [t for b in banks for t in free[b]]
        for b in banks:
            free[b] = None
        self.age = Bank.clock

    def release(self, *tokens):
        self.age[0] += 1
        for b in self.banks:
            self.free[b] = list(tokens)
            self.age[1 + b] = self.age[0]


def _params_layout():
    cols, at = {}, 0
    for name, n in [("attn_norm", 16), ("ffn_norm", 16), ("final_norm", 8), ("conv_w", 16), ("conv_b", 4),
                    ("ga_b", 4), ("gx_b", 4), ("lam", 4), ("b_ada", 48), ("norm_w2", 16), ("b_merge", 64),
                    ("qkn", 8), ("cvec", 16), ("sink", 8)]:
        cols[name] = (at, n)
        at += n
    return cols, at


def _consts_layout():
    cols, at = {}, 0
    for name, n in [("ident", 128), ("ones", 2), ("bones2", 2), ("bones", 128), ("p32", 128), ("p8", 128),
                    ("p16", 128), ("rcos", 256), ("rsin", 256), ("ncos", 256), ("nsin", 256), ("ecos", 15),
                    ("esin", 15), ("acos", 256), ("asin", 256), ("cmask", 256), ("emask", 30), ("evis", 2),
                    ("wmask", 1024), ("cs", 256), ("cn", 512), ("sn", 512), ("mhalf", 64), ("onerow", 64),
                    ("decay", 2048)]:
        cols[name] = (at, n)
        at += n
    return cols, at


def build(nc, A, out):
    ctx = ExitStack()
    with ctx:
        def sb(name, cols, dt=F32):
            return ctx.enter_context(nc.sbuf_tensor(name, [128, cols], dt))

        def sem(name):
            return ctx.enter_context(nc.semaphore(name))

        PL, PN = _params_layout()
        CL, CN = _consts_layout()
        ring = sb("ring", NSLOT * SLOT)
        par = sb("par", PN)
        con = sb("con", CN)
        X = sb("X", 4096)[:, :].rearrange("p (k n) -> p k n", k=8)
        XH = sb("XH", 4096, F32R)[:, :].rearrange("p (k n) -> p k n", k=8)
        XL = sb("XL", 4096, F32R)[:, :].rearrange("p (k n) -> p k n", k=8)
        WH = [sb(f"WH{i}", 2048, F32R)[:, :].rearrange("p (k c) -> p k c", k=8) for i in range(2)]
        WL = [sb(f"WL{i}", 2048, F32R)[:, :].rearrange("p (k c) -> p k c", k=8) for i in range(2)]
        stage = sb("stage", NSTAGE * 1024)
        MOD = sb("MOD", 96 + 64)
        SM = sb("SM", 640)
        arena = sb("arena", ARENA)
        psum = ctx.enter_context(nc.psum_tensor("psum", [128, 4096], F32))

        s_eng = [sem(n) for n in ("s_sp", "s_pe", "s_ve", "s_ac", "s_gp")]
        s_const = [sem(f"s_const{i}") for i in range(8)]
        s_slot = [sem(f"s_slot{i}") for i in range(NSLOT)]
        s_stage = [sem(f"s_stage{i}") for i in range(NSTAGE)]
        s_out = sem("s_out")

        def emit(order):
            SP, PE, VE, AC, GP = queues = [Queue(m) for m in s_eng]
            def P(name, i=0, n=1):
                a = PL[name][0] + i
                return par[:, a:a + n]

            def C(name, i=0, n=None):
                a, m = CL[name]
                return con[:, a + i:a + (m if n is None else i + n)]

            top = [0]

            def area(cols, shape=None, **dims):
                a = top[0]
                top[0] += cols
                assert top[0] <= ARENA, top[0]
                v = arena[:, a:a + cols]
                return v.rearrange(shape, **dims) if shape else v

            small_at = [0]

            def small(n):
                if small_at[0] + n > 640:
                    small_at[0] = 0
                a = small_at[0]
                small_at[0] += n
                return SM[:, a:a + n]

            bank_free = [[] for _ in range(8)]
            Bank.clock = [0] * 9

            def bank():
                b = min((b for b in range(8) if bank_free[b] is not None), key=lambda b: Bank.clock[1 + b])
                return Bank(psum[:, b * 512:(b + 1) * 512], [b], bank_free)

            def pair():
                b = min((b for b in range(0, 8, 2) if bank_free[b] is not None and bank_free[b + 1] is not None),
                        key=lambda b: max(Bank.clock[1 + b:3 + b]))
                return Bank(psum[:, b * 512:(b + 2) * 512], [b, b + 1], bank_free)

            slot_use = [[] for _ in range(NSLOT)]
            slot_n = [0] * NSLOT
            next_slot = [0]

            def load(src, shape, parts=None, **dims):
                i = next_slot[0] % NSLOT
                next_slot[0] += 1
                cols = src.shape[-1]
                SP.wait(slot_use[i])
                slot_use[i] = None
                view = ring[:, i * SLOT:i * SLOT + cols]
                for lo, hi in parts or [(0, 128)]:
                    slot_n[i] += 16
                    SP.plain(lambda e, d=ring[lo:hi, i * SLOT:i * SLOT + cols], s=src, m=s_slot[i]:
                             e.dma_start(d, s).then_inc(m, 16))
                return view.rearrange(shape, **dims), (s_slot[i], slot_n[i]), i

            def done(i, token):
                if isinstance(i, str):
                    w_use[int(i)] = [token]
                else:
                    slot_use[i] = [token]

            asked = []
            ready = {}
            w_use = [[], []]
            stage_use = [[] for _ in range(NSTAGE)]
            stage_n = [0] * NSTAGE
            next_stage = [0]

            def split(n, name, c):
                i = n % 2
                use, w_use[i] = w_use[i], None
                toks = []
                for h in range(2):
                    j = next_stage[0] % NSTAGE
                    next_stage[0] += 1
                    stage_n[j] += 16
                    src = A[name][c][:, h * 1024:(h + 1) * 1024]
                    raw = stage[:, j * 1024:(j + 1) * 1024]
                    SP.wait(stage_use[j])
                    SP.plain(lambda e, d=raw, s=src, m=s_stage[j]: e.dma_start(d, s).then_inc(m, 16))
                    raw = raw.rearrange("p (k c) -> p k c", k=4)
                    hi, lo = WH[i][:, 4 * h:4 * h + 4, :], WL[i][:, 4 * h:4 * h + 4, :]
                    t = copy(AC, hi, raw, (s_stage[j], stage_n[j]), use)
                    t2 = tt(VE, lo, raw, hi.bitcast(F32), ALU.subtract, t, use)
                    stage_use[j] = [t2]
                    toks.append([t, t2])
                return toks

            def wsplit(name, c):
                n = len(asked)
                asked.append((name, c))
                if order is None:
                    ready[n] = split(n, name, c)
                else:
                    while len(ready) < min(n + 2, len(order)):
                        ready[len(ready)] = split(len(ready), *order[len(ready)])
                return (WH[n % 2], WL[n % 2]), ready[n], str(n % 2)

            def product(dst, weights, cols, toks, k, tile, t_x, start, stop, turned, *w, sig=False):
                (wh, wl), (xh, xl) = weights, (XH, XL)
                a = [(wh, xh), (wh, xl), (wl, xh)] if not turned else [(wh, xh), (wl, xh), (wh, xl)]
                for n, (u, v) in enumerate(a):
                    u, v = u[:, k, cols], v[:, k, tile]
                    if turned:
                        u, v = v, u
                    t = mm(dst, u, v, start and n == 0, stop and n == 2, *w, toks[k // 4], t_x,
                           sig=(sig and n == 2))
                return t

            def barrier():
                tokens = [q.last() for q in (PE, VE, AC, GP)]
                for q in (PE, VE, AC, GP):
                    q.wait(tokens)
                top[0] = 0

            def mm(dst, lhsT, rhs, start, stop, *w, sig=False):
                PE.wait(*w)
                f = lambda e: e.matmul(dst, lhsT, rhs, start=start, stop=stop)
                if sig:
                    return PE.do(f, chain=False)
                PE.plain(f)

            def tr(dst, src, ident, *w, sig=False):
                PE.wait(*w)
                f = lambda e: e.transpose(dst, src, ident)
                if sig:
                    return PE.do(f, chain=False)
                PE.plain(f)

            def tt(q, dst, a, b, op, *w):
                return q.do(lambda e: e.tensor_tensor(dst, a, b, op), *w)

            def stt(dst, a, s, b, op0, op1, *w):
                return VE.do(lambda e: e.scalar_tensor_tensor(out=dst, in0=a, scalar=s, in1=b, op0=op0, op1=op1), *w)

            def ts(q, dst, a, s1, s2, op0, op1, *w):
                if s2 is None:
                    return q.do(lambda e: e.tensor_scalar(dst, a, s1, None, op0), *w)
                return q.do(lambda e: e.tensor_scalar(dst, a, s1, s2, op0, op1), *w)

            def act(dst, src, fn, *w, bias=0.0, scale=1.0, accum=None):
                if accum is None:
                    return AC.do(lambda e: e.activation(dst, src, fn, bias=bias, scale=scale), *w)
                return AC.do(lambda e: e.activation(dst, src, fn, bias=bias, scale=scale, accum_out=accum), *w)

            def copy(q, dst, src, *w):
                if q is AC:
                    return AC.do(lambda e: e.activation(dst, src, ACT.Copy), *w)
                return q.do(lambda e: e.tensor_copy(dst, src), *w)

            turn = [0]

            def evac(dst, src, *w):
                turn[0] ^= 1
                return copy(AC if turn[0] else VE, dst, src, *w)

            const_n = [0] * 8

            def cload(i, dst, src):
                const_n[i] += 16
                AC.plain(lambda e: e.dma_start(dst, src).then_inc(s_const[i], 16))
                return (s_const[i], const_n[i])

            x_in = A["xT"].rearrange("p (k n) -> p k n", k=8)
            c_in = A["ctxT"].rearrange("p (k n) -> p k n", k=8)
            t_x = cload(0, X[:, :, 0:256], x_in)
            t_par = cload(1, par[:, :], A["params"])
            cut = CL["decay"][0]
            t_con = cload(2, con[:, 0:cut], A["consts"][:, 0:cut])
            t_dec = cload(3, con[:, cut:CN], A["consts"][:, cut:CN])
            t_ctx = cload(4, X[:, :, 256:512], c_in)
            ident = C("ident")
            PE.wait(t_con)
            VE.wait(t_con, t_par)
            AC.wait(t_con, t_par)
            GP.wait(t_con, t_par)

            def power(n, src, *w):
                r = small(n)
                return r, tt(GP, r, src, C("mhalf", 0, n), ALU.pow, *w)

            def inv_rms(src, sq, t_src):
                toks = []
                for j, q in enumerate((AC, VE, GP, AC)):
                    d, s = sq[:, 2 * j:2 * j + 2, :], src[:, 2 * j:2 * j + 2, :]
                    if q is AC:
                        toks.append(act(d, s, ACT.Square, t_src))
                    else:
                        toks.append(tt(q, d, s, s, ALU.mult, t_src))
                b = bank()
                for n in range(2):
                    for k in range(8):
                        t = mm(b.ap[:, n:n + 1], sq[:, k, n * 128:(n + 1) * 128], C("ones", 0, 1), k == 0, k == 7,
                               b.w, toks[k // 2], sig=(n == 1 and k == 7))
                ms = small(2)
                t = ts(VE, ms, b.ap[:, 0:2], 1.0 / 1024, EPS, ALU.mult, ALU.add, t)
                b.release(t)
                r, t = power(2, ms, t)
                wide = small(256).rearrange("p (a n) -> p a n", a=2)
                t = copy(VE, wide, r.rearrange("p (a n) -> p a n", n=1).to_broadcast([128, 2, 128]), t)
                b = bank()
                for n in range(2):
                    t2 = mm(b.ap[:, n * 128:(n + 1) * 128], wide[:, n, :], ident, True, True, b.w, t, sig=(n == 1))
                return b, t2

            def norm(src, sq, gain, t_src, shift=None, cs=slice(0, 256)):
                b, t = inv_rms(src, sq, t_src)
                toks = []
                for k in range(8):
                    f = sq[:, k, :]
                    t1 = stt(f, src[:, k, :], gain(k), b.ap[:, 0:256], ALU.mult, ALU.mult, t)
                    if shift is not None:
                        t1 = ts(VE, f, f, shift(k), None, ALU.add, None)
                    t2 = copy(AC, XH[:, k, cs], f, t1)
                    t3 = tt(GP, XL[:, k, cs], f, XH[:, k, cs].bitcast(F32), ALU.subtract, t2)
                    toks.append([t2, t3])
                b.release(t1)
                return toks

            def plain_norm(src, sq, gain, t_src):
                b, t = inv_rms(src, sq, t_src)
                for k in range(8):
                    t1 = stt(src[:, k, :], src[:, k, :], gain(k), b.ap[:, 0:256], ALU.mult, ALU.mult, t)
                b.release(t1)
                return t1

            def feats(dst_cols, chunk, t_w, rhs, t_rhs, b, nk=8, m0=0, n=256):
                for j, c in enumerate(dst_cols):
                    for k in range(nk):
                        t = mm(b.ap[:, j * n:(j + 1) * n], chunk[:, k, c:c + 128], rhs(k), k == 0, k == nk - 1,
                               b.w, t_w, t_rhs[k] if isinstance(t_rhs, list) and len(t_rhs) == nk else t_rhs,
                               sig=(k == nk - 1))
                return t

            def feats3(dst_cols, weights, toks, t_x, b, n=256):
                for j, c in enumerate(dst_cols):
                    for k in range(8):
                        t = product(b.ap[:, j * n:(j + 1) * n], weights, slice(c, c + 128), toks, k, slice(0, n),
                                    t_x[k], k == 0, k == 7, False, b.w, sig=(k == 7))
                return t

            def rows3(b, weights, toks, t_x, tiles, cols, width):
                for j, n in enumerate(tiles):
                    for k in range(8):
                        t = product(b.ap[:, j * width:(j + 1) * width], weights, cols, toks, k,
                                    slice(n * 128, n * 128 + 128), t_x[k], k == 0, k == 7, True, b.w, sig=(k == 7))
                return t

            def wchunk(name, i):
                return load(A[name][i], "p (k c) -> p k c", k=8)

            def residual(name, rhs, t_rhs):
                for c in range(4):
                    w, t_w, i = wchunk(name, c)
                    b = bank()
                    t = feats([0, 128], w, t_w, rhs, t_rhs, b)
                    done(i, t)
                    v = b.ap.rearrange("p (a n) -> p a n", a=2)
                    t = tt(VE, X[:, 2 * c:2 * c + 2, 0:256], v, X[:, 2 * c:2 * c + 2, 0:256], ALU.add, t)
                    b.release(t)
                return t

            def rope(raw, tmp, nt, perm, cos, sin, t_raw, n=256):
                toks = []
                per = 512 // n
                for j in range(0, nt, per):
                    m = min(per, nt - j)
                    b = bank()
                    bv = b.ap[:, 0:m * n].rearrange("p (a n) -> p a n", a=m)
                    t = mm(bv, perm, raw[:, j:j + m, :], True, True, b.w, t_raw, sig=True)
                    s3 = sin.rearrange("p (a n) -> p a n", a=1).to_broadcast([128, m, n])
                    c3 = cos.rearrange("p (a n) -> p a n", a=1).to_broadcast([128, m, n])
                    t1 = tt(VE, tmp[:, j:j + m, :], bv, s3, ALU.mult, t)
                    b.release(t1)
                    t2 = tt(GP, raw[:, j:j + m, :], raw[:, j:j + m, :], c3, ALU.mult, t)
                    toks.append(tt(GP, raw[:, j:j + m, :], raw[:, j:j + m, :], tmp[:, j:j + m, :], ALU.add, t1, t2))
                return toks[-1]

            def hybrid():
                barrier()
                four = dict(shape="p (a n) -> p a n", a=4)
                xr = area(4 * 260, **four)
                conv = area(1024, **four)
                gr, gi = area(1024, **four), area(1024, **four)
                aa, uu = area(1024, **four), area(1024, **four)
                cat = area(2048, "p (a n) -> p a n", a=8)
                t_xn = norm(X[:, :, 0:256], cat, lambda k: P("attn_norm", k), t_x)
                qq, kk, gg = [area(1024, **four) for _ in range(3)]
                ro, sq = gr, gi
                vv = area(1024, "p (t c) -> p t c", t=2)
                tmp = area(1024, **four)
                tmp2 = area(1024, **four)
                sT = [v.rearrange("p a n -> p (a n)")[:, 0:768].rearrange("p (h c) -> p h c", h=2)
                      for v in (aa, uu)]
                rx = xr.rearrange("p a n -> p (a n)")[:, 0:1024].rearrange("p (t h d) -> p t h d", t=2, h=8)
                gates, t_gates, gslot = load(A["lru_gates"], "p (g t c) -> p g t c", g=2, t=4)
                t_pad = GP.do(lambda e: e.memset(xr[:, :, 0:3], 0.0))
                sp = small(4)
                neg, e_, z_, z2 = small(4), small(4), small(4), small(4)
                ts(VE, neg, P("lam", 0, 4), -1.0, None, ALU.mult, None)
                t = tt(VE, e_, neg, P("lam", 0, 4), ALU.min)
                t = act(e_, e_, ACT.Exp, t)
                ts(VE, z_, e_, 2.0, None, ALU.add, None, t)
                VE.do(lambda e: e.reciprocal(z_, z_))
                tt(VE, z_, z_, e_, ALU.mult)
                tt(VE, z2, z_, z_, ALU.mult)
                ts(VE, sp, z2, 16.0 / 15, 16.0 / 13, ALU.mult, ALU.add)
                for n in (11, 9, 7, 5, 3, 1):
                    tt(VE, sp, sp, z2, ALU.mult)
                    ts(VE, sp, sp, 16.0 / n, None, ALU.add, None)
                tt(VE, sp, sp, z_, ALU.mult)
                ts(VE, neg, neg, 0.0, 8.0, ALU.max, ALU.mult)
                t_sp = tt(VE, sp, sp, neg, ALU.add)

                def project(c, fn):
                    w, t_w, i = wsplit("ab_in", c)
                    b = bank()
                    t = feats3([0, 128], w, t_w, t_xn, b)
                    done(i, t)
                    t = fn(b.ap.rearrange("p (a n) -> p a n", a=2), t)
                    b.release(t)
                    return t

                toks = [project(2 + j, lambda v, t: evac(xr[:, 2 * j:2 * j + 2, 3:259], v, t)) for j in range(2)]
                for t_ in range(4):
                    w = lambda k: P("conv_w", t_ * 4 + k)
                    ts(VE, conv[:, t_, :], xr[:, t_, 0:256], w(0), P("conv_b", t_), ALU.mult, ALU.add, t_pad, toks[t_ // 2])
                    for k in range(1, 4):
                        t_conv = stt(conv[:, t_, :], xr[:, t_, k:k + 256], w(k), conv[:, t_, :], ALU.mult, ALU.add)
                for g, dst, bias in ((0, gr, "ga_b"), (1, gi, "gx_b")):
                    for j in range(2):
                        b = bank()
                        for h in range(2):
                            t = mm(b.ap[:, h * 256:(h + 1) * 256], gates[:, g, 2 * j + h, :], conv[:, 2 * j + h, :],
                                   True, True, b.w, t_gates, t_conv, sig=True)
                        for h in range(2):
                            t2 = act(dst[:, 2 * j + h, :], b.ap[:, h * 256:(h + 1) * 256], ACT.Sigmoid, t,
                                     bias=P(bias, 2 * j + h))
                        b.release(t2)
                done(gslot, t)
                for t_ in range(4):
                    ts(VE, gr[:, t_, :], gr[:, t_, :], sp[:, t_:t_ + 1], None, ALU.mult, None, t2, t_sp)
                t_s = VE.last()
                t_a = act(aa, gr, ACT.Exp, t_s, scale=-1.0)
                t_t = act(gr, gr, ACT.Tanh)
                tt(VE, uu, aa, aa, ALU.mult, t_a)
                t = stt(uu, uu, 1.0, gr, ALU.add, ALU.mult, t_t)
                t_g = tt(GP, gi, gi, conv, ALU.mult, t2, t_conv)
                t = act(uu, uu, ACT.Sqrt, t)
                tt(VE, uu, uu, gi, ALU.mult, t, t_g)
                for t_ in range(4):
                    t_scan = VE.do(lambda e, a=t_: e.tensor_tensor_scan(conv[:, a, :], aa[:, a, :], uu[:, a, :], 0.0,
                                                                        ALU.mult, ALU.add))
                tq = [project(4 + j, lambda v, t: evac(qq[:, 2 * j:2 * j + 2, :], v, t)) for j in range(2)]
                tk = [project(6 + j, lambda v, t: evac(kk[:, 2 * j:2 * j + 2, :], v, t)) for j in range(2)]
                t_q = rope(qq, tmp, 4, C("p32"), C("rcos"), C("rsin"), tq)
                t_k = rope(kk, tmp2, 4, C("p32"), C("rcos"), C("rsin"), tk)
                tv = []
                for j in range(2):
                    w, t_w, i = wsplit("ab_in", 8 + j)
                    b = bank()
                    t = rows3(b, w, t_w, t_xn, (0, 1), slice(0, 256), 256)
                    done(i, t)
                    tv.append(evac(vv[:, :, j * 256:(j + 1) * 256], b.ap.rearrange("p (t c) -> p t c", t=2), t))
                    b.release(tv[-1])
                tg = [project(10 + j, lambda v, t: act(gg[:, 2 * j:2 * j + 2, :], v, ACT.Silu, t)) for j in range(2)]
                ty = [project(j, lambda v, t: act(cat[:, 2 * j:2 * j + 2, :], v, ACT.Gelu_apprx_tanh, t, t_xn[7]))
                      for j in range(2)]
                t_lru = tt(GP, cat[:, 0:4, :], cat[:, 0:4, :], conv, ALU.mult, ty, t_scan)
                t_pv = [[], []]
                for t_ in range(4):
                    pr = pair()
                    for p in range(2):
                        r = slice(p * 64, p * 64 + 64)
                        c = p * 512
                        mm(pr.ap[:, c:c + 256], kk[r, t_, 0:128], qq[r, t_, 0:256], True, True, pr.w, t_q, t_k)
                        t = mm(pr.ap[:, c + 256:c + 384], kk[r, t_, 128:256], qq[r, t_, 128:256], True, True, sig=True)
                    v = pr.ap.rearrange("p (h c) -> p h c", h=2)
                    s = sT[t_ % 2]
                    dec = C("decay").rearrange("p (h c) -> p h c", h=8)[:, 2 * t_:2 * t_ + 2, :]
                    tt(VE, s[:, :, 0:256], v[:, :, 0:256], dec, ALU.mult, t, t_dec, t_pv[t_ % 2])
                    t = tt(VE, s[:, :, 256:384], v[:, :, 256:384], dec[:, :, 0:128], ALU.mult)
                    pr.release(t)
                    b = bank()
                    for p in range(2):
                        r = slice(p * 64, p * 64 + 64)
                        vc = (2 * t_ + p) * 64
                        mm(b.ap[r, 0:256], vv[:, 0, vc:vc + 64], s[:, p, 0:256], True, False, b.w, t, tv)
                        t2 = mm(b.ap[r, 128:256], vv[:, 1, vc:vc + 64], s[:, p, 256:384], False, True, sig=True)
                    t_pv[t_ % 2] = [t2]
                    t_ro = copy(AC, ro[:, t_, :], b.ap[:, 0:256], t2, t_scan, t_g)
                    b.release(t_ro)
                for j in range(2):
                    b = bank()
                    v = b.ap.rearrange("p (a n) -> p a n", a=2)
                    t = mm(v, C("bones"), ro[:, 2 * j:2 * j + 2, :], True, True, b.w, t_ro, sig=True)
                    t = stt(ro[:, 2 * j:2 * j + 2, :], v, -1.0, ro[:, 2 * j:2 * j + 2, :], ALU.mult, ALU.add, t)
                    b.release(t)
                    t_sq = act(sq[:, 2 * j:2 * j + 2, :], ro[:, 2 * j:2 * j + 2, :], ACT.Square, t)
                t_ro = t
                b = bank()
                for n in range(2):
                    for a in range(4):
                        c = n * 8 + 2 * a
                        t = mm(b.ap[:, c:c + 2], sq[:, a, n * 128:(n + 1) * 128], C("bones2"), True, True, b.w, t_sq,
                               sig=True)
                ms = small(16)
                t = ts(VE, ms, b.ap[:, 0:16], 1.0, EPS, ALU.mult, ALU.add, t)
                b.release(t)
                r, t = power(16, ms, t)
                t = copy(VE, rx, r.rearrange("p (t h d) -> p t h d", t=2, d=1).to_broadcast([128, 2, 8, 64]), t)
                for j in range(2):
                    b = bank()
                    v = b.ap.rearrange("p (a n) -> p a n", a=2)
                    for h in range(2):
                        for n in range(2):
                            a = 2 * j + h
                            t2 = mm(v[:, h, n * 128:(n + 1) * 128], rx[:, n, 2 * a:2 * a + 2, :], ident, True, True,
                                    b.w, t, sig=True)
                    t3 = tt(VE, ro[:, 2 * j:2 * j + 2, :], v, ro[:, 2 * j:2 * j + 2, :], ALU.mult, t2, t_ro)
                    b.release(t3)
                    t_ret = tt(VE, cat[:, 4 + 2 * j:6 + 2 * j, :], ro[:, 2 * j:2 * j + 2, :], gg[:, 2 * j:2 * j + 2, :],
                               ALU.mult, tg)
                return residual("ab_out", lambda k: cat[:, k, :], [t_lru, t_ret])

            def ffn(l, t_h):
                barrier()
                SQ = area(2048, "p (a n) -> p a n", a=8)
                t_xn = norm(X[:, :, 0:256], SQ, lambda k: P("ffn_norm", 8 * l + k), t_h)
                hh = area(22 * 256, "p (a n) -> p a n", a=22)
                sg = [area(512) for _ in range(2)]
                t_free = [[], []]
                t_hh = []
                for c in range(11):
                    w, t_w, i = wsplit(f"w1_{l}", c)
                    b1 = bank()
                    t1 = feats3([0, 128], w, t_w, t_xn, b1)
                    done(i, t1)
                    w, t_w, i = wsplit(f"w3_{l}", c)
                    b3 = bank()
                    t3 = feats3([0, 128], w, t_w, t_xn, b3)
                    done(i, t3)
                    s = sg[c % 2]
                    t = act(s, b1.ap, ACT.Silu, t1, t_free[c % 2])
                    b1.release(t)
                    d = hh[:, 2 * c:2 * c + 2, :].rearrange("p a n -> p (a n)")
                    t = tt(VE, d, s, b3.ap, ALU.mult, t, t3)
                    b3.release(t)
                    t_free[c % 2] = [t]
                    t_hh += [t, t]
                for m in range(8):
                    b = bank()
                    for h in range(2):
                        w, t_w, i = load(A[f"w2_{l}"][m][:, h * 1408:(h + 1) * 1408], "p (k c) -> p k c", k=11)
                        for k in range(11):
                            q_ = 11 * h + k
                            t = mm(b.ap[:, 0:256], w[:, k, :], hh[:, q_, :], q_ == 0, q_ == 21, b.w, t_w, t_hh[q_],
                                   sig=(k == 10))
                        done(i, t)
                    t = tt(VE, X[:, m, 0:256], b.ap[:, 0:256], X[:, m, 0:256], ALU.add, t)
                    b.release(t)
                return t

            def attend(units, S, T, t_S, t_T):
                N = len(units)
                scored, sums, t_exp, t_turn, t_copied, t_value = {}, {}, {}, {}, {}, {}

                def probs(n):
                    heads, J = units[n][2], units[n][3]
                    return S[n % 3][:, 0:heads * J].rearrange("p (h j) -> p h j", h=heads)

                def maximum_and_exp(n):
                    heads, J, mask, sink = units[n][2:6]
                    b, t_score = scored[n]
                    v = b.ap.rearrange("p (h j) -> p h j", h=heads)[:, :, 0:J]
                    s = probs(n)
                    t_s = t_turn[n - 3] if n >= 3 else t_S
                    nm, sm, se = small(heads), small(heads), small(heads)
                    if mask is not None:
                        m3 = mask.rearrange("p (a j) -> p a j", a=1).to_broadcast([128, heads, J])
                        t = stt(s, v, 0.125, m3, ALU.mult, ALU.add, t_score, t_s)
                        b.release(t)
                        VE.do(lambda e: e.tensor_reduce(nm, s, AX.X, ALU.max))
                        src, scale = s, 1.0
                    else:
                        VE.do(lambda e: e.tensor_reduce(nm, v, AX.X, ALU.max), t_score, t_s)
                        src, scale = v, 0.125
                    if sink is not None:
                        if mask is None:
                            ts(VE, nm, nm, 0.125, None, ALU.mult, None)
                        tt(VE, nm, nm, sink, ALU.max)
                        t_max = ts(VE, nm, nm, -1.0, None, ALU.mult, None)
                        t_sink = tt(VE, se, sink, nm, ALU.add)
                    else:
                        t_max = ts(VE, nm, nm, -scale, None, ALU.mult, None)
                    for h in range(heads):
                        t = act(s[:, h, :], src[:, h, :], ACT.Exp, t_max, bias=nm[:, h:h + 1], scale=scale,
                                accum=sm[:, h:h + 1])
                    if mask is None:
                        b.release(t)
                    if sink is not None:
                        t = act(se, se, ACT.Exp, t_sink)
                    t_exp[n] = t
                    sums[n] = (sm, se)

                def scale_and_turn(n):
                    heads, J, _, sink, gate, rowvis = units[n][2:8]
                    sm, se = sums[n]
                    s = probs(n)
                    if sink is not None:
                        tt(VE, sm, sm, se, ALU.add, t_exp[n])
                    VE.do(lambda e: e.reciprocal(sm, sm), t_exp[n])
                    if gate is not None:
                        tt(VE, sm, sm, gate, ALU.mult)
                    if rowvis is not None:
                        ts(VE, sm, sm, rowvis, None, ALU.mult, None)
                    sm3 = sm.rearrange("p (h a) -> p h a", a=1).to_broadcast([128, heads, J])
                    t_scaled = tt(VE, s, s, sm3, ALU.mult)
                    nj = (J + 127) // 128
                    kp = min(J, 128)
                    w = heads * 128
                    b = pair() if nj * w > 512 else bank()
                    for jt in range(nj):
                        for h in range(heads):
                            c = jt * w + h * 128
                            t = tr(b.ap[0:kp, c:c + 128], s[:, h, jt * 128:jt * 128 + kp], ident, b.w, t_scaled,
                                   sig=(jt == nj - 1 and h == heads - 1))
                    t_turn[n] = t
                    t_copied[n] = copy(AC, T[n % 2][0:kp, 0:nj * w], b.ap[0:kp, 0:nj * w], t,
                                       t_value[n - 2] if n >= 2 else t_T)
                    b.release(t_copied[n])

                scored[0] = units[0][0]()
                for n in range(N + 2):
                    if n + 1 < N:
                        scored[n + 1] = units[n + 1][0]()
                    if n < N:
                        maximum_and_exp(n)
                    if 1 <= n <= N:
                        scale_and_turn(n - 1)
                    if n >= 2:
                        t_value[n - 2] = units[n - 2][1](T[n % 2], t_copied[n - 2])

            def nsa(t_h):
                barrier()
                two = dict(shape="p (a n) -> p a n", a=2)
                q = area(2048, "p (a n) -> p a n", a=8)
                tmp = area(2048, "p (a n) -> p a n", a=8)
                att = tmp
                t_xn = norm(X[:, :, 0:256], tmp, lambda k: P("attn_norm", 8 + k), t_h)
                over = top[0]
                kc, vc = [area(512, **two) for _ in range(2)]
                bufk, bufv = [area(960, "p (l n) -> p l n", l=32) for _ in range(2)]
                vs, vw = [area(512, "p (t c) -> p t c", t=2) for _ in range(2)]
                ks, kw = [area(512, **two) for _ in range(2)]
                gk, gv = area(30), area(30)
                kcT = area(30, **two)
                kct = area(30, **two)
                vcs = area(256, "p (g d) -> p g d", g=4)
                gt = area(96, "p (t c) -> p t c", t=2)
                pe2 = area(64)
                t_pe = cload(5, pe2[0:64, :], A["pe"])
                t_pe = cload(5, pe2[64:128, :], A["pe"])
                S = [area(1024) for _ in range(3)]
                T = [arena[:, over + 1024 * n:over + 1024 * (n + 1)] for n in range(2)]

                def fm(c, dst):
                    w, t_w, i = wsplit("nsa_in", c)
                    b = bank()
                    t = feats3([0, 128], w, t_w, t_xn, b)
                    done(i, t)
                    t = evac(dst, b.ap.rearrange("p (a n) -> p a n", a=2), t)
                    b.release(t)
                    return t

                def tm(c, dst):
                    w, t_w, i = wsplit("nsa_in", c)
                    b = bank()
                    t = rows3(b, w, t_w, t_xn, (0, 1), slice(0, 256), 256)
                    done(i, t)
                    t = evac(dst, b.ap.rearrange("p (t c) -> p t c", t=2), t)
                    b.release(t)
                    return t

                w, t_w, i = wsplit("nsa_gates", 0)
                b = bank()
                t = rows3(b, w, t_w, t_xn, (0, 1), slice(0, 64), 64)
                done(i, t)
                t_gt = act(gt, b.ap[:, 0:128].rearrange("p (t c) -> p t c", t=2)[:, :, 0:48], ACT.Sigmoid, t)
                b.release(t_gt)
                t_kc, t_vc = fm(4, kc), fm(5, vc)
                t_ks, t_kw = fm(6, ks), fm(8, kw)
                t_ks = rope(ks, tmp[:, 0:2, :], 2, C("p8"), C("ncos"), C("nsin"), t_ks)
                t_kw = rope(kw, tmp[:, 2:4, :], 2, C("p8"), C("ncos"), C("nsin"), t_kw)
                for src, dst, pe, t in ((kc, bufk, 0, t_kc), (vc, bufv, 1, t_vc)):
                    for a in range(2):
                        for lh in range(2):
                            sv = src[:, a, lh * 16:lh * 16 + 240].rearrange("p (n l) -> p l n", l=16)
                            pv = pe2[:, pe * 32 + lh * 16:pe * 32 + lh * 16 + 16].rearrange("p (l a) -> p l a", a=1)
                            t_b = tt(VE, dst[:, lh * 16:lh * 16 + 16, a * 15:a * 15 + 15], sv,
                                     pv.to_broadcast([128, 16, 15]), ALU.add, t, t_pe)
                t_g2 = []
                halves = [(0, 64), (64, 128)]
                for src, g2, name in ((bufk, gk, "cmp_k1"), (bufv, gv, "cmp_v1")):
                    w, t_w, i = load(A[name], "p (l c) -> p l c", parts=halves, l=32)
                    for p in range(2):
                        r = slice(p * 64, p * 64 + 64)
                        b = bank()
                        for l in range(32):
                            t = mm(b.ap[r, 0:30], w[r, l, :], src[r, l, :], l == 0, l == 31, b.w, t_w, t_b,
                                   sig=(l == 31))
                        t2 = act(g2[r, :], b.ap[r, 0:30], ACT.Gelu_apprx_tanh, t)
                        b.release(t2)
                    done(i, t)
                    t_g2.append(t2)
                w2, t_w2, i = load(A["cmp_w2"], "p (a c) -> p a c", parts=halves, a=2)
                for p in range(2):
                    r = slice(p * 64, p * 64 + 64)
                    b = bank()
                    t = mm(b.ap[r, 0:30], w2[r, 0, :], gk[r, :], True, True, b.w, t_w2, t_g2, sig=True)
                    t_kc = copy(VE, kcT[r, :, :], b.ap[r, 0:30].rearrange("p (a n) -> p a n", a=2), t)
                    b.release(t_kc)
                    b = bank()
                    for a in range(2):
                        t = mm(b.ap[0:15, a * 64:a * 64 + 64], gv[r, a * 15:a * 15 + 15], w2[r, 1, :], True, True, b.w,
                               sig=True)
                    for a in range(2):
                        t_vc = copy(VE, vcs[0:15, 2 * a + p, :], b.ap[0:15, a * 64:a * 64 + 64], t)
                    b.release(t_vc)
                done(i, t)
                t_kc = rope(kcT, kct, 2, C("p8"), C("ecos"), C("esin"), t_kc, n=15)
                t_T = [PE.last(), VE.last()]
                t_vs, t_vw = tm(7, vs), tm(9, vw)
                tq = [fm(c, q[:, 2 * c:2 * c + 2, :]) for c in range(4)]
                t_q = rope(q, tmp, 8, C("p8"), C("ncos"), C("nsin"), [t_ks, t_kw] + tq)

                units = []
                t_out = [None]

                def group(it, g):
                    p, t2_ = g % 2, g // 2
                    r = slice(p * 64, p * 64 + 64)
                    out = [None]
                    J = 128 * (it + 1)

                    def branch(br, k_, v_, tk_, tv_):
                        Jb = 15 if br == 0 else J
                        W = 128 if br == 0 else 256

                        def scores():
                            pr = bank() if br == 0 else pair()
                            for h in range(4):
                                t = mm(pr.ap[:, h * W:h * W + Jb], q[r, t2_ * 4 + h, it * 128:it * 128 + 128],
                                       k_[r, t2_, 0:Jb], True, True, pr.w, t_q, tk_, sig=(h == 3))
                            return pr, t

                        def values(T, t_T):
                            if br == 0:
                                out[0] = bank()
                            b = out[0]
                            if br == 0:
                                return mm(b.ap[r, :], v_[0:15, g, :], T[0:15, 0:512], True, False, b.w, t_T, tv_,
                                          sig=True)
                            for jt in range(it + 1):
                                t = mm(b.ap[r, :], v_[:, jt, g * 64:g * 64 + 64], T[:, jt * 512:(jt + 1) * 512], False,
                                       br == 2 and jt == it, t_T, tv_, sig=(jt == it))
                            if br == 2:
                                t_out[0] = copy(VE, att[r, t2_ * 4:t2_ * 4 + 4, it * 128:it * 128 + 128],
                                                b.ap[r, :].rearrange("p (h n) -> p h n", h=4), t, t_q)
                                b.release(t_out[0])
                            return t

                        gate = gt[:, it, g * 12 + br:g * 12 + 12:3]
                        if br == 0:
                            return scores, values, 4, 15, C("emask", it * 15, 15), None, gate, C("evis", it, 1)
                        return scores, values, 4, J, C("cmask", 0 if it else 128, J), None, gate, None

                    return [branch(0, kcT, vcs, t_kc, t_vc), branch(1, ks, vs, t_ks, t_vs),
                            branch(2, kw, vw, t_kw, t_vw)]

                VE.wait(t_gt)
                for it in range(2):
                    for g in range(4):
                        units += group(it, g)
                attend(units, S, T, [], t_T)
                t = t_out[0]
                return residual("nsa_out", lambda k: att[:, k, :], t)

            def modulation():
                barrier()
                sc = small(16)
                t_c = act(sc, P("cvec", 0, 16), ACT.Silu)
                s2 = sc.rearrange("p (k v) -> p k v", v=2)
                toks = []
                row = area(3072)
                t = []
                for l in range(2):
                    t_row = []
                    for c in range(12):
                        w, t_w, i = wchunk(f"ada_{l}", c)
                        b = bank()
                        for k in range(8):
                            t1 = mm(b.ap[0:2, 0:256], s2[:, k, :], w[:, k, :], k == 0, k == 7, b.w, t_w, t_c, sig=(k == 7))
                        done(i, t1)
                        t_row.append(evac(row[0:2, c * 256:(c + 1) * 256], b.ap[0:2, 0:256], t1, t))
                        b.release(t_row[-1])
                    b = bank()
                    for m in range(24):
                        t1 = tr(b.ap[:, 2 * m:2 * m + 2], row[0:2, m * 128:(m + 1) * 128], C("ident")[0:2, 0:2], b.w,
                                t_row[m // 2], sig=(m == 23))
                    t = [t1]
                    m3 = MODS[l]
                    bias = P("b_ada", 24 * l, 24).rearrange("p (m a) -> p m a", a=1).to_broadcast([128, 24, 2])
                    t1 = tt(VE, m3, b.ap[:, 0:48].rearrange("p (m v) -> p m v", v=2), bias, ALU.add, t1)
                    b.release(t1)
                    nw = P("norm_w2", 8 * l, 8).rearrange("p (m a) -> p m a", a=1).to_broadcast([128, 8, 2])
                    toks.append(stt(m3[:, 8:16, :], m3[:, 8:16, :], 1.0, nw, ALU.add, ALU.mult))
                return toks

            MODS = [MOD[:, 0:48].rearrange("p (m v) -> p m v", v=2), MOD[:, 48:96].rearrange("p (m v) -> p m v", v=2)]

            def layer(l, t_h):
                NT = 512 if l == 0 else 256
                NC = 512
                nt = NT // 128
                barrier()
                base = top[0]
                m3 = MODS[l]
                SQ = area(2048, "p (a n) -> p a n", a=8)
                t_H = [[] for _ in range(8)]
                for v in range(2):
                    cs = slice(v * 256, v * 256 + 256)
                    toks = norm(X[:, :, cs], SQ, lambda k: m3[:, 8 + k, v:v + 1], [PE.last(), GP.last()] + t_h,
                                shift=lambda k: m3[:, k, v:v + 1], cs=cs)
                    t_H = [a + b for a, b in zip(t_H, toks)]
                top[0] = base
                barrier()
                Z = area(8 * NT, "p (r a n) -> p r a n", r=4, a=2)
                tail = top[0]
                R = [area(1536, "p (a n) -> p a n", a=3) for _ in range(2)]
                V = [area(512, "p (t c) -> p t c", t=4) for _ in range(2)]
                mid = top[0]

                def fm(w, t_w, cols, n, n0=0):
                    b = bank()
                    return b, feats3([cols], w, t_w, t_H, b, n=n)

                t_z = []
                for r, c in enumerate((2, 5, 7, 10)):
                    w, t_w, i = wsplit(f"in_{l}", c)
                    for a in range(2):
                        b, t = fm(w, t_w, a * 128, NT)
                        t1 = act(Z[:, r, a, :], b.ap[:, 0:NT], ACT.Silu, t)
                        b.release(t1)
                        t_z.append(t1)
                    done(i, t)
                U = area(2 * NT, "p (a n) -> p a n", a=2)
                VT = area(256 * nt, "p (t c) -> p t c", t=nt)
                w, t_w, i = wsplit(f"in_{l}", 8)
                for a in range(2):
                    b, t = fm(w, t_w, a * 128, NT)
                    t_u = act(U[:, a, :], b.ap[:, 0:NT], ACT.Gelu, t)
                    b.release(t_u)
                done(i, t)
                w, t_w, i = wsplit(f"in_{l}", 9)
                for j in range(nt // 2):
                    b = bank()
                    t = rows3(b, w, t_w, t_H, (2 * j, 2 * j + 1), slice(0, 256), 256)
                    t_v = act(VT[:, 2 * j:2 * j + 2, :], b.ap.rearrange("p (t c) -> p t c", t=2), ACT.Gelu, t)
                    b.release(t_v)
                done(i, t)
                t_zu = tt(GP, Z[:, 3, :, :], Z[:, 3, :, :], U, ALU.mult, t_z, t_u)
                w, t_w, i = load(A[f"sp_{l}"], "p (g q) -> p g q", g=4)
                bsp, t_bsp, i2 = load(A[f"bsp_{l}"], "p (g q) -> p g q", parts=[(0, 1)], g=4)
                for a in range(2):
                    b = bank()
                    for n in range(nt):
                        for h in range(2):
                            g = 2 * a + h
                            r = slice(h * 64, h * 64 + 64)
                            mm(b.ap[r, n * 128:(n + 1) * 128], VT[:, n, g * 64:g * 64 + 64], w[:, g, :], True, False,
                               b.w, t_w, t_v)
                            t = mm(b.ap[r, n * 128:(n + 1) * 128], C("onerow")[0:1, :], bsp[0:1, g, :], False, True,
                                   t_bsp, sig=True)
                    t_yc = tt(VE, Z[:, 3, a, :], b.ap[:, 0:NT], Z[:, 3, a, :], ALU.mult, t, t_zu)
                    b.release(t_yc)
                done(i, t)
                done(i2, t)
                barrier()
                top[0] = mid
                Fm = area(2 * NT, "p (a n) -> p a n", a=2)
                ZZ = area(1024, "p (t a c) -> p t a c", t=2, a=2)
                Y = area(512, "p (a n) -> p a n", a=2)
                w, t_w, i = wsplit(f"in_{l}", 6)
                for a in range(2):
                    b, t = fm(w, t_w, a * 128, NT)
                    t_f = evac(Fm[:, a, :], b.ap[:, 0:NT], t)
                    t_f2 = t_f if a == 0 else [t_f, t_f2]
                    b.release(t_f)
                done(i, t)
                w, t_w, i = load(A[f"fnet_{l}"], "p (a c) -> p a c", a=2)
                for v in range(NT // 256):
                    for n in range(2):
                        b = bank()
                        for a in range(2):
                            c = v * 256 + n * 128
                            t = mm(b.ap[:, a * 256:(a + 1) * 256], Fm[:, a, c:c + 128], C("cs"), True, True, b.w, t_f2,
                                   sig=True)
                        t = copy(VE, ZZ[:, n, :, :], b.ap.rearrange("p (a c) -> p a c", a=2), t, PE.last())
                        b.release(t)
                    b = bank()
                    for a in range(2):
                        for n in range(2):
                            mm(b.ap[:, a * 256:(a + 1) * 256], ZZ[:, n, a, 0:128], C("cn", n * 256, 256), n == 0, False,
                               b.w, t)
                            t2 = mm(b.ap[:, a * 256:(a + 1) * 256], ZZ[:, n, a, 128:256], C("sn", n * 256, 256), False,
                                    n == 1, sig=True)
                    t = copy(VE, Y, b.ap.rearrange("p (a n) -> p a n", a=2), t2, PE.last())
                    b.release(t)
                    b = bank()
                    for a in range(2):
                        t2 = mm(b.ap[:, a * 256:(a + 1) * 256], w[:, a, :], Y[:, a, :], True, True, b.w, t, t_w, sig=True)
                    zz = Z[:, 2, :, v * 256:v * 256 + 256]
                    t = tt(VE, zz, b.ap.rearrange("p (a n) -> p a n", a=2), zz, ALU.mult, t2, t_z)
                    b.release(t)
                done(i, t2)
                barrier()
                top[0] = mid
                S3 = area(1536, "p (a n) -> p a n", a=3)
                T3 = area(768, "p (a n) -> p a n", a=3)
                RX = area(1536, "p (t h d) -> p t h d", t=4, h=6)
                t_qk, t_vv = [], []
                for br, (cq, ck) in enumerate(((0, 1), (3, 4))):
                    raw = R[br]
                    w, t_w, i = wsplit(f"in_{l}", cq)
                    tr_ = []
                    for a in range(2):
                        b, t = fm(w, t_w, a * 128, NT)
                        tr_.append(evac(raw[:, a, 0:NT], b.ap[:, 0:NT], t))
                        b.release(tr_[-1])
                    done(i, t)
                    w, t_w, i = wsplit(f"in_{l}", ck)
                    b, t = fm(w, t_w, 0, 512)
                    tr_.append(evac(raw[:, 2, :], b.ap, t))
                    b.release(tr_[-1])
                    b = bank()
                    t = rows3(b, w, t_w, t_H, range(4), slice(128, 256), 128)
                    done(i, t)
                    t = evac(V[br], b.ap.rearrange("p (t c) -> p t c", t=4), t)
                    b.release(t)
                    t_vv.append(t)
                    t_rx = PE.last()
                    sq = [act(S3[:, 0:2, 0:NT], raw[:, 0:2, 0:NT], ACT.Square, tr_, t_rx),
                          act(S3[:, 2, :], raw[:, 2, :], ACT.Square)]
                    b = bank()
                    for n in range(4):
                        for a in range(3):
                            if a < 2 and n >= nt:
                                continue
                            c = n * 6 + 2 * a
                            t = mm(b.ap[:, c:c + 2], S3[:, a, n * 128:(n + 1) * 128], C("bones2"), True, True, b.w, sq,
                                   sig=True)
                    ms = small(24)
                    ms3 = ms.rearrange("p (t h) -> p t h", h=6)
                    b3 = b.ap[:, 0:24].rearrange("p (t h) -> p t h", h=6)
                    if nt == 4:
                        t = ts(VE, ms, b.ap[:, 0:24], 1.0, EPS, ALU.mult, ALU.add, t)
                    else:
                        ts(VE, ms3[:, 0:2, :], b3[:, 0:2, :], 1.0, EPS, ALU.mult, ALU.add, t)
                        VE.do(lambda e: e.memset(ms3[:, 2:4, 0:4], 1.0))
                        t = ts(VE, ms3[:, 2:4, 4:6], b3[:, 2:4, 4:6], 1.0, EPS, ALU.mult, ALU.add)
                    b.release(t)
                    r_, t = power(24, ms, t)
                    t = copy(VE, RX, r_.rearrange("p (t h d) -> p t h d", t=4, d=1).to_broadcast([128, 4, 6, 64]), t,
                             t_rx)
                    tn = []
                    for a in range(3):
                        n_ = nt if a < 2 else 4
                        b = bank()
                        for n in range(n_):
                            t2 = mm(b.ap[:, n * 128:(n + 1) * 128], RX[:, n, 2 * a:2 * a + 2, :], ident, True, True,
                                    b.w, t, sig=True)
                        t3 = stt(raw[:, a, 0:n_ * 128], raw[:, a, 0:n_ * 128],
                                 P("qkn", l * 4 + br * 2 + (0 if a < 2 else 1)), b.ap[:, 0:n_ * 128], ALU.mult,
                                 ALU.mult, t2)
                        b.release(t3)
                        tn.append(t3)
                    t_qk.append(rope(raw[:, :, 0:256], T3, 3, C("p16"), C("acos"), C("asin"), tn))
                top[0] = mid
                S = [area(1024) for _ in range(3)]
                T = [area(1024) for _ in range(2)]
                t_old = [PE.last(), VE.last(), GP.last()]

                def head(br, it, p):
                    raw, vv = R[br], V[br]
                    k0 = 0 if it < 2 else 256
                    J = 512 - k0
                    r = slice(p * 64, p * 64 + 64)

                    def scores():
                        pr = pair()
                        for h in range(2):
                            t = mm(pr.ap[:, h * 512:h * 512 + J], raw[r, h, it * 128:it * 128 + 128],
                                   raw[r, 2, k0:512], True, True, pr.w, t_qk[br], sig=(h == 1))
                        return pr, t

                    def values(T, t_T):
                        b = bank()
                        nj = J // 128
                        for jt in range(nj):
                            t = mm(b.ap[r, 0:256], vv[:, k0 // 128 + jt, p * 64:p * 64 + 64],
                                   T[:, jt * 256:(jt + 1) * 256], jt == 0, jt == nj - 1, b.w, t_T, t_vv[br],
                                   sig=(jt == nj - 1))
                        zz = Z[r, br, :, it * 128:it * 128 + 128]
                        b.release(tt(VE, zz, b.ap[r, 0:256].rearrange("p (h n) -> p h n", h=2), zz, ALU.mult, t, t_z))
                        return t

                    return (scores, values, 2, J, C("wmask", it * 512, 512) if br == 1 and it < 2 else None,
                            P("sink", l * 4 + 2 * p, 2) if br == 1 else None, None, None)

                attend([head(br, it, p) for br in range(2) for it in range(nt) for p in range(2)],
                       S, T, t_old, t_old)
                barrier()
                top[0] = tail
                M = area(8 * NT, "p (a n) -> p a n", a=8)
                SG = [area(NT) for _ in range(2)]
                T2 = [area(NT) for _ in range(2)]
                t_sg, t_t2 = [[], []], [[], []]
                n_ = 0
                for c in range(4):
                    wb, t_wb, ib = load(A[f"br_{l}"][c], "p (r k c) -> p r k c", r=4, k=2)
                    for r in range(4):
                        w, t_w, i = wsplit(f"merge_{l}", r * 4 + c)
                        for j in range(2):
                            m = 2 * c + j
                            b, t = fm(w, t_w, j * 128, NT)
                            s = SG[n_ % 2]
                            t = act(s, b.ap[:, 0:NT], ACT.Sigmoid, t, t_sg[n_ % 2],
                                    bias=P("b_merge", l * 32 + r * 8 + m))
                            b.release(t)
                            b = bank()
                            for k in range(2):
                                t_y = mm(b.ap[:, 0:NT], wb[:, r, k, j * 128:(j + 1) * 128], Z[:, r, k, :], k == 0,
                                         k == 1, b.w, t_wb, sig=(k == 1))
                            if r == 0:
                                t_m = tt(VE, M[:, m, :], b.ap[:, 0:NT], s, ALU.mult, t, t_y)
                                b.release(t_m)
                                t_sg[n_ % 2] = [t_m]
                            else:
                                u = T2[n_ % 2]
                                t = tt(VE, u, b.ap[:, 0:NT], s, ALU.mult, t, t_y, t_t2[n_ % 2])
                                b.release(t)
                                t_sg[n_ % 2] = [t]
                                t_m = tt(GP, M[:, m, :], M[:, m, :], u, ALU.add, t)
                                t_t2[n_ % 2] = [t_m]
                            n_ += 1
                        done(i, t_y)
                    done(ib, t_y)
                t_x = []
                for c in range(4):
                    w, t_w, i = wchunk(f"out_{l}", c)
                    for j in range(2):
                        m = 2 * c + j
                        b = bank()
                        for k in range(8):
                            t = mm(b.ap[:, 0:NT], w[:, k, j * 128:(j + 1) * 128], M[:, k, :], k == 0, k == 7, b.w, t_w,
                                   t_m, sig=(k == 7))
                        for v in range(NT // 256):
                            cs = slice(v * 256, v * 256 + 256)
                            t2 = stt(X[:, m, cs], b.ap[:, cs], m3[:, 16 + m, v:v + 1], X[:, m, cs], ALU.mult, ALU.add, t)
                        b.release(t2)
                    done(i, t)
                return t2

            t = hybrid()
            t = ffn(0, t)
            t = nsa(t)
            t = ffn(1, t)
            barrier()
            t_f = plain_norm(X[:, :, 0:256], area(2048, "p (a n) -> p a n", a=8), lambda k: P("final_norm", k), t)
            t_m = modulation()
            VE.wait(t_ctx)
            AC.wait(t_ctx)
            GP.wait(t_ctx)
            t = layer(0, [t_f] + t_m)
            t = layer(1, [t])
            SP.wait(t)
            SP.plain(lambda e: e.dma_start(out.rearrange("p (k n) -> p k n", k=8), X[:, :, 0:256]).then_inc(s_out, 16))
            SP.wait((s_out, 16))
            return queues, asked

        _, order = emit(None)
        (SP, PE, VE, AC, GP), _ = emit(order)

        with nc.Block() as block:
            @block.sync
            def _(e):
                SP.run(e)

            @block.tensor
            def _(e):
                PE.run(e)

            @block.vector
            def _(e):
                VE.run(e)

            @block.scalar
            def _(e):
                AC.run(e)

            @block.gpsimd
            def _(e):
                GP.run(e)


def constants():
    CL, CN = _consts_layout()
    c = np.zeros((128, CN), np.float32)

    def put(name, v):
        a, n = CL[name]
        c[:, a:a + n] = np.asarray(v, np.float64).reshape(128, n)

    eye = np.eye(128)
    half = np.kron(np.eye(2), np.ones((64, 64)))
    put("ident", eye)
    put("ones", np.ones((128, 2)))
    put("bones2", np.kron(np.eye(2), np.ones((64, 1))) / 64)
    put("bones", half / 64)
    put("mhalf", np.full((128, 64), -0.5))
    put("onerow", np.ones((128, 64)))
    pos = np.arange(256, dtype=np.float32)
    d = np.arange(128) % 64

    def swap(partner):
        m = np.zeros((128, 128))
        for i in range(128):
            if partner[i] >= 0:
                m[partner[i], i] = 1
        return m

    def angles(p, rot, theta, idx):
        inv = np.float32(theta) ** (-np.arange(0, rot, 2, dtype=np.float32) / np.float32(rot))
        return (p[None, :].astype(np.float32) * inv.astype(np.float32)[idx][:, None]).astype(np.float32)

    base = (np.arange(128) // 64) * 64
    put("p32", swap(base + (d + 32) % 64))
    a = angles(pos, 64, 10000.0, d % 32).astype(np.float64)
    put("rcos", np.cos(a))
    put("rsin", np.sin(a) * np.where(d < 32, -1.0, 1.0)[:, None])
    put("p8", swap(np.where(d < 16, base + (d + 8) % 16, -1)))
    for name, p in (("n", pos), ("e", np.arange(15, dtype=np.float32) * 16 + 31)):
        a = angles(p, 16, 500000.0, d % 8).astype(np.float64)
        on = (d < 16)[:, None]
        put(name + "cos", np.where(on, np.cos(a), 1.0))
        put(name + "sin", np.where(on, np.sin(a) * np.where(d < 8, -1.0, 1.0)[:, None], 0.0))
    put("p16", swap(base + (d // 32) * 32 + (d % 32 + 16) % 32))
    inv = np.float32(10000.0) ** (-np.arange(16, dtype=np.float32) / np.float32(16))
    t = np.arange(256)
    where = np.where((d < 32)[:, None], (t // 64)[None, :], (t % 64)[None, :]).astype(np.float32)
    a = (where * inv.astype(np.float32)[d % 16][:, None]).astype(np.float32).astype(np.float64)
    put("acos", np.cos(a))
    put("asin", np.sin(a) * np.where(d % 32 < 16, -1.0, 1.0)[:, None])
    i = np.arange(128)
    NEG = -1e30
    causal = np.where(i[None, :] <= i[:, None], 0.0, NEG)
    put("cmask", np.concatenate([np.zeros((128, 128)), causal], 1))
    end = np.arange(15) * 16 + 31
    vis = end[None, None, :] <= (np.arange(2)[:, None, None] * 128 + i[None, :, None])
    put("emask", np.where(vis, 0.0, NEG).transpose(1, 0, 2))
    put("evis", vis.any(-1).T.astype(float))
    w = np.zeros((128, 2, 512))
    w[:, 0, 128:256] = causal
    w[:, 1, 0:128] = np.where(i[None, :] >= i[:, None], 0.0, NEG)
    put("wmask", w)
    k = np.arange(64)
    f = 2 * np.pi * ((k[:, None] * k[None, :]) % 64) / 64
    put("cs", np.concatenate([np.kron(np.eye(2), np.cos(f)), np.kron(np.eye(2), np.sin(f))], 1))
    n = np.arange(256)
    f = 2 * np.pi * ((n[:, None] * n[None, :]) % 256) / 256
    put("cn", (np.cos(f) / 128).reshape(2, 128, 256).transpose(1, 0, 2))
    put("sn", (-np.sin(f) / 128).reshape(2, 128, 256).transpose(1, 0, 2))
    g = np.log1p(-(2.0 ** (-5.0 - np.arange(8))))
    diff = np.arange(256)[None, :] - i[:, None]
    dec = np.where(diff[None] >= 0, np.exp(np.maximum(diff, 0)[None] * g[:, None, None]), 0.0) * 0.125
    put("decay", dec.transpose(1, 0, 2))
    return c


def kernel(**inputs):
    import concourse.bacc as _bacc
    from concourse.bass_utils import run_bass_kernel_spmd as _run

    I = {k: np.asarray(v) for k, v in inputs.items()}

    def cols(w, c=256):
        K, N = w.shape
        return np.ascontiguousarray(w.reshape(K // 128, 128, N // c, c).transpose(2, 1, 0, 3)).reshape(
            N // c, 128, K // 128 * c)

    def tiles(v):
        return v.reshape(-1, 128).T

    def tokens(x):
        return np.ascontiguousarray(x.T.reshape(8, 128, 256).transpose(1, 0, 2)).reshape(128, 2048)

    def diag(w):
        n = w.shape[0]
        o = np.zeros((128, n // 2, 128), np.float32)
        for b in range(n):
            h = b % 2
            o[h * 64:h * 64 + 64, b // 2, h * 64:h * 64 + 64] = w[b]
        return o

    arr = {"xT": tokens(I["x"][0]), "ctxT": tokens(I["ctx_2"][0]), "consts": constants()}
    PL, PN = _params_layout()
    par = np.zeros((128, PN), np.float32)

    def put(name, v):
        a, n = PL[name]
        par[:, a:a + n] = v

    put("attn_norm", tiles(I["attn_norm"]))
    put("ffn_norm", tiles(I["ffn_norm"]))
    put("final_norm", tiles(I["final_norm"]))
    put("conv_w", I["conv_w"][0].reshape(4, 4, 128).transpose(2, 1, 0).reshape(128, 16))
    put("conv_b", tiles(I["conv_b"]))
    put("ga_b", tiles(I["gate_a_b"]))
    put("gx_b", tiles(I["gate_x_b"]))
    put("lam", tiles(I["lru_lambda"]))
    put("b_ada", tiles(I["b_ada_2"]))
    put("norm_w2", tiles(I["norm_w_2"]))
    put("b_merge", tiles(I["b_merge_2"]))
    qkn = np.stack([I[n] for n in ("qn_a_2", "kn_a_2", "qn_d_2", "kn_d_2")], 1)
    put("qkn", np.tile(qkn.reshape(8, 64).T, (2, 1)))
    put("cvec", np.stack([I["c_2"][0].reshape(8, 128), I["c_ctx_2"].reshape(8, 128)], 2).transpose(1, 0, 2)
        .reshape(128, 16))
    put("sink", np.broadcast_to(I["sink_d_2"].reshape(1, 8), (128, 8)))
    arr["params"] = par
    arr["ab_in"] = cols(I["ab_w_in"][0])
    arr["ab_out"] = cols(I["ab_w_out"][0])
    arr["lru_gates"] = np.stack([diag(I["gate_a_w"][0]), diag(I["gate_x_w"][0])], 1).reshape(128, 1024)
    for l in range(2):
        arr[f"w1_{l}"] = cols(I["ffn_w1"][l])
        arr[f"w3_{l}"] = cols(I["ffn_w3"][l])
        arr[f"w2_{l}"] = cols(I["ffn_w2"][l], 128)
    w = I["nsa_w_in"][0]
    heads = [(2 * t2 + p) * 4 + r for t2 in range(2) for r in range(4) for p in range(2)]
    qcols = np.concatenate([np.arange(h * 64, h * 64 + 64) for h in heads])
    arr["nsa_in"] = cols(np.concatenate([w[:, qcols], w[:, 1024:2560]], 1))
    g = np.zeros((1, 128, 8, 256), np.float32)
    g[0, :, :, 0:48] = w[:, 2560:].reshape(8, 128, 48).transpose(1, 0, 2)
    arr["nsa_gates"] = g.reshape(1, 128, 2048)
    arr["nsa_out"] = cols(I["nsa_w_out"][0][qcols])
    arr["pe"] = np.ascontiguousarray(np.concatenate([I["cmp_pe_k"][0].T, I["cmp_pe_v"][0].T], 1))
    for n in "kv":
        arr[f"cmp_{n}1"] = np.ascontiguousarray(I[f"cmp_{n}_w1"][0].reshape(32, 64, 64).transpose(1, 0, 2)).reshape(
            64, 2048)
    arr["cmp_w2"] = np.concatenate([I["cmp_k_w2"][0], I["cmp_v_w2"][0]], 1)
    hd = np.concatenate([np.arange(h * 64, h * 64 + 64) for h in (0, 2, 1, 3)])
    for l in range(2):
        w = I["w_in_2"][l]
        order = np.arange(2816)
        for c in (0, 2, 3, 5):
            order[c * 256:(c + 1) * 256] = c * 256 + hd
        arr[f"in_{l}"] = cols(w[:, order])
        arr[f"ada_{l}"] = cols(I["w_ada_2"][l])
        arr[f"merge_{l}"] = cols(I["w_merge_2"][l])
        arr[f"out_{l}"] = cols(I["w_out_2"][l])
        br = I["w_br_2"][l].copy()
        br[0], br[1] = br[0][hd], br[1][hd]
        arr[f"br_{l}"] = np.ascontiguousarray(br.reshape(4, 2, 128, 4, 256).transpose(3, 2, 0, 1, 4)).reshape(
            4, 128, 2048)
        arr[f"fnet_{l}"] = diag(I["w_fnet_2"][l]).reshape(128, 256)
        arr[f"sp_{l}"] = np.ascontiguousarray(I["w_sp_2"][l].transpose(2, 0, 1)).reshape(128, 512)
        arr[f"bsp_{l}"] = np.ascontiguousarray(I["b_sp_2"][l].reshape(1, 512))
    nc = _bacc.Bacc("TRN2", target_bir_lowering=False, num_devices=1)
    arr = {k: np.ascontiguousarray(v) for k, v in arr.items()}
    A = {k: nc.dram_tensor(k, v.shape, mybir.dt.from_np(v.dtype), kind="ExternalInput").ap() for k, v in arr.items()}
    out = nc.dram_tensor("out", (128, 2048), F32, kind="ExternalOutput").ap()
    build(nc, A, out)
    r = _run(nc, [arr], core_ids=[0])
    y = np.asarray(r.results[0]["out"])
    return np.ascontiguousarray(y.reshape(128, 8, 256).transpose(2, 1, 0)).reshape(1, 256, 1024)
```

```python
import math
import numpy as np
import concourse.bass as bass
from concourse import mybir
from contextlib import ExitStack

F32 = mybir.dt.float32
F32R = mybir.dt.float32r
ALU = mybir.AluOpType
ACT = mybir.ActivationFunctionType
AX = mybir.AxisListType
EPS = 1e-6
NSLOT = 3
SLOT = 2048
NSTAGE = 4
ARENA = 14510


class Queue:

    def __init__(self, sem):
        self.sem, self.n, self.items, self.seen = sem, 0, [], {}

    def last(self):
        return (self.sem, self.n)

    def wait(self, *tokens):
        for t in tokens:
            if isinstance(t, list):
                self.wait(*t)
                continue
            sem, value = t
            if value > self.seen.get(id(sem), 0):
                self.seen[id(sem)] = value
                self.items.append(lambda e, s=sem, v=value: e.wait_ge(s, v))

    def do(self, fn, *tokens, chain=True):
        self.wait(*tokens)
        if chain:
            self.wait(self.last())
        self.n += 1
        self.items.append(lambda e, f=fn, s=self.sem: f(e).then_inc(s, 1))
        return self.last()

    def plain(self, fn):
        self.items.append(fn)

    def run(self, e):
        for f in self.items:
            f(e)


class Bank:
    clock = None

    def __init__(self, ap, banks, free):
        self.ap, self.banks, self.free = ap, banks, free
        self.w = [t for b in banks for t in free[b]]
        for b in banks:
            free[b] = None
        self.age = Bank.clock

    def release(self, *tokens):
        self.age[0] += 1
        for b in self.banks:
            self.free[b] = list(tokens)
            self.age[1 + b] = self.age[0]


def _params_layout():
    cols, at = {}, 0
    for name, n in [("attn_norm", 16), ("ffn_norm", 16), ("final_norm", 8), ("conv_w", 16), ("conv_b", 4),
                    ("ga_b", 4), ("gx_b", 4), ("lam", 4), ("b_ada", 48), ("norm_w2", 16), ("b_merge", 64),
                    ("qkn", 8), ("cvec", 16), ("sink", 8)]:
        cols[name] = (at, n)
        at += n
    return cols, at


def _consts_layout():
    cols, at = {}, 0
    for name, n in [("ident", 128), ("onerow", 64), ("psum1", 1), ("sel", 2), ("mhalf", 24), ("bones2", 2), ("bones", 128), ("p32", 128), ("p8", 128),
                    ("p16", 128), ("rcos", 256), ("rsin", 256), ("ncos", 256), ("nsin", 256), ("ecos", 15),
                    ("esin", 15), ("acos", 256), ("asin", 256), ("cmask", 256), ("emask", 30), ("evis", 2),
                    ("wmask", 1024), ("cs", 256), ("cn", 512), ("sn", 512), 
                    ("decay", 2048)]:
        cols[name] = (at, n)
        at += n
    return cols, at


def build(nc, A, out):
    ctx = ExitStack()
    with ctx:
        def sb(name, cols, dt=F32):
            return ctx.enter_context(nc.sbuf_tensor(name, [128, cols], dt))

        def sem(name):
            return ctx.enter_context(nc.semaphore(name))

        PL, PN = _params_layout()
        CL, CN = _consts_layout()
        ring = sb("ring", NSLOT * SLOT)
        par = sb("par", PN)
        con = sb("con", CN)
        X = sb("X", 4096)[:, :].rearrange("p (k n) -> p k n", k=8)
        XH = sb("XH", 4096, F32R)[:, :].rearrange("p (k n) -> p k n", k=8)
        XL = sb("XL", 4096, F32R)[:, :].rearrange("p (k n) -> p k n", k=8)
        WH = [sb(f"WH{i}", 2048, F32R)[:, :] for i in range(2)]
        WL = [sb(f"WL{i}", 2048, F32R)[:, :] for i in range(2)]
        stage = sb("stage", NSTAGE * 1024)
        MOD = sb("MOD", 100)
        SM = sb("SM", 640)
        arena = sb("arena", ARENA)
        psum = ctx.enter_context(nc.psum_tensor("psum", [128, 4096], F32))

        s_eng = [sem(n) for n in ("s_sp", "s_pe", "s_ve", "s_ac", "s_gp")]
        s_const = [sem(f"s_const{i}") for i in range(8)]
        s_slot = [sem(f"s_slot{i}") for i in range(NSLOT)]
        s_stage = [sem(f"s_stage{i}") for i in range(NSTAGE)]
        s_out = sem("s_out")

        def emit(order):
            SP, PE, VE, AC, GP = queues = [Queue(m) for m in s_eng]
            def P(name, i=0, n=1):
                a = PL[name][0] + i
                return par[:, a:a + n]

            def C(name, i=0, n=None):
                a, m = CL[name]
                return con[:, a + i:a + (m if n is None else i + n)]

            top = [0]

            def area(cols, shape=None, **dims):
                a = top[0]
                top[0] += cols
                assert top[0] <= ARENA, top[0]
                v = arena[:, a:a + cols]
                return v.rearrange(shape, **dims) if shape else v

            small_at = [0]

            def small(n):
                if small_at[0] + n > 640:
                    small_at[0] = 0
                a = small_at[0]
                small_at[0] += n
                return SM[:, a:a + n]

            bank_free = [[] for _ in range(8)]
            Bank.clock = [0] * 9

            def bank():
                b = min((b for b in range(8) if bank_free[b] is not None), key=lambda b: Bank.clock[1 + b])
                return Bank(psum[:, b * 512:(b + 1) * 512], [b], bank_free)

            def pair():
                b = min((b for b in range(0, 8, 2) if bank_free[b] is not None and bank_free[b + 1] is not None),
                        key=lambda b: max(Bank.clock[1 + b:3 + b]))
                return Bank(psum[:, b * 512:(b + 2) * 512], [b, b + 1], bank_free)

            slot_use = [[] for _ in range(NSLOT)]
            slot_n = [0] * NSLOT
            next_slot = [0]

            def load(src, shape, parts=None, **dims):
                i = next_slot[0] % NSLOT
                next_slot[0] += 1
                cols = src.shape[-1]
                SP.wait(slot_use[i])
                slot_use[i] = None
                view = ring[:, i * SLOT:i * SLOT + cols]
                for lo, hi in parts or [(0, 128)]:
                    slot_n[i] += 16
                    SP.plain(lambda e, d=ring[lo:hi, i * SLOT:i * SLOT + cols], s=src, m=s_slot[i]:
                             e.dma_start(d, s).then_inc(m, 16))
                return view.rearrange(shape, **dims), (s_slot[i], slot_n[i]), i

            def done(i, token):
                if isinstance(i, str):
                    w_use[int(i)] = [token]
                else:
                    slot_use[i] = [token]

            asked = []
            ready = {}
            w_use = [[], []]
            stage_use = [[] for _ in range(NSTAGE)]
            stage_n = [0] * NSTAGE
            next_stage = [0]

            def split(n, name, c):
                i = n % 2
                use, w_use[i] = w_use[i], None
                if isinstance(c, tuple):
                    src, cuts, width = A[name][c[0]][:, 0:2048], (0, 8, 16), 128
                else:
                    src, cuts, width = A[name][c], (0, 4, 8), 256
                views = [v[:, 0:cuts[2] * width].rearrange("p (k c) -> p k c", k=cuts[2]) for v in (WH[i], WL[i])]
                toks = []
                for h in range(2):
                    lo_, hi_ = cuts[h] * width, cuts[h + 1] * width
                    j = next_stage[0] % NSTAGE
                    next_stage[0] += 1
                    stage_n[j] += 16
                    raw = stage[:, j * 1024:j * 1024 + hi_ - lo_]
                    SP.wait(stage_use[j])
                    SP.plain(lambda e, d=raw, s=src[:, lo_:hi_], m=s_stage[j]: e.dma_start(d, s).then_inc(m, 16))
                    hi, lo = WH[i][:, lo_:hi_], WL[i][:, lo_:hi_]
                    t = copy(AC, hi, raw, (s_stage[j], stage_n[j]), use)
                    t2 = tt(VE, lo, raw, hi.bitcast(F32), ALU.subtract, t, use)
                    stage_use[j] = [t2]
                    toks += [[t, t2]] * (cuts[h + 1] - cuts[h])
                return views, toks

            def wsplit(name, c):
                n = len(asked)
                asked.append((name, c))
                if order is None:
                    ready[n] = split(n, name, c)
                else:
                    while len(ready) < min(n + 2, len(order)):
                        ready[len(ready)] = split(len(ready), *order[len(ready)])
                return ready[n][0], ready[n][1], str(n % 2)

            def product(dst, weights, cols, toks, k, tile, t_x, start, stop, turned, *w, sig=False):
                (wh, wl), (xh, xl) = weights, (XH, XL)
                a = [(wh, xh), (wh, xl), (wl, xh)] if not turned else [(wh, xh), (wl, xh), (wh, xl)]
                for n, (u, v) in enumerate(a):
                    u, v = u[:, k, cols], v[:, k, tile]
                    if turned:
                        u, v = v, u
                    t = mm(dst, u, v, start and n == 0, stop and n == 2, *w, toks[k], t_x,
                           sig=(sig and n == 2))
                return t

            def barrier():
                tokens = [q.last() for q in (PE, VE, AC, GP)]
                for q in (PE, VE, AC, GP):
                    q.wait(tokens)
                top[0] = 0

            def mm(dst, lhsT, rhs, start, stop, *w, sig=False):
                PE.wait(*w)
                f = lambda e: e.matmul(dst, lhsT, rhs, start=start, stop=stop)
                if sig:
                    return PE.do(f, chain=False)
                PE.plain(f)

            def tr(dst, src, ident, *w, sig=False):
                PE.wait(*w)
                f = lambda e: e.transpose(dst, src, ident)
                if sig:
                    return PE.do(f, chain=False)
                PE.plain(f)

            def tt(q, dst, a, b, op, *w):
                return q.do(lambda e: e.tensor_tensor(dst, a, b, op), *w)

            def stt(dst, a, s, b, op0, op1, *w):
                return VE.do(lambda e: e.scalar_tensor_tensor(out=dst, in0=a, scalar=s, in1=b, op0=op0, op1=op1), *w)

            def ts(q, dst, a, s1, s2, op0, op1, *w):
                if s2 is None:
                    return q.do(lambda e: e.tensor_scalar(dst, a, s1, None, op0), *w)
                return q.do(lambda e: e.tensor_scalar(dst, a, s1, s2, op0, op1), *w)

            def act(dst, src, fn, *w, bias=0.0, scale=1.0, accum=None):
                if accum is None:
                    return AC.do(lambda e: e.activation(dst, src, fn, bias=bias, scale=scale), *w)
                return AC.do(lambda e: e.activation(dst, src, fn, bias=bias, scale=scale, accum_out=accum), *w)

            def copy(q, dst, src, *w):
                if q is AC:
                    return AC.do(lambda e: e.activation(dst, src, ACT.Copy), *w)
                return q.do(lambda e: e.tensor_copy(dst, src), *w)

            turn = [0]

            def evac(dst, src, *w):
                turn[0] ^= 1
                return copy(AC if turn[0] else VE, dst, src, *w)

            const_n = [0] * 8

            def cload(i, dst, src):
                const_n[i] += 16
                AC.plain(lambda e: e.dma_start(dst, src).then_inc(s_const[i], 16))
                return (s_const[i], const_n[i])

            x_in = A["xT"].rearrange("p (k n) -> p k n", k=8)
            c_in = A["ctxT"].rearrange("p (k n) -> p k n", k=8)
            t_x = cload(0, X[:, :, 0:256], x_in)
            t_par = cload(1, par[:, :], A["params"])
            cut = CL["decay"][0]
            first = CL["bones2"][0] + 2
            t_con0 = cload(2, con[:, 0:first], A["consts"][:, 0:first])
            for q in (PE, VE, AC, GP):
                q.wait(t_con0, t_par)
            ident = C("ident")

            def power(n, src, *w):
                r = small(n)
                return r, tt(GP, r, src, C("mhalf", 0, n), ALU.pow, *w)

            def run(work):
                while True:
                    try:
                        next(work)
                    except StopIteration as end:
                        return end.value

            def squares(sq, src, t_src):
                toks = []
                for j, q in enumerate((AC, VE, GP, AC)):
                    d, s = sq[:, 2 * j:2 * j + 2, :], src[:, 2 * j:2 * j + 2, :]
                    if q is AC:
                        toks += [act(d, s, ACT.Square, t_src)] * 2
                    else:
                        toks += [tt(q, d, s, s, ALU.mult, t_src)] * 2
                return toks

            def inv_rms(sq, t_sq):
                b = bank()
                for k in range(8):
                    g = slice(32 * (k % 4), 32 * (k % 4) + 32)
                    t = mm(b.ap[g, 0:256], C("onerow", 0, 32), sq[:, k, :], k < 4, k >= 4, b.w, t_sq[k], sig=(k == 7))
                part = small(256)
                t = copy(VE, part, b.ap[:, 0:256], t)
                b.release(t)
                yield
                b = bank()
                for n in range(2):
                    t = mm(b.ap[:, n:n + 1], part[:, n * 128:(n + 1) * 128], C("psum1"), True, True, b.w, t,
                           sig=True)
                ms = small(2)
                t = ts(VE, ms, b.ap[:, 0:2], EPS, None, ALU.add, None, t)
                b.release(t)
                r, t = power(2, ms, t)
                wide = small(256).rearrange("p (a n) -> p a n", a=2)
                t = copy(VE, wide, r.rearrange("p (a n) -> p a n", n=1).to_broadcast([128, 2, 128]), t)
                yield
                b = bank()
                for n in range(2):
                    t2 = mm(b.ap[:, n * 128:(n + 1) * 128], wide[:, n, :], ident, True, True, b.w, t, sig=(n == 1))
                return b, t2

            def norm(src, sq, gain, t_sq, out, shift=None, cs=slice(0, 256)):
                b, t = yield from inv_rms(sq, t_sq)
                for k in range(8):
                    f = sq[:, k, :]
                    t1 = stt(f, src[:, k, :], gain(k), b.ap[:, 0:256], ALU.mult, ALU.mult, t)
                    if shift is not None:
                        t1 = ts(VE, f, f, shift(k), None, ALU.add, None)
                    t2 = copy(AC, XH[:, k, cs], f, t1)
                    t3 = tt(GP, XL[:, k, cs], f, XH[:, k, cs].bitcast(F32), ALU.subtract, t2)
                    out.append([t2, t3])
                    if k == 7:
                        b.release(t1)
                    yield

            def plain_norm(src, sq, gain, t_sq, sq2, out):
                b, t = yield from inv_rms(sq, t_sq)
                for k in range(8):
                    t1 = stt(src[:, k, :], src[:, k, :], gain(k), b.ap[:, 0:256], ALU.mult, ALU.mult, t)
                    out.append(act(sq2[:, k, :], src[:, k, :], ACT.Square, t1))
                    if k == 7:
                        b.release(t1)
                    yield

            def feats(dst_cols, chunk, t_w, rhs, t_rhs, b, nk=8, m0=0, n=256):
                for j, c in enumerate(dst_cols):
                    for k in range(nk):
                        t = mm(b.ap[:, j * n:(j + 1) * n], chunk[:, k, c:c + 128], rhs(k), k == 0, k == nk - 1,
                               b.w, t_w, t_rhs[k] if isinstance(t_rhs, list) and len(t_rhs) == nk else t_rhs,
                               sig=(k == nk - 1))
                return t

            def feats3(dst_cols, weights, toks, t_x, b, n=256):
                for j, c in enumerate(dst_cols):
                    for k in range(8):
                        t = product(b.ap[:, j * n:(j + 1) * n], weights, slice(c, c + 128), toks, k, slice(0, n),
                                    t_x[k], k == 0, k == 7, False, b.w, sig=(k == 7))
                return t

            def rows3(b, weights, toks, t_x, tiles, cols, width):
                for j, n in enumerate(tiles):
                    for k in range(8):
                        t = product(b.ap[:, j * width:(j + 1) * width], weights, cols, toks, k,
                                    slice(n * 128, n * 128 + 128), t_x[k], k == 0, k == 7, True, b.w, sig=(k == 7))
                return t

            def wchunk(name, i):
                return load(A[name][i], "p (k c) -> p k c", k=8)

            def parts(k, cs, x, *w, low=None):
                t = copy(AC, XH[:, k, cs], x, *w)
                q = low or (GP, VE)[k % 2]
                return [t, tt(q, XL[:, k, cs], x, XH[:, k, cs].bitcast(F32), ALU.subtract, t, *w)]

            def residual(name, src, t_src):
                t_x, t_sq = [], []
                t_old = PE.last()
                for k in range(8):
                    t_x.append(parts(k, slice(0, 256), src[:, k, :], t_src[k], t_old))
                for c in range(4):
                    w, t_w, i = wsplit(name, c)
                    b = bank()
                    t = feats3([0, 128], w, t_w, t_x, b)
                    done(i, t)
                    v = b.ap.rearrange("p (a n) -> p a n", a=2)
                    t = tt(VE, X[:, 2 * c:2 * c + 2, 0:256], v, X[:, 2 * c:2 * c + 2, 0:256], ALU.add, t)
                    b.release(t)
                    t_sq += [act(SQ0[:, 2 * c:2 * c + 2, :], X[:, 2 * c:2 * c + 2, 0:256], ACT.Square, t, t_x)] * 2
                return t_sq

            def rope(raw, tmp, nt, perm, cos, sin, t_raw, n=256):
                toks = []
                per = 512 // n
                for j in range(0, nt, per):
                    m = min(per, nt - j)
                    b = bank()
                    bv = b.ap[:, 0:m * n].rearrange("p (a n) -> p a n", a=m)
                    t = mm(bv, perm, raw[:, j:j + m, :], True, True, b.w, t_raw, sig=True)
                    s3 = sin.rearrange("p (a n) -> p a n", a=1).to_broadcast([128, m, n])
                    c3 = cos.rearrange("p (a n) -> p a n", a=1).to_broadcast([128, m, n])
                    t1 = tt(VE, tmp[:, j:j + m, :], bv, s3, ALU.mult, t)
                    b.release(t1)
                    t2 = tt(GP, raw[:, j:j + m, :], raw[:, j:j + m, :], c3, ALU.mult, t)
                    toks.append(tt(GP, raw[:, j:j + m, :], raw[:, j:j + m, :], tmp[:, j:j + m, :], ALU.add, t1, t2))
                return toks[-1]

            def halves(low, high, *w):
                GP.do(lambda e: e.tensor_copy(high[64:128], low[64:128]), *w)
                GP.do(lambda e: e.memset(high[0:64], 0.0))
                return GP.do(lambda e: e.memset(low[64:128], 0.0))

            SQ0, SQ1 = [arena[:, n * 2048:(n + 1) * 2048].rearrange("p (a n) -> p a n", a=8) for n in range(2)]

            t_late = []

            def hybrid():
                barrier()
                four = dict(shape="p (a n) -> p a n", a=4)
                xr = area(4 * 260, **four)
                conv = area(1024, **four)
                gr, gi = area(1024, **four), area(1024, **four)
                aa, uu = area(1024, **four), area(1024, **four)
                cat = area(2048, "p (a n) -> p a n", a=8)
                t_xn = []
                run(norm(X[:, :, 0:256], cat, lambda k: P("attn_norm", k), squares(cat, X[:, :, 0:256], t_x), t_xn))
                qq, kk, gg = [area(1024, **four) for _ in range(3)]
                ro, sq = gr, gi
                vv = area(1024, "p (t c) -> p t c", t=2)
                tmp = area(1024, **four)
                kk1 = area(1024, **four)
                sT = [v.rearrange("p a n -> p (a n)")[:, 0:768].rearrange("p (h c) -> p h c", h=2)
                      for v in (aa, uu)]
                rx = xr.rearrange("p a n -> p (a n)")[:, 0:1024].rearrange("p (t h d) -> p t h d", t=2, h=8)
                t_pad = GP.do(lambda e: e.memset(xr[:, :, 0:3], 0.0))
                def project(c, fn):
                    w, t_w, i = wsplit("ab_in", c)
                    b = bank()
                    t = feats3([0, 128], w, t_w, t_xn, b)
                    done(i, t)
                    t = fn(b.ap.rearrange("p (a n) -> p a n", a=2), t)
                    b.release(t)
                    return t

                late = []

                def recurrent_input(j, v, t):
                    if j == 0:
                        late.append(cload(6, con[:, first:cut], A["consts"][:, first:cut]))
                        late.append(cload(3, con[:, cut:CN], A["consts"][:, cut:CN]))
                        t_late.append(cload(4, X[:, :, 256:512], c_in))
                    return evac(xr[:, 2 * j:2 * j + 2, 3:259], v, t)

                toks = [project(2 + j, lambda v, t: recurrent_input(j, v, t)) for j in range(2)]
                t_con, t_dec = late
                gates, t_gates, gslot = load(A["lru_gates"], "p (g t c) -> p g t c", g=2, t=4)
                for t_ in range(4):
                    w = lambda k: P("conv_w", t_ * 4 + k)
                    ts(VE, conv[:, t_, :], xr[:, t_, 0:256], w(0), P("conv_b", t_), ALU.mult, ALU.add, t_pad, toks[t_ // 2])
                    for k in range(1, 4):
                        t_conv = stt(conv[:, t_, :], xr[:, t_, k:k + 256], w(k), conv[:, t_, :], ALU.mult, ALU.add)
                tq = [project(4 + j, lambda v, t: evac(qq[:, 2 * j:2 * j + 2, :], v, t)) for j in range(2)]
                sp = small(4)
                neg, e_, z_, z2 = small(4), small(4), small(4), small(4)
                ts(VE, neg, P("lam", 0, 4), -1.0, None, ALU.mult, None)
                t = tt(VE, e_, neg, P("lam", 0, 4), ALU.min)
                t = act(e_, e_, ACT.Exp, t)
                ts(VE, z_, e_, 2.0, None, ALU.add, None, t)
                VE.do(lambda e: e.reciprocal(z_, z_))
                tt(VE, z_, z_, e_, ALU.mult)
                tt(VE, z2, z_, z_, ALU.mult)
                ts(VE, sp, z2, 16.0 / 15, 16.0 / 13, ALU.mult, ALU.add)
                for n in (11, 9, 7, 5, 3, 1):
                    tt(VE, sp, sp, z2, ALU.mult)
                    ts(VE, sp, sp, 16.0 / n, None, ALU.add, None)
                tt(VE, sp, sp, z_, ALU.mult)
                ts(VE, neg, neg, 0.0, 8.0, ALU.max, ALU.mult)
                t_sp = tt(VE, sp, sp, neg, ALU.add)

                for g, dst, bias in ((0, gr, "ga_b"), (1, gi, "gx_b")):
                    for j in range(2):
                        b = bank()
                        for h in range(2):
                            t = mm(b.ap[:, h * 256:(h + 1) * 256], gates[:, g, 2 * j + h, :], conv[:, 2 * j + h, :],
                                   True, True, b.w, t_gates, t_conv, sig=True)
                        for h in range(2):
                            t2 = act(dst[:, 2 * j + h, :], b.ap[:, h * 256:(h + 1) * 256], ACT.Sigmoid, t,
                                     bias=P(bias, 2 * j + h))
                        b.release(t2)
                t_gi = t2
                done(gslot, t)
                tk = [project(6 + j, lambda v, t: evac(kk[:, 2 * j:2 * j + 2, :], v, t)) for j in range(2)]
                for t_ in range(4):
                    ts(VE, gr[:, t_, :], gr[:, t_, :], sp[:, t_:t_ + 1], None, ALU.mult, None, t_gi, t_sp)
                t_s = VE.last()
                t_a = act(aa, gr, ACT.Exp, t_s, scale=-1.0)
                t_t = act(gr, gr, ACT.Tanh)
                tt(VE, uu, aa, aa, ALU.mult, t_a)
                t = stt(uu, uu, 1.0, gr, ALU.add, ALU.mult, t_t)
                t_g = tt(GP, gi, gi, conv, ALU.mult, t_gi, t_conv)
                t = act(uu, uu, ACT.Sqrt, t)
                tt(VE, uu, uu, gi, ALU.mult, t, t_g)
                for t_ in range(4):
                    t_scan = VE.do(lambda e, a=t_: e.tensor_tensor_scan(conv[:, a, :], aa[:, a, :], uu[:, a, :], 0.0,
                                                                        ALU.mult, ALU.add))
                PE.wait(t_con)
                VE.wait(t_con)
                GP.wait(t_con)
                t_q = rope(qq, tmp, 4, C("p32"), C("rcos"), C("rsin"), tq)
                t_k = rope(kk, tmp, 4, C("p32"), C("rcos"), C("rsin"), tk + [t_q])
                t_k = halves(kk, kk1, t_k)
                tv = []
                for j in range(2):
                    w, t_w, i = wsplit("ab_in", 8 + j)
                    b = bank()
                    t = rows3(b, w, t_w, t_xn, (0, 1), slice(0, 256), 256)
                    done(i, t)
                    tv.append(evac(vv[:, :, j * 256:(j + 1) * 256], b.ap.rearrange("p (t c) -> p t c", t=2), t))
                    b.release(tv[-1])
                def gate(n):
                    if n < 2:
                        tg.append(project(10 + n, lambda v, t: act(gg[:, 2 * n:2 * n + 2, :], v, ACT.Silu, t)))
                    else:
                        j = n - 2
                        ty.append(project(j, lambda v, t: act(cat[:, 2 * j:2 * j + 2, :], v, ACT.Gelu_apprx_tanh, t,
                                                              t_xn[7])))

                tg, ty = [], []
                t_pv = [[], []]
                for t_ in range(4):
                    pr = pair()
                    for p in range(2):
                        c = p * 512
                        kp = (kk, kk1)[p]
                        mm(pr.ap[:, c:c + 256], kp[:, t_, 0:128], qq[:, t_, 0:256], True, True, pr.w, t_q, t_k)
                        t = mm(pr.ap[:, c + 256:c + 384], kp[:, t_, 128:256], qq[:, t_, 128:256], True, True,
                               sig=True)
                    v = pr.ap.rearrange("p (h c) -> p h c", h=2)
                    s = sT[t_ % 2]
                    dec = C("decay").rearrange("p (h c) -> p h c", h=8)[:, 2 * t_:2 * t_ + 2, :]
                    tt(VE, s[:, :, 0:256], v[:, :, 0:256], dec, ALU.mult, t, t_dec, t_pv[t_ % 2])
                    t = tt(VE, s[:, :, 256:384], v[:, :, 256:384], dec[:, :, 0:128], ALU.mult)
                    pr.release(t)
                    if t_ < 3:
                        gate(t_)
                    b = bank()
                    for jt in range(2):
                        for p in range(2):
                            r = slice(p * 64, p * 64 + 64)
                            vc = (2 * t_ + p) * 64
                            t2 = mm(b.ap[r, 128 * jt:256], vv[:, jt, vc:vc + 64],
                                    s[:, p, 256 * jt:256 + 128 * jt], jt == 0, jt == 1, b.w, t, tv,
                                    sig=(jt == 1))
                    t_pv[t_ % 2] = [t2]
                    t_ro = copy(AC, ro[:, t_, :], b.ap[:, 0:256], t2, t_scan, t_g)
                    b.release(t_ro)
                for j in range(2):
                    b = bank()
                    v = b.ap.rearrange("p (a n) -> p a n", a=2)
                    t = mm(v, C("bones"), ro[:, 2 * j:2 * j + 2, :], True, True, b.w, t_ro, sig=True)
                    t = stt(ro[:, 2 * j:2 * j + 2, :], v, -1.0, ro[:, 2 * j:2 * j + 2, :], ALU.mult, ALU.add, t)
                    b.release(t)
                    t_sq = act(sq[:, 2 * j:2 * j + 2, :], ro[:, 2 * j:2 * j + 2, :], ACT.Square, t)
                t_ro = t
                gate(3)
                t_lru = tt(GP, cat[:, 0:4, :], cat[:, 0:4, :], conv, ALU.mult, ty, t_scan)
                b = bank()
                for n in range(2):
                    for a in range(4):
                        c = n * 8 + 2 * a
                        t = mm(b.ap[:, c:c + 2], sq[:, a, n * 128:(n + 1) * 128], C("bones2"), True, True, b.w, t_sq,
                               sig=True)
                ms = small(16)
                t = ts(VE, ms, b.ap[:, 0:16], 1.0, EPS, ALU.mult, ALU.add, t)
                b.release(t)
                r, t = power(16, ms, t)
                t_r2 = [None, None]
                t = copy(VE, rx, r.rearrange("p (t h d) -> p t h d", t=2, d=1).to_broadcast([128, 2, 8, 64]), t)
                for j in range(2):
                    b = bank()
                    v = b.ap.rearrange("p (a n) -> p a n", a=2)
                    for h in range(2):
                        for n in range(2):
                            a = 2 * j + h
                            t2 = mm(v[:, h, n * 128:(n + 1) * 128], rx[:, n, 2 * a:2 * a + 2, :], ident, True, True,
                                    b.w, t, sig=True)
                    t3 = tt(VE, ro[:, 2 * j:2 * j + 2, :], v, ro[:, 2 * j:2 * j + 2, :], ALU.mult, t2, t_ro)
                    b.release(t3)
                    t_r2[j] = tt(VE, cat[:, 4 + 2 * j:6 + 2 * j, :], ro[:, 2 * j:2 * j + 2, :], gg[:, 2 * j:2 * j + 2, :],
                               ALU.mult, tg)
                return residual("ab_out", cat, [t_lru] * 4 + [t_r2[0]] * 2 + [t_r2[1]] * 2)

            def ffn(l, t_h, beside):
                barrier()
                area(2048)
                t_xn, t_sq = [], []
                run(norm(X[:, :, 0:256], SQ0, lambda k: P("ffn_norm", 8 * l + k), t_h, t_xn))
                hh = area(22 * 256, "p (a n) -> p a n", a=22)
                t_old = [PE.last(), GP.last()]
                sg = [area(512) for _ in range(2)]
                t_free = [[], []]
                t_hh = []
                for c in range(11):
                    w, t_w, i = wsplit(f"w1_{l}", c)
                    b1 = bank()
                    t1 = feats3([0, 128], w, t_w, t_xn, b1)
                    done(i, t1)
                    w, t_w, i = wsplit(f"w3_{l}", c)
                    b3 = bank()
                    t3 = feats3([0, 128], w, t_w, t_xn, b3)
                    done(i, t3)
                    s = sg[c % 2]
                    t = act(s, b1.ap, ACT.Silu, t1, t_free[c % 2])
                    b1.release(t)
                    d = hh[:, 2 * c:2 * c + 2, :]
                    t = tt(VE, d, s.rearrange("p (a n) -> p a n", a=2), b3.ap.rearrange("p (a n) -> p a n", a=2),
                           ALU.mult, t, t3)
                    b3.release(t)
                    t_free[c % 2] = [t]
                    t_hh += [parts(2 * c + j, slice(256, 512), hh[:, 2 * c + j, :], t, t_old) if c < 4 else t
                             for j in range(2)]
                beside = beside(area(2048, "p (a n) -> p a n", a=8))
                t_old = PE.last()
                for k in range(8):
                    t_hh[8 + k] = parts(k, slice(0, 256), hh[:, 8 + k, :], t_hh[8 + k], t_old)
                for m in range(8):
                    b = bank()
                    w, t_w, i = wsplit(f"w2_{l}", (m,))
                    w2, t_w2, i2 = load(A[f"w2_{l}"][m][:, 2048:2816], "p (k c) -> p k c", k=6)
                    for k in range(8):
                        product(b.ap[:, 0:256], w, slice(0, 128), t_w, k, slice(256, 512), t_hh[k], k == 0, False,
                                False, b.w)
                    for k in range(6):
                        t = mm(b.ap[:, 0:256], w2[:, k, :], hh[:, 16 + k, :], False, False, t_w2, t_hh[16 + k],
                               sig=(k == 5))
                    done(i2, t)
                    for k in range(8):
                        t = product(b.ap[:, 0:256], [v[:, 8:16, :] for v in w], slice(0, 128), t_w[8:16], k,
                                    slice(0, 256), t_hh[8 + k], False, k == 7, False, sig=(k == 7))
                    done(i, t)
                    t = tt(VE, X[:, m, 0:256], b.ap[:, 0:256], X[:, m, 0:256], ALU.add, t)
                    b.release(t)
                    t_sq.append(act(SQ0[:, m, :], X[:, m, 0:256], ACT.Square, t))
                    next(beside, None)
                return t_sq

            def steps(*work):
                work = list(work)
                while work:
                    work = [g for g in work if next(g, g) is not g]

            def attend(units, S, T, t_S, t_T, beside, per):
                N, NT_ = len(units), len(T)
                scored, sums, t_exp, t_scaled_, t_turn, t_copied, t_value = {}, {}, {}, {}, {}, {}, {}

                def probs(n):
                    heads, J = units[n][2], units[n][3]
                    return S[n % 3][:, 0:heads * J].rearrange("p (h j) -> p h j", h=heads)

                def maximum_and_exp(n):
                    heads, J, mask, sink = units[n][2:6]
                    b, t_score = scored[n]
                    v = b.ap.rearrange("p (h j) -> p h j", h=heads)[:, :, 0:J]
                    s = probs(n)
                    t_s = t_turn[n - 3] if n >= 3 else t_S
                    nm, sm, se = small(heads), small(heads), small(heads)
                    if mask is not None:
                        m3 = mask.rearrange("p (a j) -> p a j", a=1).to_broadcast([128, heads, J])
                        t = stt(s, v, 0.125, m3, ALU.mult, ALU.add, t_score, t_s)
                        b.release(t)
                        t_max = VE.do(lambda e: e.tensor_reduce(nm, s, AX.X, ALU.max, negate=True))
                        src, scale = s, 1.0
                    else:
                        VE.do(lambda e: e.tensor_reduce(nm, v, AX.X, ALU.max, negate=True), t_score, t_s)
                        t_max = ts(VE, nm, nm, 0.125, None, ALU.mult, None)
                        src, scale = v, 0.125
                    if sink is not None:
                        t_max = tt(VE, nm, nm, sink[1], ALU.min)
                        t_sink = tt(VE, se, sink[0], nm, ALU.add)
                    for h in range(heads):
                        t = act(s[:, h, :], src[:, h, :], ACT.Exp, t_max, bias=nm[:, h:h + 1], scale=scale,
                                accum=sm[:, h:h + 1])
                    if mask is None:
                        b.release(t)
                    if sink is not None:
                        t = act(se, se, ACT.Exp, t_sink)
                    t_exp[n] = t
                    sums[n] = (sm, se)

                def scale(n):
                    heads, J, _, sink, gate, rowvis = units[n][2:8]
                    sm, se = sums[n]
                    s = probs(n)
                    if sink is not None:
                        tt(VE, sm, sm, se, ALU.add, t_exp[n])
                    VE.do(lambda e: e.reciprocal(sm, sm), t_exp[n])
                    if gate is not None:
                        tt(VE, sm, sm, gate, ALU.mult)
                    if rowvis is not None:
                        ts(VE, sm, sm, rowvis, None, ALU.mult, None)
                    sm3 = sm.rearrange("p (h a) -> p h a", a=1).to_broadcast([128, heads, J])
                    t_scaled = tt(VE, s, s, sm3, ALU.mult)
                    t_scaled_[n] = t_scaled

                def turn(n):
                    heads, J = units[n][2:4]
                    s, t_scaled = probs(n), t_scaled_[n]
                    nj = (J + 127) // 128
                    kp = min(J, 128)
                    w = heads * 128
                    b = pair() if nj * w > 512 else bank()
                    for jt in range(nj):
                        for h in range(heads):
                            c = jt * w + h * 128
                            t = tr(b.ap[0:kp, c:c + 128], s[:, h, jt * 128:jt * 128 + kp], ident, b.w, t_scaled,
                                   sig=(jt == nj - 1 and h == heads - 1))
                    t_turn[n] = t
                    t_copied[n] = copy(AC, T[n % NT_][0:kp, 0:nj * w], b.ap[0:kp, 0:nj * w], t,
                                       t_value[n - NT_] if n >= NT_ else t_T)
                    b.release(t_copied[n])

                scored[0] = units[0][0]()
                for n in range(N + 2):
                    if n + 1 < N:
                        scored[n + 1] = units[n + 1][0]()
                    finish = None
                    if n >= 2:
                        t_value[n - 2], finish = units[n - 2][1](T[(n - 2) % NT_], t_copied[n - 2])
                    if n < N:
                        maximum_and_exp(n)
                    if 1 <= n <= N:
                        scale(n - 1)
                    if finish is not None:
                        finish()
                    for _ in range(per):
                        next(beside, None)
                    if 1 <= n <= N:
                        turn(n - 1)
                steps(beside)

            def nsa(t_h):
                barrier()
                two = dict(shape="p (a n) -> p a n", a=2)
                q = area(2048, "p (a n) -> p a n", a=8)
                tmp = area(2048, "p (a n) -> p a n", a=8)
                att = tmp
                t_xn = []
                run(norm(X[:, :, 0:256], SQ0, lambda k: P("attn_norm", 8 + k), t_h, t_xn))
                over = top[0]
                kc, vc = [area(512, **two) for _ in range(2)]
                bufk, bufv = [area(960, "p (l n) -> p l n", l=16) for _ in range(2)]
                vs, vw = [area(512, "p (t c) -> p t c", t=2) for _ in range(2)]
                ks, kw, ks1, kw1 = [area(512, **two) for _ in range(4)]
                gk, gv = area(60), area(60)
                kcT, kcT1 = area(30, **two), area(30, **two)
                kct = area(30, **two)
                vcs = area(256, "p (g d) -> p g d", g=4)
                Tc = area(512)
                gt = area(96, "p (t c) -> p t c", t=2)
                pe2 = area(64)
                t_pe = cload(5, pe2[0:64, :], A["pe"])
                t_pe = cload(5, pe2[64:128, :], A["pe"])
                S = [area(1024) for _ in range(3)]
                T = [Tc] + [arena[:, over + 1024 * n:over + 1024 * (n + 1)] for n in range(2)]

                def fm(c, dst):
                    w, t_w, i = wsplit("nsa_in", c)
                    b = bank()
                    t = feats3([0, 128], w, t_w, t_xn, b)
                    done(i, t)
                    t = evac(dst, b.ap.rearrange("p (a n) -> p a n", a=2), t)
                    b.release(t)
                    return t

                def tm(c, dst):
                    w, t_w, i = wsplit("nsa_in", c)
                    b = bank()
                    t = rows3(b, w, t_w, t_xn, (0, 1), slice(0, 256), 256)
                    done(i, t)
                    t = evac(dst, b.ap.rearrange("p (t c) -> p t c", t=2), t)
                    b.release(t)
                    return t

                w, t_w, i = wsplit("nsa_gates", 0)
                b = bank()
                t = rows3(b, w, t_w, t_xn, (0, 1), slice(0, 64), 64)
                done(i, t)
                t_gt = act(gt, b.ap[:, 0:128].rearrange("p (t c) -> p t c", t=2)[:, :, 0:48], ACT.Sigmoid, t)
                b.release(t_gt)
                t_kc, t_vc = fm(4, kc), fm(5, vc)
                t_ks, t_kw = fm(6, ks), fm(8, kw)
                t_zero = [GP.do(lambda e, v=v: e.memset(v, 0.0)) for v in (vcs, Tc, gk, gv)]
                t_ks = rope(ks, tmp[:, 0:2, :], 2, C("p8"), C("ncos"), C("nsin"), t_ks)
                t_kw = rope(kw, tmp[:, 2:4, :], 2, C("p8"), C("ncos"), C("nsin"), t_kw)
                t_ks = halves(ks, ks1, t_ks)
                t_kw = halves(kw, kw1, t_kw)
                for src, dst, pe, t in ((kc, bufk, 0, t_kc), (vc, bufv, 1, t_vc)):
                    for g in range(4):
                        r = slice((g % 2) * 64, (g % 2) * 64 + 64)
                        for par in range(2):
                            for lh in range(2):
                                sv = src[r, g // 2, lh * 16:lh * 16 + 240].rearrange("p (n l a) -> p a l n", l=8, a=2)
                                a0 = pe * 32 + lh * 16
                                pv = pe2[r, a0:a0 + 16].rearrange("p (l a b) -> p a l b", a=2, b=1)[:, par]
                                t_b = tt(VE, dst[par * 64:par * 64 + 64, lh * 8:lh * 8 + 8, g * 15:g * 15 + 15],
                                         sv[:, par], pv.to_broadcast([64, 8, 15]), ALU.add, t, t_pe)
                t_vs, t_vw = tm(7, vs), tm(9, vw)
                tq = [fm(c, q[:, 2 * c:2 * c + 2, :]) for c in range(4)]
                t_q = rope(q, tmp, 8, C("p8"), C("ncos"), C("nsin"), [t_ks, t_kw] + tq)
                t_g2 = []
                for src, g2, name in ((bufk, gk, "cmp_k1"), (bufv, gv, "cmp_v1")):
                    w, t_w, i = load(A[name], "p (m c) -> p m c", m=16)
                    b = bank()
                    for m in range(16):
                        t = mm(b.ap[0:64, 0:60], w[:, m, :], src[:, m, :], m == 0, m == 15, b.w, t_w, t_b,
                               sig=(m == 15))
                    done(i, t)
                    t_g2.append(act(g2[0:64, :], b.ap[0:64, 0:60], ACT.Gelu_apprx_tanh, t, t_zero))
                    b.release(t_g2[-1])
                w2, t_w2, i = load(A["cmp_w2"], "p (a c) -> p a c", a=2)
                b = bank()
                for p in range(2):
                    g3 = gk.rearrange("p (a q n) -> p q a n", a=2, q=2)[:, p]
                    t = mm(b.ap[p * 64:p * 64 + 64, 0:30], w2[:, 0, :], g3, True, True, b.w, t_w2, t_g2, sig=True)
                t_kc = copy(VE, kcT, b.ap[:, 0:30].rearrange("p (a n) -> p a n", a=2), t)
                b.release(t_kc)
                b = bank()
                for g in range(4):
                    t = mm(b.ap[0:15, g * 64:g * 64 + 64], gv[:, g * 15:g * 15 + 15], w2[:, 1, :], True, True, b.w,
                           sig=True)
                t_vc = copy(VE, vcs[0:15, :, :], b.ap[0:15, 0:256].rearrange("p (g d) -> p g d", g=4), t)
                b.release(t_vc)
                done(i, t)
                t_kc = rope(kcT, kct, 2, C("p8"), C("ecos"), C("esin"), t_kc, n=15)
                t_kc = halves(kcT, kcT1, t_kc)
                t_T = [PE.last(), VE.last()]

                units = []
                t_out = [None]

                def group(it, g):
                    p, t2_ = g % 2, g // 2
                    r = slice(p * 64, p * 64 + 64)
                    out = [None]
                    J = 128 * (it + 1)

                    def branch(br, k_, v_, tk_, tv_):
                        Jb = 15 if br == 0 else J
                        W = 128 if br == 0 else 256

                        def scores():
                            pr = bank() if br == 0 else pair()
                            for h in range(4):
                                t = mm(pr.ap[:, h * W:h * W + Jb], q[:, t2_ * 4 + h, it * 128:it * 128 + 128],
                                       k_[p][:, t2_, 0:Jb], True, True, pr.w, t_q, tk_, sig=(h == 3))
                            return pr, t

                        def values(T, t_T):
                            if br == 0:
                                out[0] = bank()
                            b = out[0]
                            if br == 0:
                                return mm(b.ap[r, :], v_[:, g, :], T[:, 0:512], True, False, b.w, t_T, tv_,
                                          sig=True), None
                            for jt in range(it + 1):
                                t = mm(b.ap[r, :], v_[:, jt, g * 64:g * 64 + 64], T[:, jt * 512:(jt + 1) * 512],
                                       False, br == 2 and jt == it, t_T, tv_, sig=(jt == it))

                            def finish():
                                t_out[0] = copy(VE, att[r, t2_ * 4:t2_ * 4 + 4, it * 128:it * 128 + 128],
                                                b.ap[r, :].rearrange("p (h n) -> p h n", h=4), t, t_q)
                                b.release(t_out[0])

                            return t, finish if br == 2 else None

                        gate = gt[:, it, g * 12 + br:g * 12 + 12:3]
                        if br == 0:
                            return scores, values, 4, 15, C("emask", it * 15, 15), None, gate, C("evis", it, 1)
                        return scores, values, 4, J, C("cmask", 0 if it else 128, J), None, gate, None

                    return [branch(0, (kcT, kcT1), vcs, t_kc, t_vc), branch(1, (ks, ks1), vs, t_ks, t_vs),
                            branch(2, (kw, kw1), vw, t_kw, t_vw)]

                VE.wait(t_gt)
                small_c = C("decay", 0, 256).rearrange("p (k v) -> p k v", v=32)
                buf = [C("decay", 256 + 256 * n, 256) for n in range(2)]
                for it in range(2):
                    for g in range(4):
                        units += group(it, g)
                attend(units, S, T, [], t_T, modulation(small_c, buf, []), 1)
                t = t_out[0]
                return residual("nsa_out", att, [t] * 8)

            def modulation(small_c, buf, t_buf):
                s2 = small_c
                t_c = GP.do(lambda e: e.memset(s2, 0.0))
                t_c = act(s2[:, :, 0:2], P("cvec", 0, 16).rearrange("p (k v) -> p k v", v=2), ACT.Silu, t_c)
                before = None
                for l in range(2):
                    for c in range(13):
                        if before is not None:
                            m, r_, t_ = before
                            b = bank()
                            for j in range(2):
                                t1 = mm(b.ap[:, 2 * j:2 * j + 2], r_[:, j * 128:(j + 1) * 128], C("sel"), True, True,
                                        b.w, t_, sig=(j == 1))
                            t_buf = [t1]
                            bias = P("b_ada", 24 * l + m, 2).rearrange("p (m a) -> p m a", a=1)\
                                .to_broadcast([128, 2, 2])
                            t = tt(VE, MODS[l][:, m:m + 2, :], b.ap[:, 0:4].rearrange("p (m v) -> p m v", v=2), bias,
                                   ALU.add, t1)
                            b.release(t)
                        if c < 12:
                            w, t_w, i = wchunk(f"ada_{l}", c)
                            b = bank()
                            for k in range(8):
                                g = slice(32 * (k % 4), 32 * (k % 4) + 32)
                                t1 = mm(b.ap[g, 0:256], s2[:, k, :], w[:, k, :], k < 4, k >= 4, b.w, t_w, t_c,
                                        sig=(k == 7))
                            done(i, t1)
                            r = buf[c % 2]
                            t_r = copy(AC, r, b.ap[:, 0:256], t1, t_buf)
                            b.release(t_r)
                        before = (2 * c, r, t_r) if c < 12 else None
                        yield
                    m3 = MODS[l]
                    nw = P("norm_w2", 8 * l, 8).rearrange("p (m a) -> p m a", a=1).to_broadcast([128, 8, 2])
                    stt(m3[:, 8:16, :], m3[:, 8:16, :], 1.0, nw, ALU.add, ALU.mult)

            MODS = [MOD[:, 0:48].rearrange("p (m v) -> p m v", v=2), MOD[:, 48:96].rearrange("p (m v) -> p m v", v=2)]

            def adapted(l, v, sq, t_sq, out):
                cs = slice(v * 256, v * 256 + 256)
                m3 = MODS[l]
                return norm(X[:, :, cs], sq, lambda k: m3[:, 8 + k, v:v + 1], t_sq, out,
                            shift=lambda k: m3[:, k, v:v + 1], cs=cs)

            def layer(l, t_H):
                NT = 512 if l == 0 else 256
                nt = NT // 128
                m3 = MODS[l]
                top[0] = 0
                Z = area(8 * NT, "p (r a n) -> p r a n", r=4, a=2)
                tail = top[0]
                R = [area(1536, "p (a n) -> p a n", a=3) for _ in range(2)]
                V = [area(512, "p (t c) -> p t c", t=4) for _ in range(2)]
                K1 = [area(512) for _ in range(2)]
                mid = top[0]

                def fm(w, t_w, cols, n, n0=0):
                    b = bank()
                    return b, feats3([cols], w, t_w, t_H, b, n=n)

                NZ = 2 * NT
                decay = C("decay")
                U = decay[:, 0:NZ].rearrange("p (a n) -> p a n", a=2)
                VT = decay[:, NZ:2 * NZ].rearrange("p (t c) -> p t c", t=nt)
                Fm = decay[:, 0:NZ].rearrange("p (a n) -> p a n", a=2)
                ZZ = decay[:, NZ:NZ + 1024].rearrange("p (t a c) -> p t a c", t=2, a=2)
                t_z, t_uv = [], []

                def outer():
                    for r, c in enumerate((2, 5)):
                        w, t_w, i = wsplit(f"in_{l}", c)
                        for a in range(2):
                            b, t = fm(w, t_w, a * 128, NT)
                            t_z.append(act(Z[:, r, a, :], b.ap[:, 0:NT], ACT.Silu, t))
                            b.release(t_z[-1])
                        done(i, t)
                        yield
                    w, t_w, i = wsplit(f"in_{l}", 8)
                    for a in range(2):
                        b, t = fm(w, t_w, a * 128, NT)
                        t_uv.append(act(U[:, a, :], b.ap[:, 0:NT], ACT.Gelu, t))
                        b.release(t_uv[-1])
                    done(i, t)
                    yield
                    w, t_w, i = wsplit(f"in_{l}", 9)
                    for j in range(nt // 2):
                        b = bank()
                        t = rows3(b, w, t_w, t_H, (2 * j, 2 * j + 1), slice(0, 256), 256)
                        t_uv.append(act(VT[:, 2 * j:2 * j + 2, :], b.ap.rearrange("p (t c) -> p t c", t=2), ACT.Gelu,
                                        t))
                        b.release(t_uv[-1])
                    done(i, t)
                    yield

                def inner():
                    t_2z = [None, None]
                    for r, c in ((3, 10), (2, 7)):
                        w, t_w, i = wsplit(f"in_{l}", c)
                        for a in range(2):
                            b, t = fm(w, t_w, a * 128, NT)
                            t = act(Z[:, r, a, :], b.ap[:, 0:NT], ACT.Tanh, t, scale=0.5)
                            t_2z[r - 2] = stt(Z[:, r, a, :], Z[:, r, a, :], 1.0, b.ap[:, 0:NT], ALU.add, ALU.mult, t)
                            b.release(t_2z[r - 2])
                            if a == 1:
                                done(i, PE.last())
                            yield
                    t_zu = tt(GP, Z[:, 3, :, :], Z[:, 3, :, :], U, ALU.mult, t_2z[1], t_uv)
                    w, t_w, i = load(A[f"sp_{l}"], "p (g q) -> p g q", g=4)
                    bsp, t_bsp, i2 = load(A[f"bsp_{l}"], "p (g q) -> p g q", g=4)
                    for a in range(2):
                        b = bank()
                        for n in range(nt):
                            for st in range(2):
                                for h in range(2):
                                    g = 2 * a + h
                                    r = slice(h * 64, h * 64 + 64)
                                    lh, rh = ((VT[:, n, g * 64:g * 64 + 64], w[:, g, :]),
                                              (C("onerow"), bsp[:, g, :]))[st]
                                    t = mm(b.ap[r, n * 128:(n + 1) * 128], lh, rh, st == 0, st == 1, b.w, t_w, t_uv,
                                           t_bsp, sig=True)
                        t_yc = stt(Z[:, 3, a, :], b.ap[:, 0:NT], 0.5, Z[:, 3, a, :], ALU.mult, ALU.mult, t, t_zu)
                        b.release(t_yc)
                        if a == 1:
                            done(i, t)
                            done(i2, t)
                        yield
                    t_old_uv = [PE.last(), t_zu]
                    w, t_w, i = wsplit(f"in_{l}", 6)
                    t_f = []
                    for a in range(2):
                        b, t = fm(w, t_w, a * 128, NT)
                        t_f.append(evac(Fm[:, a, :], b.ap[:, 0:NT], t, t_old_uv))
                        b.release(t_f[-1])
                        if a == 1:
                            done(i, t)
                        yield
                    w, t_w, i = load(A[f"fnet_{l}"], "p (a c) -> p a c", a=2)
                    t_zz = t_old_uv
                    for v in range(NT // 256):
                        for n in range(2):
                            b = bank()
                            for a in range(2):
                                c = v * 256 + n * 128
                                t = mm(b.ap[:, a * 256:(a + 1) * 256], Fm[:, a, c:c + 128], C("cs"), True, True, b.w,
                                       t_f, sig=True)
                            t = copy(VE, ZZ[:, n, :, :], b.ap.rearrange("p (a c) -> p a c", a=2), t, t_zz)
                            b.release(t)
                        yield
                        b = bank()
                        for a in range(2):
                            for n in range(2):
                                mm(b.ap[:, a * 256:(a + 1) * 256], ZZ[:, n, a, 0:128], C("cn", n * 256, 256), n == 0,
                                   False, b.w, t)
                                t2 = mm(b.ap[:, a * 256:(a + 1) * 256], ZZ[:, n, a, 128:256], C("sn", n * 256, 256),
                                        False, n == 1, sig=True)
                        t_zz = [t2]
                        Y = Fm[:, :, v * 256:v * 256 + 256]
                        t = copy(VE, Y, b.ap.rearrange("p (a n) -> p a n", a=2), t2)
                        b.release(t)
                        yield
                        b = bank()
                        for a in range(2):
                            t2 = mm(b.ap[:, a * 256:(a + 1) * 256], w[:, a, :], Y[:, a, :], True, True, b.w, t, t_w,
                                    sig=True)
                        zz = Z[:, 2, :, v * 256:v * 256 + 256]
                        t = stt(zz, b.ap.rearrange("p (a n) -> p a n", a=2), 0.5, zz, ALU.mult, ALU.mult, t2,
                                t_2z[0])
                        b.release(t)
                        yield
                    done(i, t2)

                S3 = area(1536, "p (a n) -> p a n", a=3)
                T3 = area(768, "p (a n) -> p a n", a=3)
                RX = area(1536, "p (t h d) -> p t h d", t=4, h=6)
                t_qk, t_vv = [None, None], [None, None]
                nsink = MOD[:, 96:100]
                ts(VE, nsink, P("sink", l * 4, 4), -1.0, None, ALU.mult, None)

                def keys():
                    for br, (cq, ck) in enumerate(((0, 1), (3, 4))):
                        raw = R[br]
                        w, t_w, i = wsplit(f"in_{l}", cq)
                        tr_ = []
                        for a in range(2):
                            b, t = fm(w, t_w, a * 128, NT)
                            tr_.append(evac(raw[:, a, 0:NT], b.ap[:, 0:NT], t))
                            b.release(tr_[-1])
                        done(i, t)
                        w, t_w, i = wsplit(f"in_{l}", ck)
                        b, t = fm(w, t_w, 0, 512)
                        tr_.append(evac(raw[:, 2, :], b.ap, t))
                        b.release(tr_[-1])
                        b = bank()
                        t = rows3(b, w, t_w, t_H, range(4), slice(128, 256), 128)
                        done(i, t)
                        t = evac(V[br], b.ap.rearrange("p (t c) -> p t c", t=4), t)
                        b.release(t)
                        t_vv[br] = t
                        t_rx = PE.last()
                        sq = [act(S3[:, 0:2, 0:NT], raw[:, 0:2, 0:NT], ACT.Square, tr_, t_rx),
                              act(S3[:, 2, :], raw[:, 2, :], ACT.Square)]
                        yield
                        b = bank()
                        for n in range(4):
                            for a in range(3):
                                if a < 2 and n >= nt:
                                    continue
                                c = n * 6 + 2 * a
                                t = mm(b.ap[:, c:c + 2], S3[:, a, n * 128:(n + 1) * 128], C("bones2"), True, True, b.w, sq,
                                       sig=True)
                        ms = small(24)
                        ms3 = ms.rearrange("p (t h) -> p t h", h=6)
                        b3 = b.ap[:, 0:24].rearrange("p (t h) -> p t h", h=6)
                        if nt == 4:
                            t = ts(VE, ms, b.ap[:, 0:24], 1.0, EPS, ALU.mult, ALU.add, t)
                        else:
                            ts(VE, ms3[:, 0:2, :], b3[:, 0:2, :], 1.0, EPS, ALU.mult, ALU.add, t)
                            VE.do(lambda e, m=ms3: e.memset(m[:, 2:4, 0:4], 1.0))
                            t = ts(VE, ms3[:, 2:4, 4:6], b3[:, 2:4, 4:6], 1.0, EPS, ALU.mult, ALU.add)
                        b.release(t)
                        r_, t = power(24, ms, t)
                        t = copy(VE, RX, r_.rearrange("p (t h d) -> p t h d", t=4, d=1).to_broadcast([128, 4, 6, 64]), t,
                                 t_rx)
                        yield
                        tn = []
                        for a in range(3):
                            n_ = nt if a < 2 else 4
                            b = bank()
                            for n in range(n_):
                                t2 = mm(b.ap[:, n * 128:(n + 1) * 128], RX[:, n, 2 * a:2 * a + 2, :], ident, True, True,
                                        b.w, t, sig=True)
                            t3 = stt(raw[:, a, 0:n_ * 128], raw[:, a, 0:n_ * 128],
                                     P("qkn", l * 4 + br * 2 + (0 if a < 2 else 1)), b.ap[:, 0:n_ * 128], ALU.mult,
                                     ALU.mult, t2)
                            b.release(t3)
                            tn.append(t3)
                        yield
                        t_r = rope(raw[:, :, 0:256], T3, 3, C("p16"), C("acos"), C("asin"), tn)
                        t_qk[br] = halves(raw[:, 2, :], K1[br], t_r)
                steps(keys(), outer())
                top[0] = mid
                S = [area(1024) for _ in range(3)]
                T = [area(1024) for _ in range(2)]
                t_old = [PE.last(), VE.last(), GP.last()]
                VE.wait(t_z)

                def head(br, it, p):
                    raw, vv = R[br], V[br]
                    k0 = 0 if it < 2 else 256
                    J = 512 - k0
                    r = slice(p * 64, p * 64 + 64)

                    def scores():
                        pr = pair()
                        for h in range(2):
                            t = mm(pr.ap[:, h * 512:h * 512 + J], raw[:, h, it * 128:it * 128 + 128],
                                   (raw[:, 2, :], K1[br])[p][:, k0:512], True, True, pr.w, t_qk[br], sig=(h == 1))
                        return pr, t

                    def values(T, t_T):
                        b = bank()
                        nj = J // 128
                        for jt in range(nj):
                            t = mm(b.ap[r, 0:256], vv[:, k0 // 128 + jt, p * 64:p * 64 + 64],
                                   T[:, jt * 256:(jt + 1) * 256], jt == 0, jt == nj - 1, b.w, t_T, t_vv[br],
                                   sig=(jt == nj - 1))
                        zz = Z[r, br, :, it * 128:it * 128 + 128]

                        def finish():
                            b.release(tt(VE, zz, b.ap[r, 0:256].rearrange("p (h n) -> p h n", h=2), zz, ALU.mult, t,
                                         t_z))

                        return t, finish

                    return (scores, values, 2, J, C("wmask", it * 512, 512) if br == 1 and it < 2 else None,
                            (P("sink", l * 4 + 2 * p, 2), nsink[:, 2 * p:2 * p + 2]) if br == 1 else None, None, None)

                attend([head(br, it, p) for br in range(2) for it in range(nt) for p in range(2)],
                       S, T, t_old, t_old, inner(), 1 if l == 0 else 2)
                t_Z = [q_.last() for q_ in (PE, VE, AC, GP)]
                for q_ in (VE, AC, GP):
                    q_.wait(t_Z)
                top[0] = tail
                M = area(8 * NT, "p (a n) -> p a n", a=8)
                t_M = [None] * 8
                SG = [area(NT) for _ in range(2)]
                T2 = [area(NT) for _ in range(2)]
                t_sg, t_t2 = [[], []], [[], []]
                n_ = 0
                for c in range(4):
                    wb, t_wb, ib = load(A[f"br_{l}"][c], "p (r k c) -> p r k c", r=4, k=2)
                    for r in range(4):
                        w, t_w, i = wsplit(f"merge_{l}", r * 4 + c)
                        for j in range(2):
                            m = 2 * c + j
                            b, t = fm(w, t_w, j * 128, NT)
                            s = SG[n_ % 2]
                            t = act(s, b.ap[:, 0:NT], ACT.Sigmoid, t, t_sg[n_ % 2],
                                    bias=P("b_merge", l * 32 + r * 8 + m))
                            b.release(t)
                            b = bank()
                            for k in range(2):
                                t_y = mm(b.ap[:, 0:NT], wb[:, r, k, j * 128:(j + 1) * 128], Z[:, r, k, :], k == 0,
                                         k == 1, b.w, t_wb, t_Z, sig=(k == 1))
                            if r == 0:
                                t_m = tt(VE, M[:, m, :], b.ap[:, 0:NT], s, ALU.mult, t, t_y)
                                b.release(t_m)
                                t_sg[n_ % 2] = [t_m]
                            else:
                                u = T2[n_ % 2]
                                t = tt(VE, u, b.ap[:, 0:NT], s, ALU.mult, t, t_y, t_t2[n_ % 2])
                                b.release(t)
                                t_sg[n_ % 2] = [t]
                                t_m = tt(GP, M[:, m, :], M[:, m, :], u, ALU.add, t)
                                t_t2[n_ % 2] = [t_m]
                            if r == 3:
                                t_M[m] = parts(m, slice(256, 512), M[:, m, :], t_m, t_Z) if l == 1 else t_m
                            n_ += 1
                        done(i, t_y)
                    done(ib, t_y)
                t_sq = [[], []]
                t_z = PE.last()
                ms = slice(0, 512) if l == 0 else slice(256, 512)
                if l == 0:
                    t_M = [parts(k, ms, M[:, k, :], t_M[k], t_z) for k in range(8)]
                for c in range(4):
                    w, t_w, i = wsplit(f"out_{l}", c)
                    for j in range(2):
                        m = 2 * c + j
                        b = bank()
                        for k in range(8):
                            t = product(b.ap[:, 0:NT], w, slice(j * 128, (j + 1) * 128), t_w, k, ms, t_M[k],
                                        k == 0, k == 7, False, b.w, sig=(k == 7))
                        for v in range(NT // 256):
                            cs = slice(v * 256, v * 256 + 256)
                            t2 = stt(X[:, m, cs], b.ap[:, cs], m3[:, 16 + m, v:v + 1], X[:, m, cs], ALU.mult, ALU.add, t)
                            if l == 0:
                                t_sq[v].append(act((SQ0, SQ1)[v][:, m, :], X[:, m, cs], ACT.Square, t2, t_z))
                        b.release(t2)
                    done(i, t)
                return t2, t_sq

            t_H = [[], [], [], []]

            context_steps = []

            def context(sq):
                for q in (VE, AC, GP):
                    q.wait(t_late)
                g = adapted(0, 1, sq, squares(sq, X[:, :, 256:512], []), t_H[1])
                context_steps.append(g)
                yield
                for _ in range(2):
                    next(g)
                    yield

            t = hybrid()
            t = ffn(0, t, lambda sq: iter(()))
            t = nsa(t)
            t = ffn(1, t, context)
            barrier()
            t_sq = []
            steps(plain_norm(X[:, :, 0:256], SQ0, lambda k: P("final_norm", k), t, SQ1, t_sq), context_steps[0])
            run(adapted(0, 0, SQ1, t_sq, t_H[0]))
            _, t_sq = layer(0, [a + b for a, b in zip(t_H[0], t_H[1])])
            barrier()
            steps(adapted(1, 0, SQ0, t_sq[0], t_H[2]), adapted(1, 1, SQ1, t_sq[1], t_H[3]))
            t, _ = layer(1, [a + b for a, b in zip(t_H[2], t_H[3])])
            SP.wait(t)
            SP.plain(lambda e: e.dma_start(out.rearrange("p (k n) -> p k n", k=8), X[:, :, 0:256]).then_inc(s_out, 16))
            SP.wait((s_out, 16))
            return queues, asked

        _, order = emit(None)
        (SP, PE, VE, AC, GP), _ = emit(order)

        with nc.Block() as block:
            @block.sync
            def _(e):
                SP.run(e)

            @block.tensor
            def _(e):
                PE.run(e)

            @block.vector
            def _(e):
                VE.run(e)

            @block.scalar
            def _(e):
                AC.run(e)

            @block.gpsimd
            def _(e):
                GP.run(e)


def constants():
    CL, CN = _consts_layout()
    c = np.zeros((128, CN), np.float32)

    def put(name, v):
        a, n = CL[name]
        c[:, a:a + n] = np.asarray(v, np.float64).reshape(128, n)

    eye = np.eye(128)
    half = np.kron(np.eye(2), np.ones((64, 64)))
    put("ident", eye)
    put("psum1", np.full((128, 1), 1.0 / 32768))
    put("sel", np.arange(128)[:, None] % 32 == np.arange(2)[None, :])
    put("bones2", np.kron(np.eye(2), np.ones((64, 1))) / 64)
    put("bones", half / 64)
    put("mhalf", np.full((128, 24), -0.5))
    put("onerow", np.ones((128, 64)))
    pos = np.arange(256, dtype=np.float32)
    d = np.arange(128) % 64

    def swap(partner):
        m = np.zeros((128, 128))
        for i in range(128):
            if partner[i] >= 0:
                m[partner[i], i] = 1
        return m

    def angles(p, rot, theta, idx):
        inv = np.float32(theta) ** (-np.arange(0, rot, 2, dtype=np.float32) / np.float32(rot))
        return (p[None, :].astype(np.float32) * inv.astype(np.float32)[idx][:, None]).astype(np.float32)

    base = (np.arange(128) // 64) * 64
    put("p32", swap(base + (d + 32) % 64))
    a = angles(pos, 64, 10000.0, d % 32).astype(np.float64)
    put("rcos", np.cos(a))
    put("rsin", np.sin(a) * np.where(d < 32, -1.0, 1.0)[:, None])
    put("p8", swap(np.where(d < 16, base + (d + 8) % 16, -1)))
    for name, p in (("n", pos), ("e", np.arange(15, dtype=np.float32) * 16 + 31)):
        a = angles(p, 16, 500000.0, d % 8).astype(np.float64)
        on = (d < 16)[:, None]
        put(name + "cos", np.where(on, np.cos(a), 1.0))
        put(name + "sin", np.where(on, np.sin(a) * np.where(d < 8, -1.0, 1.0)[:, None], 0.0))
    put("p16", swap(base + (d // 32) * 32 + (d % 32 + 16) % 32))
    inv = np.float32(10000.0) ** (-np.arange(16, dtype=np.float32) / np.float32(16))
    t = np.arange(256)
    where = np.where((d < 32)[:, None], (t // 64)[None, :], (t % 64)[None, :]).astype(np.float32)
    a = (where * inv.astype(np.float32)[d % 16][:, None]).astype(np.float32).astype(np.float64)
    put("acos", np.cos(a))
    put("asin", np.sin(a) * np.where(d % 32 < 16, -1.0, 1.0)[:, None])
    i = np.arange(128)
    NEG = -1e30
    causal = np.where(i[None, :] <= i[:, None], 0.0, NEG)
    put("cmask", np.concatenate([np.zeros((128, 128)), causal], 1))
    end = np.arange(15) * 16 + 31
    vis = end[None, None, :] <= (np.arange(2)[:, None, None] * 128 + i[None, :, None])
    put("emask", np.where(vis, 0.0, NEG).transpose(1, 0, 2))
    put("evis", vis.any(-1).T.astype(float))
    w = np.zeros((128, 2, 512))
    w[:, 0, 128:256] = causal
    w[:, 1, 0:128] = np.where(i[None, :] >= i[:, None], 0.0, NEG)
    put("wmask", w)
    k = np.arange(64)
    f = 2 * np.pi * ((k[:, None] * k[None, :]) % 64) / 64
    put("cs", np.concatenate([np.kron(np.eye(2), np.cos(f)), np.kron(np.eye(2), np.sin(f))], 1))
    n = np.arange(256)
    f = 2 * np.pi * ((n[:, None] * n[None, :]) % 256) / 256
    put("cn", (np.cos(f) / 128).reshape(2, 128, 256).transpose(1, 0, 2))
    put("sn", (-np.sin(f) / 128).reshape(2, 128, 256).transpose(1, 0, 2))
    g = np.log1p(-(2.0 ** (-5.0 - np.arange(8))))
    diff = np.arange(256)[None, :] - i[:, None]
    dec = np.where(diff[None] >= 0, np.exp(np.maximum(diff, 0)[None] * g[:, None, None]), 0.0) * 0.125
    put("decay", dec.transpose(1, 0, 2))
    return c


def kernel(**inputs):
    import concourse.bacc as _bacc
    from concourse.bass_utils import run_bass_kernel_spmd as _run

    I = {k: np.asarray(v) for k, v in inputs.items()}

    def cols(w, c=256):
        K, N = w.shape
        return np.ascontiguousarray(w.reshape(K // 128, 128, N // c, c).transpose(2, 1, 0, 3)).reshape(
            N // c, 128, K // 128 * c)

    def tiles(v):
        return v.reshape(-1, 128).T

    def tokens(x):
        return np.ascontiguousarray(x.T.reshape(8, 128, 256).transpose(1, 0, 2)).reshape(128, 2048)

    def diag(w):
        n = w.shape[0]
        o = np.zeros((128, n // 2, 128), np.float32)
        for b in range(n):
            h = b % 2
            o[h * 64:h * 64 + 64, b // 2, h * 64:h * 64 + 64] = w[b]
        return o

    arr = {"xT": tokens(I["x"][0]), "ctxT": tokens(I["ctx_2"][0]), "consts": constants()}
    PL, PN = _params_layout()
    par = np.zeros((128, PN), np.float32)

    def put(name, v):
        a, n = PL[name]
        par[:, a:a + n] = v

    put("attn_norm", tiles(I["attn_norm"]))
    put("ffn_norm", tiles(I["ffn_norm"]))
    put("final_norm", tiles(I["final_norm"]))
    put("conv_w", I["conv_w"][0].reshape(4, 4, 128).transpose(2, 1, 0).reshape(128, 16))
    put("conv_b", tiles(I["conv_b"]))
    put("ga_b", tiles(I["gate_a_b"]))
    put("gx_b", tiles(I["gate_x_b"]))
    put("lam", tiles(I["lru_lambda"]))
    put("b_ada", tiles(I["b_ada_2"]))
    put("norm_w2", tiles(I["norm_w_2"]))
    put("b_merge", tiles(I["b_merge_2"]))
    qkn = np.stack([I[n] for n in ("qn_a_2", "kn_a_2", "qn_d_2", "kn_d_2")], 1)
    put("qkn", np.tile(qkn.reshape(8, 64).T, (2, 1)))
    put("cvec", np.stack([I["c_2"][0].reshape(8, 128), I["c_ctx_2"].reshape(8, 128)], 2).transpose(1, 0, 2)
        .reshape(128, 16))
    put("sink", np.broadcast_to(I["sink_d_2"].reshape(1, 8), (128, 8)))
    arr["params"] = par
    arr["ab_in"] = cols(I["ab_w_in"][0])
    arr["ab_out"] = cols(I["ab_w_out"][0])
    arr["lru_gates"] = np.stack([diag(I["gate_a_w"][0]), diag(I["gate_x_w"][0])], 1).reshape(128, 1024)
    for l in range(2):
        arr[f"w1_{l}"] = cols(I["ffn_w1"][l])
        arr[f"w3_{l}"] = cols(I["ffn_w3"][l])
        arr[f"w2_{l}"] = cols(I["ffn_w2"][l], 128)
    w = I["nsa_w_in"][0]
    heads = [(2 * t2 + p) * 4 + r for t2 in range(2) for r in range(4) for p in range(2)]
    qcols = np.concatenate([np.arange(h * 64, h * 64 + 64) for h in heads])
    arr["nsa_in"] = cols(np.concatenate([w[:, qcols], w[:, 1024:2560]], 1))
    g = np.zeros((1, 128, 8, 256), np.float32)
    g[0, :, :, 0:48] = w[:, 2560:].reshape(8, 128, 48).transpose(1, 0, 2)
    arr["nsa_gates"] = g.reshape(1, 128, 2048)
    arr["nsa_out"] = cols(I["nsa_w_out"][0][qcols])
    arr["pe"] = np.ascontiguousarray(np.concatenate([I["cmp_pe_k"][0].T, I["cmp_pe_v"][0].T], 1))
    for n in "kv":
        arr[f"cmp_{n}1"] = np.ascontiguousarray(I[f"cmp_{n}_w1"][0].reshape(16, 128, 64).transpose(1, 0, 2)).reshape(
            128, 1024)
    arr["cmp_w2"] = np.zeros((128, 128), np.float32)
    arr["cmp_w2"][0:64, 0:64] = I["cmp_k_w2"][0]
    arr["cmp_w2"][0:64, 64:128] = I["cmp_v_w2"][0]
    hd = np.concatenate([np.arange(h * 64, h * 64 + 64) for h in (0, 2, 1, 3)])
    for l in range(2):
        w = I["w_in_2"][l]
        order = np.arange(2816)
        for c in (0, 2, 3, 5):
            order[c * 256:(c + 1) * 256] = c * 256 + hd
        arr[f"in_{l}"] = cols(w[:, order])
        arr[f"ada_{l}"] = cols(I["w_ada_2"][l])
        arr[f"merge_{l}"] = cols(I["w_merge_2"][l])
        arr[f"out_{l}"] = cols(I["w_out_2"][l])
        br = I["w_br_2"][l].copy()
        br[0], br[1] = br[0][hd], br[1][hd]
        arr[f"br_{l}"] = np.ascontiguousarray(br.reshape(4, 2, 128, 4, 256).transpose(3, 2, 0, 1, 4)).reshape(
            4, 128, 2048)
        arr[f"fnet_{l}"] = diag(I["w_fnet_2"][l]).reshape(128, 256)
        arr[f"sp_{l}"] = np.ascontiguousarray(I["w_sp_2"][l].transpose(2, 0, 1)).reshape(128, 512)
        bsp = np.zeros((128, 512), np.float32)
        bsp[0] = I["b_sp_2"][l].reshape(512)
        arr[f"bsp_{l}"] = bsp
    nc = _bacc.Bacc("TRN2", target_bir_lowering=False, num_devices=1)
    arr = {k: np.ascontiguousarray(v) for k, v in arr.items()}
    A = {k: nc.dram_tensor(k, v.shape, mybir.dt.from_np(v.dtype), kind="ExternalInput").ap() for k, v in arr.items()}
    out = nc.dram_tensor("out", (128, 2048), F32, kind="ExternalOutput").ap()
    build(nc, A, out)
    r = _run(nc, [arr], core_ids=[0])
    y = np.asarray(r.results[0]["out"])
    return np.ascontiguousarray(y.reshape(128, 8, 256).transpose(2, 1, 0)).reshape(1, 256, 1024)
```
